# Optimizing a Trainium2 kernel written in Bass

```python
import math
import jax, jax.numpy as jnp
from jax import lax
import numpy as np

D_MODEL = 2048
BATCH = 1
SEQ = 256
DEPTH = 1

D_MIX = D_MODEL
CONF_WIDTH = D_MIX // 2
HYENA_WIDTH = D_MIX - CONF_WIDTH
CONF_KERNEL = 31
SHORT_KERNEL = 3
HYENA_ORDER = 2
HYENA_EMB = 33
HYENA_FILTER_ORDER = 64
HYENA_INNER_MLPS = 2
HYENA_FAST_DECAY = 0.3
HYENA_SLOW_DECAY = 1.5
HYENA_TARGET = 1e-2
N_MEM = 256
XATTN_HEADS = 4
XATTN_HEAD_DIM = D_MODEL // XATTN_HEADS
D_FF = 5632
FFN_KERNEL = 3
EPS = 1e-6
IN_COLS = 2 * CONF_WIDTH + (HYENA_ORDER + 1) * HYENA_WIDTH

kernel_name = "hybrid_conformer_hyena_encoder_block"

F32 = jnp.float32

def rms_norm(x, g):
    xf = x.astype(F32)
    y = xf * lax.rsqrt(jnp.mean(xf * xf, axis=-1, keepdims=True) + EPS)
    return (y * g.astype(F32)).astype(x.dtype)

def layer_norm(x, g, b):
    xf = x.astype(F32)
    xc = xf - jnp.mean(xf, axis=-1, keepdims=True)
    y = xc * lax.rsqrt(jnp.mean(xc * xc, axis=-1, keepdims=True) + EPS)
    return (y * g.astype(F32) + b.astype(F32)).astype(x.dtype)

def depthwise_conv_centred(u, w, b):
    pad = w.shape[0] // 2
    y = lax.conv_general_dilated(
        u, w[:, None, :].astype(u.dtype), window_strides=(1,), padding=[(pad, pad)],
        dimension_numbers=("NWC", "WIO", "NWC"), feature_group_count=u.shape[-1])
    return y + b.astype(u.dtype)

def conformer_conv_group(p, dw_w, dw_b, ln_g, ln_b):
    a, gate = jnp.split(p, 2, axis=-1)
    u = a * jax.nn.sigmoid(gate)
    u = depthwise_conv_centred(u, dw_w, dw_b)
    u = layer_norm(u, ln_g, ln_b)
    return jax.nn.silu(u)

def hyena_position_features(length):
    t = jnp.linspace(0.0, 1.0, length, dtype=F32)[:, None]
    w = 2.0 * math.pi * jnp.arange(length, dtype=F32)[:, None] / length
    bands = (HYENA_EMB - 1) // 2
    f = jnp.linspace(1e-4, bands - 1, bands, dtype=F32)[None, :]
    z = jnp.concatenate([t, jnp.cos(f * w), -jnp.sin(f * w)], axis=-1)
    return t, z

def hyena_filters(length, w1, b1, w_inner, b_inner, w_filt, sin_freq):
    t, z = hyena_position_features(length)
    freq = sin_freq.astype(F32)
    h = jnp.sin(freq * (z @ w1.astype(F32) + b1.astype(F32)))
    for i in range(HYENA_INNER_MLPS):
        h = jnp.sin(freq * (h @ w_inner[i].astype(F32) + b_inner[i].astype(F32)))
    h = (h @ w_filt.astype(F32)).reshape(length, HYENA_ORDER, 2, HYENA_WIDTH)
    max_decay = math.log(HYENA_TARGET) / HYENA_FAST_DECAY
    min_decay = math.log(HYENA_TARGET) / HYENA_SLOW_DECAY
    deltas = jnp.abs(jnp.linspace(min_decay, max_decay, HYENA_WIDTH, dtype=F32))
    h = h * jnp.exp(-t[:, :, None, None] * deltas)
    k_fwd = h[:, :, 0]
    k_bwd = h[:, :, 1]
    k2 = jnp.concatenate(
        [k_fwd, jnp.zeros((1, HYENA_ORDER, HYENA_WIDTH), F32), k_bwd[: length - 1][::-1]], axis=0)
    return k2 * lax.rsqrt(jnp.sum(k2 * k2, axis=0, keepdims=True) + EPS)

def fft_conv_two_sided(u, k2, skip):
    length = u.shape[1]
    uf = jnp.fft.rfft(u.astype(F32), n=2 * length, axis=1)
    kf = jnp.fft.rfft(k2, n=2 * length, axis=0)
    y = jnp.fft.irfft(uf * kf[None], n=2 * length, axis=1)[:, :length]
    return (y + u.astype(F32) * skip.astype(F32)).astype(u.dtype)

def hyena_group(p, short_w, short_b, k2, skip):
    uc = depthwise_conv_centred(p, short_w, short_b)
    chunks = jnp.split(uc, HYENA_ORDER + 1, axis=-1)
    z = chunks[0]
    for o in range(HYENA_ORDER):
        z = chunks[o + 1] * fft_conv_two_sided(z, k2[:, o], skip[o])
    return z

def cross_attention(h, m, w_q, w_k, w_v, w_o):
    b, s, _ = h.shape
    n_mem = m.shape[1]
    q = (h @ w_q).reshape(b, s, XATTN_HEADS, XATTN_HEAD_DIM)
    k = (m @ w_k).reshape(b, n_mem, XATTN_HEADS, XATTN_HEAD_DIM)
    v = (m @ w_v).reshape(b, n_mem, XATTN_HEADS, XATTN_HEAD_DIM)
    scores = jnp.einsum("bshd,bmhd->bhsm", q, k).astype(F32) * (XATTN_HEAD_DIM ** -0.5)
    probs = jax.nn.softmax(scores, axis=-1).astype(v.dtype)
    o = jnp.einsum("bhsm,bmhd->bshd", probs, v).reshape(b, s, D_MODEL)
    return o @ w_o

def conv_glu_ffn(h, w_up, dw_w, dw_b, w_down):
    gate, val = jnp.split(h @ w_up, 2, axis=-1)
    gate = depthwise_conv_centred(gate, dw_w, dw_b)
    return (jax.nn.silu(gate) * val) @ w_down

def setup_inputs(seed: int = 0) -> dict:
    key = jax.random.key(seed)
    ks = iter(jax.random.split(key, 40))

    def nrm(shape, scale):
        return jax.random.normal(next(ks), shape, F32) * scale

    def gain(shape):
        return 1.0 + nrm(shape, 0.02)

    L = DEPTH
    return {
        "x": nrm((BATCH, SEQ, D_MODEL), 1.0),
        "mem": nrm((BATCH, N_MEM, D_MODEL), 1.0),
        "g_mix": gain((L, D_MODEL)),
        "w_in": nrm((L, D_MODEL, IN_COLS), D_MODEL ** -0.5),
        "conf_dw_w": nrm((L, CONF_KERNEL, CONF_WIDTH), CONF_KERNEL ** -0.5),
        "conf_dw_b": nrm((L, CONF_WIDTH), 0.02),
        "conf_ln_g": gain((L, CONF_WIDTH)),
        "conf_ln_b": nrm((L, CONF_WIDTH), 0.02),
        "hyena_short_w": nrm((L, SHORT_KERNEL, (HYENA_ORDER + 1) * HYENA_WIDTH), SHORT_KERNEL ** -0.5),
        "hyena_short_b": nrm((L, (HYENA_ORDER + 1) * HYENA_WIDTH), 0.02),
        "hyena_w1": nrm((L, HYENA_EMB, HYENA_FILTER_ORDER), HYENA_EMB ** -0.5),
        "hyena_b1": nrm((L, HYENA_FILTER_ORDER), 0.02),
        "hyena_w_inner": nrm((L, HYENA_INNER_MLPS, HYENA_FILTER_ORDER, HYENA_FILTER_ORDER), HYENA_FILTER_ORDER ** -0.5),
        "hyena_b_inner": nrm((L, HYENA_INNER_MLPS, HYENA_FILTER_ORDER), 0.02),
        "hyena_w_filt": nrm((L, HYENA_FILTER_ORDER, HYENA_ORDER * 2 * HYENA_WIDTH), HYENA_FILTER_ORDER ** -0.5),
        "hyena_sin_freq": gain((L, HYENA_FILTER_ORDER)),
        "hyena_skip": nrm((L, HYENA_ORDER, HYENA_WIDTH), 0.1),
        "w_out": nrm((L, D_MIX, D_MODEL), D_MIX ** -0.5),
        "g_xattn": gain((L, D_MODEL)),
        "g_mem": gain((L, D_MODEL)),
        "w_q": nrm((L, D_MODEL, D_MODEL), D_MODEL ** -0.5),
        "w_k": nrm((L, D_MODEL, D_MODEL), D_MODEL ** -0.5),
        "w_v": nrm((L, D_MODEL, D_MODEL), D_MODEL ** -0.5),
        "w_o": nrm((L, D_MODEL, D_MODEL), D_MODEL ** -0.5),
        "g_ffn": gain((L, D_MODEL)),
        "w_ffn_up": nrm((L, D_MODEL, 2 * D_FF), D_MODEL ** -0.5),
        "ffn_dw_w": nrm((L, FFN_KERNEL, D_FF), FFN_KERNEL ** -0.5),
        "ffn_dw_b": nrm((L, D_FF), 0.02),
        "w_ffn_down": nrm((L, D_FF, D_MODEL), D_FF ** -0.5),
        "g_final": gain((D_MODEL,)),
    }

def reference(x, mem, g_mix, w_in, conf_dw_w, conf_dw_b, conf_ln_g, conf_ln_b,
              hyena_short_w, hyena_short_b, hyena_w1, hyena_b1, hyena_w_inner, hyena_b_inner,
              hyena_w_filt, hyena_sin_freq, hyena_skip, w_out, g_xattn, g_mem,
              w_q, w_k, w_v, w_o, g_ffn, w_ffn_up, ffn_dw_w, ffn_dw_b, w_ffn_down, g_final):
    length = x.shape[1]
    for l in range(DEPTH):
        p = rms_norm(x, g_mix[l]) @ w_in[l]
        p_conf = p[..., : 2 * CONF_WIDTH]
        p_hyena = p[..., 2 * CONF_WIDTH:]
        y_conf = conformer_conv_group(p_conf, conf_dw_w[l], conf_dw_b[l], conf_ln_g[l], conf_ln_b[l])
        k2 = hyena_filters(length, hyena_w1[l], hyena_b1[l], hyena_w_inner[l], hyena_b_inner[l],
                           hyena_w_filt[l], hyena_sin_freq[l])
        y_hyena = hyena_group(p_hyena, hyena_short_w[l], hyena_short_b[l], k2, hyena_skip[l])
        x = x + jnp.concatenate([y_conf, y_hyena], axis=-1) @ w_out[l]
        x = x + cross_attention(rms_norm(x, g_xattn[l]), rms_norm(mem, g_mem[l]),
                                w_q[l], w_k[l], w_v[l], w_o[l])
        x = x + conv_glu_ffn(rms_norm(x, g_ffn[l]), w_ffn_up[l], ffn_dw_w[l], ffn_dw_b[l], w_ffn_down[l])
    return rms_norm(x, g_final)


_drawn_inputs = setup_inputs


def setup_inputs(seed=0):
    import zlib

    import numpy as np

    out = dict(_drawn_inputs(seed))
    spreads = {}
    factors = {'g_mix': 2.69,
     'conf_dw_b': 3.758,
     'conf_ln_g': 6.101,
     'conf_ln_b': 7.475,
     'g_xattn': 8.0,
     'g_mem': 8.0,
     'g_ffn': 12.79,
     'ffn_dw_b': 18.062,
     'g_final': 8.136}
    for name, (base, spread) in spreads.items():
        noise = np.random.default_rng([zlib.crc32(name.encode()), seed]).standard_normal(out[name].shape)
        drawn = base * np.exp(spread * noise) if base else spread * noise
        out[name] = __import__('jax').numpy.asarray(drawn.astype(out[name].dtype))
    for name, factor in factors.items():
        out[name] = (out[name] * factor).astype(out[name].dtype)
    return out
```

```python
from contextlib import ExitStack

import concourse.bass as bass
import numpy as np
from concourse import mybir

F32 = mybir.dt.float32
F32R = mybir.dt.float32r
ALU = mybir.AluOpType
ACT = mybir.ActivationFunctionType
AX_X = mybir.AxisListType.X

P = 128
S = 256
D = 2048
KT = D // P
HALF = 512
CONF = 1024
HY = 1024
TAPS = 31
HEADS = 4
FF = 5632
SLABS = FF // 512
RING = 4
MLP = 64
FEATURES = 33
EPS = 1e-6
SM_SCALE = float(D // HEADS) ** -0.5
PANELS = 30
SLOTS = 2 * PANELS

CONF_PANELS = [("gate", 0), ("value", 0), ("gate", 1), ("value", 1)]
HYENA_PANELS = [(0, 0), (1, 0), (0, 1), (1, 1), (2, 0), (2, 1)]
K0, V0, OUT0, Q0, O0 = 10, 14, 18, 22, 26

COL = {}
_at = 0
for _name, _n in (("conf_w", TAPS * 8), ("conf_b", 8), ("ln_g", 8), ("ln_b", 8),
                  ("short_w", 3 * 24), ("short_b", 24), ("ffn", SLABS * 16),
                  ("g_mix", KT), ("g_mem", KT), ("g_xattn", KT), ("g_ffn", KT), ("g_final", KT),
                  ("mlp_b", 3), ("freq", 1)):
    COL[_name] = _at
    _at += _n
PARAM_COLS = _at
PARAM_TILES = -(-PARAM_COLS // P)

SIDE = [("params", "L"), ("mlp0", "R"), ("mlp1", "R"), ("mlp2", "R"), ("stats0", "L"),
        ("taps0", "LR"), ("energy0", "L"), ("spec0", "LR"), ("spec_im0", "L"),
        ("taps1", "LR"), ("energy1", "L"), ("spec1", "LR"), ("spec_im1", "L"),
        ("taps2", "LR"), ("energy2", "L"), ("spec2", "LR"), ("spec_im2", "L"),
        ("taps3", "LR"), ("energy3", "L"), ("turn0", "L"), ("spec3", "LR"), ("spec_im3", "L"),
        ("turn1", "L"), ("turn2", "L"), ("stats1", "R"), ("turn3", "L"),
        ("dft0", "LR"), ("idft0", "L"), ("dft1", "LR"), ("idft1", "L"),
        ("dft2", "LR"), ("idft2", "L"), ("dft3", "LR"), ("idft3", "L"),
        ("mean", "R"), ("variance", "R"), ("stats2", "R"),
        ("scores0", "R"), ("turn_p0", "L"), ("scores1", "R"), ("pv0", "L"), ("turn_p1", "L"),
        ("scores2", "R"), ("pv1", "L"), ("turn_p2", "L"), ("scores3", "R"), ("pv2", "L"),
        ("turn_p3", "L"), ("pv3", "L"), ("stats3", "R")]


def side_counts():
    full, free, need = {"L": 0, "R": 0}, {"L": 0, "R": 0}, {}
    for name, pairs in SIDE:
        for b in pairs:
            before = free[b]
            free[b] += 1
            full[b] += not name.startswith("stats")
            need[name, b] = (before, full[b], free[b])
    return need, full, free


SIDE_AT, SIDE_FULL_END, SIDE_FREE_END = side_counts()


def before(name, b):
    return SIDE_AT[name, b][0]


def filled(name, b):
    return SIDE_AT[name, b][1]


def emptied(name, b):
    return SIDE_AT[name, b][2]


def block_program(nc, x_t, mem_t, params, w_in, w1, w_inner, w_filt, skip, w_out, w_q, w_k, w_v,
                  w_o, w_up, w_down, dft, idft, decay, features, out):
    KB = 1024
    base = 16512

    def at(name, kb, shape, dt=F32):
        return nc.alloc_sbuf_tensor_at(name, shape, dt, offset=base + int(kb * KB))

    with ExitStack() as ctx:
        def sem(name):
            return ctx.enter_context(nc.semaphore(name))

        raw = at("raw", 0, [P, RING, 1024])
        w_hi = at("w_hi", 16, [P, RING, 1024], F32R)
        w_lo = at("w_lo", 32, [P, RING, 1024], F32R)
        par = at("par", 48, [P, PARAM_TILES * P])
        eps, peak, shift, total, inv_total = (
            at(name, 50.5 + i / 32, [P, n])
            for i, (name, n) in enumerate((("eps", 1), ("peak", 2), ("shift", 2), ("total", 2), ("inv_total", 2))))
        ident = at("ident", 51, [P, P])
        ones = at("ones", 51.5, [P, P])
        root = at("root", 52, [P, S])
        inv_rms = at("inv_rms", 53, [P, S])
        a_hi = at("a_hi", 54, [P, KT, S], F32R)
        a_lo = at("a_lo", 70, [P, KT, S], F32R)
        x_first = at("x_first", 86, [P, KT, S])
        taps = at("taps", 86, [P, 4, HALF])
        folded = at("folded", 94, [P, 4, HALF])
        mem_x = at("mem_x", 86, [P, KT, S])
        keys = at("keys", 86, [P, KT, S])
        spec = [at("spec_first", 102, [P, 2, 5, HALF]), at("spec_second", 122, [P, 2, 5, HALF])]
        values = at("values", 102, [P, 2, D])
        dft_sb = at("dft_sb", 142, [P, 2, 768])
        idft_sb = at("idft_sb", 148, [P, 4, S])
        u = at("u", 152, [P, 8, S])
        conf = at("conf", 160, [P, 8, S])
        v_t = at("v_t", 168, [P, 2, 2, HALF])
        x1_t = at("x1_t", 176, [P, 2, 2, HALF])
        x2 = at("x2", 184, [P, 8, S])
        decay_sb = at("decay_sb", 184, [P, 4, HALF])
        spectrum = at("spectrum", 192, [P, 4, HALF])
        sigm = at("sigm", 192, [P, 4, S])
        skip_sb = at("skip_sb", 196, [P, HALF])
        k_norm = at("k_norm", 198, [P, HALF])
        w_filt_sb = at("w_filt_sb", 200, [MLP, 2, HALF])
        cross = at("cross", 200, [P, 2, HALF])
        turned = at("turned", 200, [P, 4, S])
        squares_x = at("squares_x", 168, [P, 2, 4, S])
        scaled_x = at("scaled_x", 174 + 2, [P, 2, 4, S])
        squares_m = at("squares_m", 192, [P, 2, 4, S])
        scaled_m = at("scaled_m", 192, [P, 2, 4, S])
        feat = at("feat", 102, [FEATURES, S])
        w1_sb = at("w1_sb", 103, [FEATURES, MLP])
        w_inner_sb = at("w_inner_sb", 103.5, [MLP, 2, MLP])
        angle = at("angle", 104, [MLP, S])
        turns = at("turns", 105, [MLP, S])
        hidden = at("hidden", 204, [MLP, 2, S + 1])
        params_raw = at("params_raw", 106, [P, PARAM_TILES, P])
        x = at("x", 191.75, [P, KT, S])
        scaled = at("scaled", 174, [P, 2, 4, S])
        squares = at("squares", 186, [P, 1, 4, S])
        b_hi = at("b_hi", 142, [P, KT, S], F32R)
        b_lo = at("b_lo", 158, [P, KT, S], F32R)
        q = at("q", 174, [P, 2, 4, S])
        prob = at("prob", 182, [P, 2, S])
        prob_t = at("prob_t", 184, [P, 2, S])
        h_hi = at("h_hi", 86, [P, SLABS * 4, S], F32R)
        h_lo = at("h_lo", 130, [P, SLABS * 4, S], F32R)
        gate = at("gate", 174, [P, 4, S])
        silu = at("silu", 178, [P, 4, S])
        hv = at("hv", 182, [P, 4, S])
        ffn_par = at("ffn_par", 190, [P, 16])
        y_out = at("y_out", 86, [P, KT, S])

        stream = ctx.enter_context(nc.psum_tensor("stream", [P, 4, 2, S], F32))
        side = ctx.enter_context(nc.psum_tensor("side", [P, 4, 512], F32))

        def stream_bank(b):
            return stream[:, b, :, :]

        raw_landed = [sem(f"raw_landed{i}") for i in range(RING)]
        hi_done, lo_done, piece_used = sem("hi_done"), sem("lo_done"), sem("piece_used")
        stream_full = [sem(f"stream_full{b}") for b in range(4)]
        stream_free = [sem(f"stream_free{b}") for b in range(4)]
        side_full = {b: sem(f"side_full_{b}") for b in "LR"}
        side_free = {b: sem(f"side_free_{b}") for b in "LR"}
        params_landed, mlp_landed, x_landed = sem("params_landed"), sem("mlp_landed"), sem("x_landed")
        dft_landed, decay_landed = sem("dft_landed"), sem("decay_landed")
        w_filt_landed, skip_landed = sem("w_filt_landed"), sem("skip_landed")
        mem_landed, x_again_landed = sem("mem_landed"), sem("x_again_landed")
        out_written = sem("out_written")
        zeroed, ident_made, made = sem("zeroed"), sem("ident_made"), sem("made")
        angle_step, sin_done = sem("angle_step"), sem("sin_done")
        squared, squares_used, rms_ready = sem("squared"), sem("squares_used"), sem("rms_ready")
        scaled_done, a_hi_done, a_ready = sem("scaled_done"), sem("a_hi_done"), sem("a_ready")
        k_squared, k_norm_ready = sem("k_squared"), sem("k_norm_ready")
        k_folded, spec_done = sem("k_folded"), sem("spec_done")
        short_center, short_left = sem("short_center"), sem("short_left")
        product_step, product_done = sem("product_step"), sem("product_done")
        conf_center, conf_taps = sem("conf_center"), sem("conf_taps")
        conf_squared, ln_step, conf_done = sem("conf_squared"), sem("ln_step"), sem("conf_done")
        peak_done, shift_done = sem("peak_done"), sem("shift_done")
        inv_total_done, prob_ready, o_hi_done = sem("inv_total_done"), sem("prob_ready"), sem("o_hi_done")
        ffn_par_ready, gate_center, gate_left = sem("ffn_par_ready"), sem("gate_center"), sem("gate_left")
        silu_done, h_hi_done, h_ready = sem("silu_done"), sem("h_hi_done"), sem("h_ready")
        down_full, down_added = sem("down_full"), sem("down_added")

        block = ctx.enter_context(nc.Block())

        def norm_phase(n):
            return [(x_first, "g_mix", squares_x, 2, scaled_x, "L"),
                    (mem_x, "g_mem", squares_m, 2, scaled_m, "R"),
                    (x, "g_xattn", squares, 1, scaled, "R"),
                    (x, "g_ffn", squares, 1, scaled, "R"),
                    (x, "g_final", squares, 1, scaled, "L")][n]

        def pair(b):
            return side[:, 0:2, :] if b == "L" else side[:, 2:4, :]

        A_PHASE = [0, 1, 3, 4]
        A_FREE = [0, 8 * K0, 8 * OUT0, 8 * Q0, 8 * O0]
        FFN_PIECE0 = 8 * PANELS
        DOWN_PIECE0 = FFN_PIECE0 + 16 * SLABS

        @block.sync
        def _(sp):
            def panel_source(panel):
                if panel < 4:
                    kind, i = CONF_PANELS[panel]
                    return w_in, (CONF if kind == "gate" else 0) + i * HALF
                if panel < K0:
                    part, half = HYENA_PANELS[panel - 4]
                    return w_in, 2 * CONF + part * HY + half * HALF
                for w, first in ((w_k, K0), (w_v, V0), (w_out, OUT0), (w_q, Q0), (w_o, O0)):
                    if first <= panel < first + 4:
                        return w, (panel - first) * HALF

            def rows(w, r0, c0):
                return w[bass.ds(r0, 256), bass.ds(c0, HALF)].rearrange("(k p) n -> p k n", p=P)

            def load_piece(p, source, lap):
                slot = p % RING
                sp.dma_start(raw[:, slot, :].rearrange("p (k n) -> p k n", k=2),
                             source).then_inc(raw_landed[slot], 16)

            sp.dma_start(params_raw[:, :, :], params).then_inc(params_landed, 16)
            sp.dma_start(feat[:, :], features).then_inc(mlp_landed, 16)
            sp.dma_start(w1_sb[:, :], w1).then_inc(mlp_landed, 16)
            sp.dma_start(w_inner_sb[:, :, :], w_inner.rearrange("l k n -> k l n")).then_inc(mlp_landed, 16)
            for g in range(4):
                sp.dma_start(x_first[:, 4 * g:4 * g + 4, :], x_t[:, 4 * g:4 * g + 4, :]).then_inc(x_landed, 16)
            for s in range(SLOTS):
                f = s // 3
                if s % 3 == 0 and f < 4:
                    if f:
                        sp.wait_ge(side_full["R"], filled(f"taps{f - 1}", "R"))
                    half, order = f // 2, f % 2
                    w = w_filt.rearrange("k (o d c) -> k o d c", o=2, d=2)
                    sp.dma_start(w_filt_sb[:, :, :], w[:, order, :, half * HALF:(half + 1) * HALF]).then_inc(w_filt_landed, 16)
                if s % 6 == 0 and s < 12:
                    if s:
                        sp.wait_ge(side_free["R"], emptied("taps1", "R"))
                    sp.dma_start(decay_sb[:, :, :], decay[s // 6]).then_inc(decay_landed, 16)
                if s % 3 == 2 and f < 4:
                    if f:
                        sp.wait_ge(spec_done, f)
                    half, order = f // 2, f % 2
                    sp.dma_start(skip_sb[:, :], skip[order:order + 1, half * HALF:(half + 1) * HALF]
                                 .to_broadcast([P, HALF])).then_inc(skip_landed, 16)
                if s == 0:
                    sp.dma_start(dft_sb[:, :, :], dft).then_inc(dft_landed, 16)
                    sp.dma_start(idft_sb[:, :, :], idft).then_inc(dft_landed, 16)
                if s == 14:
                    sp.wait_ge(side_full["L"], filled("spec_im3", "L"))
                    sp.dma_start(mem_x[:, :, :], mem_t).then_inc(mem_landed, 16)
                if s == 38:
                    sp.wait_ge(a_ready, 12)
                    sp.dma_start(x[:, :, :], x_t).then_inc(x_again_landed, 16)
                for p in range(4 * s, 4 * s + 4):
                    if p >= RING:
                        sp.wait_ge(lo_done, p - RING + 1)
                    w, c0 = panel_source(p // 8)
                    load_piece(p, rows(w, (p % 8) * 256, c0), p // RING)
            with sp.Fori(0, SLABS) as i:
                for j in range(16):
                    sp.wait_ge(lo_done, i * 16 + (FFN_PIECE0 + j - RING + 1))
                    load_piece(j, rows(w_up, (j % 8) * 256, i * HALF + (j // 8) * FF), None)
            with sp.Fori(0, SLABS) as g:
                for j in range(8):
                    sp.wait_ge(lo_done, g * 8 + (DOWN_PIECE0 + j - RING + 1))
                    load_piece(j, rows(w_down, g * 512 + (j % 2) * 256, (j // 2) * HALF), None)
            for g in range(4):
                sp.wait_ge(scaled_done, 4 * 4 + g + 1)
                sp.dma_start(out[:, 4 * g:4 * g + 4, :], y_out[:, 4 * g:4 * g + 4, :]).then_inc(out_written, 16)
            sp.wait_ge(out_written, 64)

        @block.gpsimd
        def _(pool):
            pool.memset(ident[:, :], 0.0).then_inc(zeroed, 1)
            pool.memset(ones[:, :], 1.0).then_inc(made, 1)
            pool.memset(eps[:, :], EPS).then_inc(made, 1)
            pool.memset(hidden[:, :, 0:1], 0.0).then_inc(made, 1)
            pool.wait_ge(zeroed, 1)
            pool.affine_select(out=ident[:, :], in_=ident[:, :], compare_op=ALU.not_equal, fill=1.0,
                               base=0, pattern=[[-1, P]], channel_multiplier=1).then_inc(ident_made, 1)

        @block.tensor
        def _(pe):
            def products(out_, wh, wl, ah, al, start, stop, shared):
                pe.matmul(out_, wh, ah, start=start, stop=False, skip_group_check=shared)
                pe.matmul(out_, wh, al, start=False, stop=False, skip_group_check=shared)
                return pe.matmul(out_, wl, ah, start=False, stop=stop, skip_group_check=shared)

            def half_panel(s):
                panel, first = s // 2, (s % 2) * 4
                banks = (panel % 2) * 2
                act_hi, act_lo = (b_hi, b_lo) if panel >= O0 else (a_hi, a_lo)
                if s % 2 == 0 and panel >= 2:
                    for b in (banks, banks + 1):
                        pe.wait_ge(stream_free[b], panel // 2)
                for j in range(first, first + 4):
                    phase = [0, K0, OUT0, Q0].index(panel) if panel in (0, K0, OUT0, Q0) else None
                    if phase is not None and j % 2 == 0:
                        pe.wait_ge(a_ready, 4 * phase + j // 2 + 1)
                    if panel == O0 and j % 2 == 0:
                        pe.wait_ge(side_free["L"], emptied(f"pv{j // 2}", "L"))
                    p = 8 * panel + j
                    pe.wait_ge(lo_done, p + 1)
                    piece(banks, p % RING, j, V0 <= panel < OUT0, act_hi, act_lo, 2 * j,
                          j == 0, j == 7)
                    if panel == O0 and j == 5:
                        attend(3)

            def piece(banks, slot, j, swapped, act_hi, act_lo, kt, first, last):
                if swapped:
                    for m in range(2):
                        for k in range(2):
                            a = bass.ts(m, P)
                            w = bass.ts(k, HALF)
                            mm = products(stream_bank(banks + m).rearrange("p a b -> p (a b)"),
                                          act_hi[:, kt + k, a], act_lo[:, kt + k, a],
                                          w_hi[:, slot, w], w_lo[:, slot, w],
                                          first and k == 0, last and k == 1, False)
                        if last and m == 0:
                            mm.then_inc(stream_full[banks], 1)
                    mm.then_inc(piece_used, 1)
                    return
                for t in range(4):
                    for k in range(2):
                        w = bass.ds(k * HALF + t * P, P)
                        mm = products(stream[:, banks + t // 2, t % 2, :],
                                      w_hi[:, slot, w], w_lo[:, slot, w],
                                      act_hi[:, kt + k, :], act_lo[:, kt + k, :],
                                      first and t % 2 == 0 and k == 0, last and k == 1, True)
                    if last and t == 1:
                        mm.then_inc(stream_full[banks], 1)
                mm.then_inc(piece_used, 1)

            def claim(name, pairs):
                for b in pairs:
                    if before(name, b):
                        pe.wait_ge(side_free[b], before(name, b))

            def statistics(n, groups):
                b = norm_phase(n)[5]
                bufs, count = norm_phase(n)[2], norm_phase(n)[3]
                for g in groups:
                    if g == 0 and n < 4:
                        claim(f"stats{n}", b)
                    pe.wait_ge(squared, 4 * n + g + 1)
                    for j in range(4):
                        mm = pe.matmul(pair(b)[:, 0, 0:S], ones[:, :], bufs[:, g % count, j, :],
                                       start=(g == 0 and j == 0), stop=(g == 3 and j == 3))
                    mm.then_inc(squares_used, 1)

            def mlp_layer(layer):
                claim(f"mlp{layer}", "R")
                if layer == 0:
                    pe.wait_ge(mlp_landed, 48)
                    w, h = w1_sb[:, :], feat[:, :]
                else:
                    pe.wait_ge(sin_done, layer)
                    w, h = w_inner_sb[:, layer - 1, :], hidden[:, (layer - 1) % 2, 1:S + 1]
                pe.matmul(side[0:MLP, 2, 0:S], w, h, start=True, stop=True).then_inc(side_full["R"], 1)

            def filter_taps(f):
                claim(f"taps{f}", "LR")
                pe.wait_ge(w_filt_landed, 16 * (f + 1))
                if f == 0:
                    pe.wait_ge(sin_done, 3)
                    pe.wait_ge(made, 3)
                for d in range(2):
                    for t in range(2):
                        mm = pe.matmul(side[:, 2 * d + t, :], hidden[:, 0, bass.ds(1 - d + t * P, P)],
                                       w_filt_sb[:, d, :], start=True, stop=True)
                    mm.then_inc(side_full["LR"[d]], 1)

            def filter_energy(f):
                claim(f"energy{f}", "L")
                pe.wait_ge(k_squared, f + 1)
                for j in range(4):
                    mm = pe.matmul(side[:, 0, :], ones[:, :], folded[:, j, :], start=(j == 0), stop=(j == 3))
                mm.then_inc(side_full["L"], 1)

            def spectrum_tile(bank, column, part):
                for k in range(2):
                    mm = pe.matmul(side[:, bank, :], dft_sb[:, k, bass.ts(column, P)],
                                   folded[:, 2 * part + k, :], start=(k == 0), stop=(k == 1))
                return mm

            def filter_spectrum(f):
                claim(f"spec{f}", "LR")
                if f == 0:
                    pe.wait_ge(dft_landed, 32)
                pe.wait_ge(k_folded, 2 * f + 1)
                spectrum_tile(0, 0, 0)
                spectrum_tile(1, 1, 0).then_inc(side_full["L"], 1)
                spectrum_tile(2, 5, 0)
                pe.wait_ge(k_folded, 2 * f + 2)
                spectrum_tile(3, 4, 1).then_inc(side_full["R"], 1)
                claim(f"spec_im{f}", "L")
                spectrum_tile(0, 3, 1).then_inc(side_full["L"], 1)

            def turn(e):
                claim(f"turn{e}", "L")
                for b in range(2):
                    bank = ((4 + e) % 2) * 2 + b
                    pe.wait_ge(stream_free[bank], (4 + e) // 2 + 1)
                for t in range(2):
                    for c in range(4):
                        mm = pe.transpose(side[:, t, bass.ts(c, P)], turned[:, c, bass.ts(t, P)], ident[:, :])
                mm.then_inc(side_full["L"], 1)

            def transform(c):
                claim(f"dft{c}", "LR")
                order, half = c // 2, c % 2
                if order == 0:
                    pe.wait_ge(side_free["L"], emptied(f"turn{2 * half}", "L"))
                else:
                    pe.wait_ge(side_free["L"], emptied(f"idft{half}", "L"))
                source = (v_t, x1_t)[order]
                for j in range(4):
                    for k in range(2):
                        mm = pe.matmul(side[:, j, :], dft_sb[:, k, bass.ts(j, P)], source[:, half, k, :],
                                       start=(k == 0), stop=(k == 1))
                    if j % 2:
                        mm.then_inc(side_full["LR"[j // 2]], 1)

            def transform_back(c):
                claim(f"idft{c}", "L")
                pe.wait_ge(product_done, 2 * (c + 1))
                if c < 2:
                    for t in range(2):
                        for k in range(4):
                            mm = pe.matmul(side[:, t, :], idft_sb[:, k, bass.ts(t, P)], spectrum[:, k, :],
                                           start=(k == 0), stop=(k == 3))
                else:
                    for t in range(4):
                        for k in range(4):
                            mm = pe.matmul(side[:, t // 2, bass.ts(t % 2, S)], spectrum[:, k, bass.ts(t, P)],
                                           idft_sb[:, k, :], start=(k == 0), stop=(k == 3))
                mm.then_inc(side_full["L"], 1)

            def channel_sum(name, source):
                claim(name, "R")
                for j in range(8):
                    mm = pe.matmul(side[:, 2, 0:S], ones[:, :], source[:, j, :], start=(j == 0), stop=(j == 7))
                mm.then_inc(side_full["R"], 1)

            def scores(h):
                claim(f"scores{h}", "R")
                for b in range(2):
                    bank = ((Q0 + h) % 2) * 2 + b
                    pe.wait_ge(stream_free[bank], (Q0 + h) // 2 + 1)
                for t in range(2):
                    for k in range(4):
                        mm = pe.matmul(side[:, 2, bass.ts(t, S)], q[:, h % 2, k, bass.ts(t, P)],
                                       keys[:, 4 * h + k, :], start=(k == 0), stop=(k == 3))
                mm.then_inc(side_full["R"], 1)

            def turn_probs(h):
                claim(f"turn_p{h}", "L")
                pe.wait_ge(prob_ready, h + 1)
                for m in range(2):
                    for t in range(2):
                        mm = pe.transpose(side[:, 0, bass.ds(m * S + t * P, P)], prob[:, t, bass.ts(m, P)], ident[:, :])
                mm.then_inc(side_full["L"], 1)

            def attend(h):
                claim(f"pv{h}", "L")
                for t in range(4):
                    for m in range(2):
                        mm = pe.matmul(side[:, t // 2, bass.ts(t % 2, S)],
                                       values[:, m, bass.ds(h * HALF + t * P, P)], prob_t[:, m, :],
                                       start=(m == 0), stop=(m == 1))
                mm.then_inc(side_full["L"], 1)

            pe.wait_ge(ident_made, 1)
            pe.wait_ge(params_landed, 16)
            for t in range(PARAM_TILES):
                mm = pe.transpose(side[:, t // 4, bass.ts(t % 4, P)], params_raw[:, t, :], ident[:, :])
            mm.then_inc(side_full["L"], 1)
            for layer in range(3):
                mlp_layer(layer)
            pe.wait_ge(made, 1)
            statistics(0, range(4))
            for s in range(SLOTS):
                half_panel(s)
                if s < 12:
                    (filter_taps, filter_energy, filter_spectrum)[s % 3](s // 3)
                if s in (10, 12, 14, 16):
                    turn((s - 10) // 2)
                if s == 16:
                    statistics(1, (0, 1))
                if s == 17:
                    statistics(1, (2, 3))
                if s in (19, 22, 25, 28):
                    transform((s - 19) // 3)
                if s in (21, 24, 27, 30):
                    transform_back((s - 21) // 3)
                if s == 32:
                    pe.wait_ge(conf_taps, 8 * (TAPS - 1))
                    channel_sum("mean", conf)
                if s == 33:
                    pe.wait_ge(conf_squared, 1)
                    channel_sum("variance", u)
                if s in (38, 40, 42, 43):
                    statistics(2, ((s - 38) // 2 if s < 43 else 3,))
                if s in (48, 50):
                    attend(s // 2 - 24)
                if s in (46, 48, 50):
                    scores(s // 2 - 23)
                if s in (47, 49, 51):
                    turn_probs(s // 2 - 23)
                if s == 51:
                    scores(3)
                    attend(2)
                if s == 52:
                    turn_probs(3)
                if s in (54, 56, 58, 59):
                    statistics(3, ((s - 54) // 2 if s < 59 else 3,))
            for g in range(4):
                pe.wait_ge(a_ready, 4 * 4 + g + 1)
            with pe.Fori(0, SLABS) as i:
                for j in range(16):
                    if j % 8 == 0:
                        for b in (j // 4, j // 4 + 1):
                            pe.wait_ge(stream_free[b], i + PANELS // 2)
                    pe.wait_ge(lo_done, i * 16 + (FFN_PIECE0 + j + 1))
                    piece((j // 8) * 2, j % RING, j % 8, False, a_hi, a_lo, 2 * (j % 8), j % 8 == 0, j % 8 == 7)

            def down_tile(panel, t):
                if panel < 2:
                    return side[:, 2 * panel + t // 2, bass.ts(t % 2, S)]
                return stream[:, 2 * (panel - 2) + t // 2, t % 2, :]

            def down_group(g, first, last):
                for j in range(8):
                    panel, half = j // 2, j % 2
                    if first and half == 0:
                        if panel < 2:
                            b = "LR"[panel]
                            pe.wait_ge(side_free[b], SIDE_FREE_END[b])
                        else:
                            for b in (2 * (panel - 2), 2 * (panel - 2) + 1):
                                pe.wait_ge(stream_free[b], PANELS // 2 + SLABS)
                    pe.wait_ge(lo_done, g * 8 + (DOWN_PIECE0 + j + 1))
                    for t in range(4):
                        for k in range(2):
                            w = bass.ds(k * HALF + t * P, P)
                            kt = g * 4 + (2 * half + k)
                            mm = products(down_tile(panel, t), w_hi[:, j % RING, w], w_lo[:, j % RING, w],
                                          h_hi[:, bass.ds(kt, 1), :].rearrange("p a b -> p (a b)"),
                                          h_lo[:, bass.ds(kt, 1), :].rearrange("p a b -> p (a b)"),
                                          first and half == 0 and t % 2 == 0 and k == 0,
                                          last and half == 1 and k == 1, True)
                        if last and half == 1 and t == 1:
                            mm.then_inc(down_full, 1)
                    mm.then_inc(piece_used, 1)

            pe.wait_ge(h_ready, SLABS - 1)
            down_group(0, True, False)
            with pe.Fori(1, SLABS - 1) as g:
                down_group(g, False, False)
            pe.wait_ge(h_ready, SLABS)
            down_group(SLABS - 1, False, True)
            pe.wait_ge(down_added, 2)
            statistics(4, range(4))

        def wait_bank(eng, panel, b):
            if b == 0:
                eng.wait_ge(stream_full[(panel % 2) * 2], panel // 2 + 1)
            else:
                eng.wait_ge(piece_used, 8 * panel + 8)

        @block.scalar
        def _(act):
            def split(s):
                for p in range(4 * s, 4 * s + 4):
                    act.wait_ge(raw_landed[p % RING], 16 * (p // RING + 1))
                    if p >= RING:
                        act.wait_ge(piece_used, p - RING + 1)
                    act.activation(w_hi[:, p % RING, :], raw[:, p % RING, :], ACT.Copy).then_inc(hi_done, 1)

            def evacuate(panel, tiles):
                for b in range(2):
                    bank = (panel % 2) * 2 + b
                    wait_bank(act, panel, b)
                    act.activation(tiles(b), stream_bank(bank), ACT.Copy).then_inc(stream_free[bank], 1)

            def square(n, g):
                source, _, bufs, count, _, _ = norm_phase(n)
                used = 4 * n + g + 1 - count
                if used > 0:
                    act.wait_ge(squares_used, used)
                act.activation(bufs[:, g % count, :, :], source[:, 4 * g:4 * g + 4, :], ACT.Square).then_inc(squared, 1)

            def rms_root(n):
                b = norm_phase(n)[5]
                act.wait_ge(squares_used, 4 * n + 4)
                act.activation(root[:, :], pair(b)[:, 0, 0:S], ACT.Sqrt, bias=eps[:, 0:1],
                               scale=1.0 / D).then_inc(side_free[b], 1)

            def split_scaled(n):
                m = A_PHASE[n]
                for g in range(4):
                    act.wait_ge(scaled_done, 4 * n + g + 1)
                    if g == 0 and m:
                        act.wait_ge(piece_used, A_FREE[m])
                    act.activation(a_hi[:, 4 * g:4 * g + 4, :], norm_phase(n)[4][:, g % 2, :, :],
                                   ACT.Copy).then_inc(a_hi_done, 1)

            def column(name, i):
                return par[:, COL[name] + i:COL[name] + i + 1]

            def short_centers(e):
                panel = 4 + e
                part, half = HYENA_PANELS[e]
                if 1 <= e < 4:
                    act.wait_ge(side_full["L"], filled(f"turn{e - 1}", "L"))
                for t in range(4):
                    if t % 2 == 0:
                        wait_bank(act, panel, t // 2)
                    c = part * 8 + half * 4 + t
                    to = x2[:, 4 * half + t, :] if part == 2 else turned[:, t, :]
                    act.activation(to, stream[:, (panel % 2) * 2 + t // 2, t % 2, :], ACT.Identity,
                                   bias=column("short_b", c), scale=column("short_w", 24 + c)).then_inc(short_center, 1)

            def evacuate_turned(e):
                part, half = HYENA_PANELS[e]
                act.wait_ge(side_full["L"], filled(f"turn{e}", "L"))
                act.activation((v_t, x1_t)[part][:, half, :, :], pair("L"), ACT.Copy).then_inc(side_free["L"], 1)

            def filter_square(f):
                act.wait_ge(side_free["R"], emptied(f"taps{f}", "R"))
                if f:
                    act.wait_ge(side_full["L"], filled(f"spec_im{f - 1}", "L"))
                act.activation(folded[:, :, :], taps[:, :, :], ACT.Square).then_inc(k_squared, 1)

            def filter_root(f):
                act.wait_ge(side_full["L"], filled(f"energy{f}", "L"))
                if f:
                    act.wait_ge(spec_done, f)
                act.activation(k_norm[:, :], side[:, 0, :], ACT.Sqrt, bias=eps[:, 0:1]).then_inc(side_free["L"], 1)

            def conf_centers(i):
                for b in range(2):
                    act.wait_ge(stream_free[2 + b], i + 1)
                for t in range(4 * i, 4 * i + 4):
                    act.activation(conf[:, t, :], u[:, t, :], ACT.Identity, bias=column("conf_b", t),
                                   scale=column("conf_w", (TAPS // 2) * 8 + t)).then_inc(conf_center, 1)

            def softmax(h):
                act.wait_ge(shift_done, h + 1)
                if h:
                    act.wait_ge(side_full["L"], filled(f"turn_p{h - 1}", "L"))
                for t in range(2):
                    e = act.activation(prob[:, t, :], side[:, 2, bass.ts(t, S)], ACT.Exp, bias=shift[:, t:t + 1],
                                       scale=SM_SCALE, accum_out=total[:, t:t + 1])
                e.then_inc(side_free["R"], 1)

            def evacuate_probs(h):
                act.wait_ge(side_full["L"], filled(f"turn_p{h}", "L"))
                act.activation(prob_t[:, :, :], side[:, 0, :].rearrange("p (a b) -> p a b", a=2), ACT.Copy).then_inc(side_free["L"], 1)

            def split_head(h):
                act.wait_ge(side_full["L"], filled(f"pv{h}", "L"))
                act.activation(b_hi[:, 4 * h:4 * h + 4, :], pair("L").rearrange("p a (t s) -> p (a t) s", t=2),
                               ACT.Copy).then_inc(o_hi_done, 1)

            act.wait_ge(side_full["L"], filled("params", "L"))
            n = min(PARAM_TILES, 4) * P
            act.activation(par[:, 0:n], side[:, 0, 0:n], ACT.Copy)
            act.activation(par[:, n:PARAM_TILES * P], side[:, 1, 0:PARAM_TILES * P - n], ACT.Copy).then_inc(side_free["L"], 1)
            for layer in range(3):
                act.wait_ge(angle_step, 5 * (layer + 1))
                act.activation(hidden[:, layer % 2, 1:S + 1], angle[:, :], ACT.Sin).then_inc(sin_done, 1)
            for g in range(4):
                act.wait_ge(x_landed, 64)
                square(0, g)
            act.wait_ge(made, 3)
            rms_root(0)
            split(0)
            split_scaled(0)
            for s in range(SLOTS):
                if s + 1 < SLOTS:
                    split(s + 1)
                else:
                    for j in range(4):
                        p = FFN_PIECE0 + j
                        act.wait_ge(raw_landed[j], 16 * (p // RING + 1))
                        act.wait_ge(piece_used, p - RING + 1)
                        act.activation(w_hi[:, j, :], raw[:, j, :], ACT.Copy).then_inc(hi_done, 1)
                if s < 12 and s % 3 == 0:
                    filter_square(s // 3)
                if s < 12 and s % 3 == 1:
                    filter_root(s // 3)
                if s in (1, 5):
                    i = s // 4
                    if i:
                        for b in range(2):
                            act.wait_ge(stream_free[2 + b], i)
                    for b in range(2):
                        wait_bank(act, 2 * i, b)
                        act.activation(sigm[:, 2 * b:2 * b + 2, :], stream_bank(b), ACT.Sigmoid).then_inc(stream_free[b], 1)
                if s in (3, 7):
                    conf_centers(s // 4)
                if s in (10, 12, 14, 16):
                    evacuate_turned((s - 10) // 2)
                if s in (9, 11, 13, 15, 17, 19):
                    short_centers((s - 9) // 2)
                if s in (15, 16):
                    if s == 15:
                        act.wait_ge(mem_landed, 16)
                    for g in ((0, 1), (2, 3))[s - 15]:
                        square(1, g)
                if s == 17:
                    rms_root(1)
                if s == 19:
                    split_scaled(1)
                if s in (21, 23, 25, 27):
                    i = (s - 21) // 2
                    evacuate(K0 + i, lambda b: keys[:, 4 * i + 2 * b:4 * i + 2 * b + 2, :])
                if s in (29, 31, 33, 35):
                    i = (s - 29) // 2
                    evacuate(V0 + i, lambda b: values[:, b, i * HALF:(i + 1) * HALF].rearrange("p (a s) -> p a s", a=2))
                if s == 32:
                    act.wait_ge(side_free["R"], emptied("mean", "R"))
                    act.activation(u[:, :, :], conf[:, :, :], ACT.Square).then_inc(conf_squared, 1)
                if s == 33:
                    act.wait_ge(side_full["R"], filled("variance", "R"))
                    act.activation(root[:, :], side[:, 2, 0:S], ACT.Sqrt, bias=eps[:, 0:1], scale=1.0 / CONF).then_inc(side_free["R"], 1)
                if s == 34:
                    for t in range(8):
                        if t % 4 == 0:
                            act.wait_ge(ln_step, 2 + t // 4)
                        act.activation(conf[:, t, :], conf[:, t, :], ACT.Silu, bias=column("ln_b", t),
                                       scale=column("ln_g", t)).then_inc(conf_done, 1)
                if s == 35:
                    act.wait_ge(piece_used, A_FREE[2])
                    act.wait_ge(conf_done, 8)
                    for g in range(4):
                        if g == 2:
                            act.wait_ge(side_free["L"], emptied("idft3", "L"))
                        source = conf[:, 4 * g:4 * g + 4, :] if g < 2 else x2[:, 4 * g - 8:4 * g - 4, :]
                        act.activation(a_hi[:, 4 * g:4 * g + 4, :], source, ACT.Copy).then_inc(a_hi_done, 1)
                if s in (37, 39, 41, 43, 53, 55, 57, 59):
                    g = (s - 37) // 2 % 4
                    n = 2 if s < 44 else 3
                    for b in range(2):
                        panel = s // 2
                        act.wait_ge(stream_free[(panel % 2) * 2 + b], panel // 2 + 1)
                    square(n, g)
                    if g == 3:
                        rms_root(n)
                        split_scaled(n)
                if s in (45, 47, 49, 51):
                    h = (s - 45) // 2
                    if h >= 2:
                        act.wait_ge(side_full["R"], filled(f"scores{h - 2}", "R"))
                    evacuate(Q0 + h, lambda b: q[:, h % 2, 2 * b:2 * b + 2, :])
                if s in (47, 49):
                    evacuate_probs((s - 47) // 2)
                if s in (48, 50):
                    split_head((s - 48) // 2)
                if s in (46, 48, 50):
                    softmax((s - 46) // 2)
                if s == 51:
                    evacuate_probs(2)
                    softmax(3)
                    split_head(2)
                if s == 52:
                    evacuate_probs(3)
                    split_head(3)
            with act.Fori(0, SLABS) as i:
                for j in range(4, 20):
                    act.wait_ge(raw_landed[j % RING], i * 64 + 16 * ((FFN_PIECE0 + j) // RING + 1))
                    act.wait_ge(piece_used, i * 16 + (FFN_PIECE0 + j - RING + 1))
                    act.activation(w_hi[:, j % RING, :], raw[:, j % RING, :], ACT.Copy).then_inc(hi_done, 1)
                    if j == 11:
                        act.wait_ge(ffn_par_ready, i + 1)
                        act.wait_ge(hi_done, i * 16 + (FFN_PIECE0 + j + 1))
                        for t in range(4):
                            if t == 0:
                                act.wait_ge(stream_full[0], i + (PANELS // 2 + 1))
                            if t == 2:
                                act.wait_ge(piece_used, i * 16 + (FFN_PIECE0 + 8))
                            act.activation(gate[:, t, :], stream[:, t // 2, t % 2, :], ACT.Identity,
                                           bias=ffn_par[:, 12 + t:13 + t], scale=ffn_par[:, 4 + t:5 + t]).then_inc(gate_center, 1)
                        for b in range(2):
                            act.wait_ge(stream_free[b], i + (PANELS // 2 + 1))
                        act.wait_ge(stream_free[3], i + PANELS // 2)
                        act.activation(silu[:, :, :], gate[:, :, :], ACT.Silu).then_inc(silu_done, 1)
                act.wait_ge(stream_free[3], i + (PANELS // 2 + 1))
                act.activation(h_hi[:, bass.ds(i * 4, 4), :], hv[:, :, :], ACT.Copy).then_inc(h_hi_done, 1)
            def split_down(g, first, last):
                for j in range(first, last):
                    act.wait_ge(raw_landed[j % RING], g * 32 + 16 * ((DOWN_PIECE0 + j) // RING + 1))
                    act.wait_ge(piece_used, g * 8 + (DOWN_PIECE0 + j - RING + 1))
                    act.activation(w_hi[:, j % RING, :], raw[:, j % RING, :], ACT.Copy).then_inc(hi_done, 1)

            with act.Fori(0, SLABS - 1) as g:
                split_down(g, 4, 12)
            split_down(SLABS - 1, 4, 8)
            for g in range(4):
                act.wait_ge(down_added, 2 * g + 2)
                square(4, g)
            act.wait_ge(squares_used, 20)
            act.activation(root[:, :], side[:, 0, 0:S], ACT.Sqrt, bias=eps[:, 0:1], scale=1.0 / D).then_inc(side_free["L"], 1)

        @block.vector
        def _(dve):
            rounds = iter(range(2 * (TAPS - 1)))

            def conf_round():
                r = next(rounds, None)
                if r is None:
                    return
                i, tap = r // (TAPS - 1), r % (TAPS - 1)
                off = [j for j in range(TAPS) if j != TAPS // 2][tap] - TAPS // 2
                a, b = max(0, -off), S - max(0, off)
                for t in range(4):
                    c = 4 * i + t
                    if tap == 0:
                        dve.wait_ge(conf_center, c + 1)
                    else:
                        dve.wait_ge(conf_taps, 4 * (r - 1) + t + 1)
                    w = COL["conf_w"] + (off + TAPS // 2) * 8 + c
                    dve.scalar_tensor_tensor(out=conf[:, c, a:b], in0=u[:, c, a + off:b + off],
                                             scalar=par[:, w:w + 1], in1=conf[:, c, a:b],
                                             op0=ALU.mult, op1=ALU.add).then_inc(conf_taps, 1)

            def split(s, conv):
                for j in range(4):
                    p = 4 * s + j
                    dve.wait_ge(hi_done, p + 1)
                    dve.tensor_tensor(w_lo[:, p % RING, :], raw[:, p % RING, :],
                                      w_hi[:, p % RING, :].bitcast(F32), ALU.subtract).then_inc(lo_done, 1)
                    if j >= 4 - conv:
                        conf_round()

            def rms_inverse(n):
                b = norm_phase(n)[5]
                dve.wait_ge(side_free[b], emptied(f"stats{n}", b) if n < 4 else SIDE_FREE_END["L"] + 1)
                dve.reciprocal(inv_rms[:, :], root[:, :]).then_inc(rms_ready, 1)
                dve.wait_ge(rms_ready, n + 1)

            def scale_group(n, g):
                source, gain, _, _, bufs, _ = norm_phase(n)
                m = A_PHASE[n]
                if g >= 2:
                    dve.wait_ge(a_ready, 4 * m + g - 1)
                for j in range(4):
                    c = COL[gain] + 4 * g + j
                    op = dve.scalar_tensor_tensor(out=bufs[:, g % 2, j, :], in0=source[:, 4 * g + j, :],
                                                  scalar=par[:, c:c + 1], in1=inv_rms[:, :],
                                                  op0=ALU.mult, op1=ALU.mult)
                op.then_inc(scaled_done, 1)

            def split_lo(m, g, source):
                dve.wait_ge(a_hi_done, 4 * m + g + 1)
                dve.tensor_tensor(a_lo[:, 4 * g:4 * g + 4, :], source,
                                  a_hi[:, 4 * g:4 * g + 4, :].bitcast(F32), ALU.subtract).then_inc(a_ready, 1)

            def norm_split(n):
                m, bufs = A_PHASE[n], norm_phase(n)[4]
                scale_group(n, 0)
                for g in range(4):
                    if g < 3:
                        scale_group(n, g + 1)
                    split_lo(m, g, bufs[:, g % 2, :, :])

            def add_panel(panel, i):
                for b in range(2):
                    bank = (panel % 2) * 2 + b
                    wait_bank(dve, panel, b)
                    rows = x[:, 4 * i + 2 * b:4 * i + 2 * b + 2, :]
                    dve.tensor_tensor(rows, stream_bank(bank), rows, ALU.add).then_inc(stream_free[bank], 1)

            def short_sides(e):
                panel = 4 + e
                part, half = HYENA_PANELS[e]
                for b in range(2):
                    bank = (panel % 2) * 2 + b
                    dve.wait_ge(short_center, 4 * e + 2 * b + 2)
                    for side_ in range(2):
                        for t in range(2):
                            to = x2[:, 4 * half + 2 * b + t, :] if part == 2 else turned[:, 2 * b + t, :]
                            c = COL["short_w"] + 48 * side_ + part * 8 + half * 4 + 2 * b + t
                            o, i_ = ((1, S), (0, S - 1)) if side_ == 0 else ((0, S - 1), (1, S))
                            if side_:
                                dve.wait_ge(short_left, 4 * e + 2 * b + t + 1)
                            op = dve.scalar_tensor_tensor(out=to[:, o[0]:o[1]], in0=stream[:, bank, t, i_[0]:i_[1]],
                                                          scalar=par[:, c:c + 1], in1=to[:, o[0]:o[1]],
                                                          op0=ALU.mult, op1=ALU.add)
                            if side_ == 0:
                                op.then_inc(short_left, 1)
                            elif t:
                                op.then_inc(stream_free[bank], 1)

            def filter_window(f):
                if f % 2 == 0:
                    dve.wait_ge(decay_landed, 16 * (f // 2 + 1))
                if f:
                    dve.wait_ge(k_folded, 2 * f)
                for d in range(2):
                    dve.wait_ge(side_full["LR"[d]], filled(f"taps{f}", "LR"[d]))
                    dve.tensor_tensor(taps[:, 2 * d:2 * d + 2, :], side[:, 2 * d:2 * d + 2, :],
                                      decay_sb[:, 2 * d:2 * d + 2, :], ALU.mult).then_inc(side_free["LR"[d]], 1)

            def filter_fold(f):
                dve.wait_ge(side_free["L"], emptied(f"energy{f}", "L"))
                dve.tensor_tensor(folded[:, 0:2, :], taps[:, 0:2, :], taps[:, 2:4, :], ALU.add).then_inc(k_folded, 1)
                dve.tensor_tensor(folded[:, 2:4, :], taps[:, 0:2, :], taps[:, 2:4, :], ALU.subtract).then_inc(k_folded, 1)
                dve.reciprocal(k_norm[:, :], k_norm[:, :]).then_inc(k_norm_ready, 1)

            def filter_finish(f):
                to = spec[f % 2]
                half = f // 2
                dve.wait_ge(k_norm_ready, f + 1)
                dve.wait_ge(side_full["L"], filled(f"spec{f}", "L"))
                norm2 = k_norm[:, :].rearrange("p (a n) -> p a n", a=1).to_broadcast([P, 2, HALF])
                dve.tensor_tensor(to[:, half, 0:2, :], pair("L"), norm2, ALU.mult).then_inc(side_free["L"], 1)
                dve.wait_ge(side_full["R"], filled(f"spec{f}", "R"))
                dve.tensor_tensor(to[:, half, 2:4, :], pair("R"), norm2, ALU.mult).then_inc(side_free["R"], 1)
                dve.wait_ge(side_full["L"], filled(f"spec_im{f}", "L"))
                dve.tensor_tensor(to[:, half, 4, :], side[:, 0, :], k_norm[:, :], ALU.mult).then_inc(side_free["L"], 1)
                dve.wait_ge(skip_landed, 16 * (f + 1))
                dve.wait_ge(side_free["L"], emptied(f"spec_im{f}", "L"))
                skip3 = skip_sb[:, :].rearrange("p (a n) -> p a n", a=1).to_broadcast([P, 3, HALF])
                dve.tensor_tensor(to[:, half, 0:3, :], to[:, half, 0:3, :], skip3, ALU.add).then_inc(spec_done, 1)

            def multiply(c):
                order, half = c // 2, c % 2
                k = spec[order]
                real, real_nyq = [k[:, half, 0, :], k[:, half, 1, :]], [k[:, half, 2, :], k[:, half, 1, :]]
                if c == 0:
                    dve.wait_ge(a_ready, 8)
                dve.wait_ge(side_full["L"], filled(f"dft{c}", "L"))
                dve.tensor_tensor(spectrum[:, 0:2, :], pair("L"), k[:, half, 0:2, :], ALU.mult)
                dve.tensor_tensor(spectrum[:, 2:4, :], pair("L"), k[:, half, 3:5, :], ALU.mult).then_inc(side_free["L"], 1)
                dve.wait_ge(side_full["R"], filled(f"dft{c}", "R"))
                if c:
                    dve.wait_ge(product_done, 2 * c)
                dve.tensor_tensor(cross[:, :, :], pair("R"), k[:, half, 3:5, :], ALU.mult).then_inc(product_step, 1)
                dve.wait_ge(product_step, 2 * c + 1)
                dve.tensor_tensor(spectrum[:, 0:2, :], spectrum[:, 0:2, :], cross[:, :, :], ALU.subtract).then_inc(product_done, 1)
                dve.wait_ge(product_done, 2 * c + 1)
                dve.tensor_tensor(cross[:, 0, :], side[:, 2, :], real_nyq[0], ALU.mult).then_inc(product_step, 1)
                dve.tensor_tensor(cross[:, 1, :], side[:, 3, :], real_nyq[1], ALU.mult).then_inc(side_free["R"], 1)
                dve.wait_ge(side_free["R"], emptied(f"dft{c}", "R"))
                dve.tensor_tensor(spectrum[:, 2:4, :], spectrum[:, 2:4, :], cross[:, :, :], ALU.add).then_inc(product_done, 1)

            def gate_by(c):
                dve.wait_ge(side_full["L"], filled(f"idft{c}", "L"))
                half = c % 2
                if c < 2:
                    to = x1_t[:, half, :, :]
                    dve.wait_ge(side_free["L"], emptied(f"turn{2 * half + 1}", "L"))
                    dve.tensor_tensor(to, pair("L"), to, ALU.mult).then_inc(side_free["L"], 1)
                else:
                    to = x2[:, 4 * half:4 * half + 4, :]
                    dve.tensor_tensor(to, pair("L").rearrange("p a (t s) -> p (a t) s", t=2), to,
                                      ALU.mult).then_inc(side_free["L"], 1)

            def softmax_shift(h):
                dve.wait_ge(side_full["R"], filled(f"scores{h}", "R"))
                dve.tensor_reduce(peak[:, :], side[:, 2, :].rearrange("p (a s) -> p a s", a=2), AX_X,
                                  ALU.max).then_inc(peak_done, 1)
                dve.wait_ge(peak_done, h + 1)
                dve.tensor_scalar(shift[:, :], peak[:, :], -SM_SCALE, None, ALU.mult).then_inc(shift_done, 1)

            def softmax_norm(h):
                dve.wait_ge(side_free["R"], emptied(f"scores{h}", "R"))
                dve.reciprocal(inv_total[:, :], total[:, :]).then_inc(inv_total_done, 1)
                dve.wait_ge(inv_total_done, h + 1)
                for t in range(2):
                    op = dve.tensor_scalar(prob[:, t, :], prob[:, t, :], inv_total[:, t:t + 1], None, ALU.mult)
                op.then_inc(prob_ready, 1)

            def split_head(h):
                dve.wait_ge(o_hi_done, h + 1)
                dve.tensor_tensor(b_lo[:, 4 * h:4 * h + 4, :], pair("L").rearrange("p a (t s) -> p (a t) s", t=2),
                                  b_hi[:, 4 * h:4 * h + 4, :].bitcast(F32), ALU.subtract).then_inc(side_free["L"], 1)

            magic = 1.5 * 2.0 ** 23
            two_pi_hi = 6.28125
            two_pi_lo = 2 * np.pi - two_pi_hi
            for layer in range(3):
                dve.wait_ge(side_full["R"], filled(f"mlp{layer}", "R"))
                if layer == 0:
                    dve.wait_ge(side_free["L"], emptied("params", "L"))
                else:
                    dve.wait_ge(sin_done, layer)
                b = COL["mlp_b"] + layer
                dve.tensor_scalar(angle[:, :], side[0:MLP, 2, 0:S], par[0:MLP, b:b + 1],
                                  par[0:MLP, COL["freq"]:COL["freq"] + 1], ALU.add, ALU.mult).then_inc(side_free["R"], 1)
                dve.wait_ge(side_free["R"], emptied(f"mlp{layer}", "R"))
                dve.tensor_scalar(turns[:, :], angle[:, :], 1.0 / (2 * np.pi), magic, ALU.mult, ALU.add).then_inc(angle_step, 1)
                dve.wait_ge(angle_step, 5 * layer + 1)
                dve.tensor_scalar(turns[:, :], turns[:, :], -magic, None, ALU.add).then_inc(angle_step, 1)
                dve.wait_ge(angle_step, 5 * layer + 2)
                dve.scalar_tensor_tensor(out=angle[:, :], in0=turns[:, :], scalar=-two_pi_hi, in1=angle[:, :],
                                         op0=ALU.mult, op1=ALU.add).then_inc(angle_step, 1)
                dve.wait_ge(angle_step, 5 * layer + 3)
                dve.scalar_tensor_tensor(out=angle[:, :], in0=turns[:, :], scalar=-two_pi_lo, in1=angle[:, :],
                                         op0=ALU.mult, op1=ALU.add).then_inc(angle_step, 1)
                dve.wait_ge(angle_step, 5 * layer + 4)
                dve.tensor_scalar(angle[:, :], angle[:, :], PI_BELOW, -PI_BELOW, ALU.min, ALU.max).then_inc(angle_step, 1)
            split(0, 0)
            rms_inverse(0)
            norm_split(0)
            for s in range(SLOTS):
                if s + 1 < SLOTS:
                    split(s + 1, 0 if s < 4 else 3 if s % 7 == 0 else 2)
                else:
                    for j in range(4):
                        p = FFN_PIECE0 + j
                        dve.wait_ge(hi_done, p + 1)
                        dve.tensor_tensor(w_lo[:, j, :], raw[:, j, :], w_hi[:, j, :].bitcast(F32),
                                          ALU.subtract).then_inc(lo_done, 1)
                if s < 12:
                    (filter_window, filter_fold, filter_finish)[s % 3](s // 3)
                if s in (3, 7):
                    i = s // 4
                    panel = 2 * i + 1
                    for b in range(2):
                        dve.wait_ge(stream_free[b], i + 1)
                        wait_bank(dve, panel, b)
                        dve.tensor_tensor(u[:, 4 * i + 2 * b:4 * i + 2 * b + 2, :], stream_bank(2 + b),
                                          sigm[:, 2 * b:2 * b + 2, :], ALU.mult).then_inc(stream_free[2 + b], 1)
                if s in (9, 11, 13, 15, 17, 19):
                    short_sides((s - 9) // 2)
                if s == 19:
                    rms_inverse(1)
                    norm_split(1)
                if s in (19, 22, 25, 28):
                    multiply((s - 19) // 3)
                if s in (21, 24, 27, 30):
                    gate_by((s - 21) // 3)
                if s == 32:
                    dve.wait_ge(side_full["R"], filled("mean", "R"))
                    mean4 = side[:, 2:3, 0:S].to_broadcast([P, 4, S])
                    dve.wait_ge(conf_taps, 8 * (TAPS - 1))
                    for i in range(2):
                        c = conf[:, 4 * i:4 * i + 4, :]
                        op = dve.scalar_tensor_tensor(out=c, in0=mean4, scalar=-1.0 / CONF, in1=c,
                                                      op0=ALU.mult, op1=ALU.add)
                    op.then_inc(side_free["R"], 1)
                if s == 33:
                    dve.wait_ge(side_free["R"], emptied("variance", "R"))
                    dve.reciprocal(inv_rms[:, :], root[:, :]).then_inc(ln_step, 1)
                    dve.wait_ge(ln_step, 1)
                    inv4 = inv_rms[:, :].rearrange("p (a s) -> p a s", a=1).to_broadcast([P, 4, S])
                    for i in range(2):
                        c = conf[:, 4 * i:4 * i + 4, :]
                        dve.tensor_tensor(c, c, inv4, ALU.mult).then_inc(ln_step, 1)
                if s == 35:
                    for g in range(4):
                        source = conf[:, 4 * g:4 * g + 4, :] if g < 2 else x2[:, 4 * g - 8:4 * g - 4, :]
                        split_lo(2, g, source)
                if s in (37, 39, 41, 43, 53, 55, 57, 59):
                    i = (s - 37) // 2 % 4
                    if s == 37:
                        dve.wait_ge(x_again_landed, 16)
                    add_panel(s // 2, i)
                    if i == 3:
                        n = 2 if s < 44 else 3
                        rms_inverse(n)
                        norm_split(n)
                if s in (48, 50):
                    split_head((s - 48) // 2)
                if s in (46, 48, 50):
                    softmax_shift((s - 46) // 2)
                    softmax_norm((s - 46) // 2)
                if s == 51:
                    softmax_shift(3)
                    softmax_norm(3)
                    split_head(2)
                if s == 52:
                    split_head(3)
            with dve.Fori(0, SLABS) as i:
                dve.wait_ge(stream_free[1], i + PANELS // 2)
                dve.tensor_copy(ffn_par[:, :], par[:, bass.ds(i * 16 + COL["ffn"], 16)]).then_inc(ffn_par_ready, 1)
                for j in range(4, 20):
                    dve.wait_ge(hi_done, i * 16 + (FFN_PIECE0 + j + 1))
                    dve.tensor_tensor(w_lo[:, j % RING, :], raw[:, j % RING, :],
                                      w_hi[:, j % RING, :].bitcast(F32), ALU.subtract).then_inc(lo_done, 1)
                    if j == 11:
                        dve.wait_ge(ffn_par_ready, i + 1)
                        for b in range(2):
                            dve.wait_ge(gate_center, i * 4 + (2 * b + 2))
                            for side_ in range(2):
                                for t in range(2):
                                    c = 8 * side_ + 2 * b + t
                                    o, i_ = ((1, S), (0, S - 1)) if side_ == 0 else ((0, S - 1), (1, S))
                                    if side_:
                                        dve.wait_ge(gate_left, i * 4 + (2 * b + t + 1))
                                    op = dve.scalar_tensor_tensor(
                                        out=gate[:, 2 * b + t, o[0]:o[1]], in0=stream[:, b, t, i_[0]:i_[1]],
                                        scalar=ffn_par[:, c:c + 1], in1=gate[:, 2 * b + t, o[0]:o[1]],
                                        op0=ALU.mult, op1=ALU.add)
                                    if side_ == 0:
                                        op.then_inc(gate_left, 1)
                                    elif t:
                                        op.then_inc(stream_free[b], 1)
                dve.wait_ge(silu_done, i + 1)
                dve.wait_ge(lo_done, i * 16 + (FFN_PIECE0 + 20))
                for b in range(2):
                    if b == 0:
                        dve.wait_ge(stream_full[2], i + (PANELS // 2 + 1))
                    else:
                        dve.wait_ge(piece_used, i * 16 + (FFN_PIECE0 + 16))
                    dve.tensor_tensor(hv[:, 2 * b:2 * b + 2, :], stream_bank(2 + b),
                                      silu[:, 2 * b:2 * b + 2, :], ALU.mult).then_inc(stream_free[2 + b], 1)
                dve.wait_ge(h_hi_done, i + 1)
                dve.tensor_tensor(h_lo[:, bass.ds(i * 4, 4), :], hv[:, :, :],
                                  h_hi[:, bass.ds(i * 4, 4), :].bitcast(F32), ALU.subtract).then_inc(h_ready, 1)
            def split_down(g, first, last):
                for j in range(first, last):
                    dve.wait_ge(hi_done, g * 8 + (DOWN_PIECE0 + j + 1))
                    dve.tensor_tensor(w_lo[:, j % RING, :], raw[:, j % RING, :],
                                      w_hi[:, j % RING, :].bitcast(F32), ALU.subtract).then_inc(lo_done, 1)

            with dve.Fori(0, SLABS - 1) as g:
                split_down(g, 4, 12)
            split_down(SLABS - 1, 4, 8)
            for panel in range(4):
                for b in range(2):
                    if b == 0:
                        dve.wait_ge(down_full, panel + 1)
                    else:
                        dve.wait_ge(piece_used, DOWN_PIECE0 + 8 * (SLABS - 1) + 2 * panel + 2)
                    if panel < 2:
                        tiles = side[:, 2 * panel + b, :].rearrange("p (a s) -> p a s", a=2)
                    else:
                        tiles = stream_bank(2 * (panel - 2) + b)
                    rows = x[:, 4 * panel + 2 * b:4 * panel + 2 * b + 2, :]
                    dve.tensor_tensor(rows, tiles, rows, ALU.add).then_inc(down_added, 1)
            rms_inverse(4)
            for g in range(4):
                for j in range(4):
                    c = COL["g_final"] + 4 * g + j
                    op = dve.scalar_tensor_tensor(out=y_out[:, 4 * g + j, :], in0=x[:, 4 * g + j, :],
                                                  scalar=par[:, c:c + 1], in1=inv_rms[:, :],
                                                  op0=ALU.mult, op1=ALU.mult)
                op.then_inc(scaled_done, 1)


PI_BELOW = float(np.nextafter(np.float32(np.pi), np.float32(0)))


def transform_tables():
    n = 2 * S
    t = np.arange(S)[:, None]
    f = np.arange(S)[None, :]
    turn = 2 * np.pi * ((t * f) % n) / n
    re, im = np.cos(turn), -np.sin(turn)
    nyquist = np.where(t % 2 == 0, 1.0, -1.0)
    im_nyq, re_nyq = im.copy(), re.copy()
    im_nyq[:, 0:1] = nyquist
    re_nyq[:, 0:1] = nyquist
    forward = np.concatenate([re[:, :P], re[:, P:], im_nyq[:, :P], im[:, P:], im[:, :P], re_nyq[:, :P]], axis=1)
    back_re, back_im = 2 * re.T / n, 2 * im.T / n
    back_re[0] = 1.0 / n
    back_im[0] = nyquist[:, 0] / n
    back = np.concatenate([back_re, back_im], axis=0)
    tile = lambda a: np.ascontiguousarray(a.reshape(-1, P, a.shape[1]).transpose(1, 0, 2)).astype(np.float32)
    return tile(forward), tile(back)


def filter_tables():
    f32 = np.float32
    t = np.linspace(0.0, 1.0, S, dtype=f32)
    w = (f32(2.0 * np.pi) * np.arange(S, dtype=f32)) / f32(S)
    bands = (FEATURES - 1) // 2
    f = np.linspace(1e-4, bands - 1, bands, dtype=f32)
    angle = (f[None, :] * w[:, None]).astype(f32).astype(np.float64)
    features = np.concatenate([t[:, None], np.cos(angle), -np.sin(angle)], axis=1).astype(f32).T
    deltas = np.abs(np.linspace(np.log(1e-2) / 1.5, np.log(1e-2) / 0.3, HY, dtype=f32))
    fwd = np.exp((-t[:, None] * deltas[None, :]).astype(f32).astype(np.float64)).astype(f32)
    bwd = np.concatenate([np.zeros((1, HY), f32), fwd[:-1]], axis=0)
    both = np.stack([fwd, bwd]).reshape(2, 2, P, 2, HALF)
    return np.ascontiguousarray(features), np.ascontiguousarray(both.transpose(3, 2, 0, 1, 4).reshape(2, P, 4, HALF))


def kernel(x, mem, g_mix, w_in, conf_dw_w, conf_dw_b, conf_ln_g, conf_ln_b, hyena_short_w,
           hyena_short_b, hyena_w1, hyena_b1, hyena_w_inner, hyena_b_inner, hyena_w_filt,
           hyena_sin_freq, hyena_skip, w_out, g_xattn, g_mem, w_q, w_k, w_v, w_o, g_ffn, w_ffn_up,
           ffn_dw_w, ffn_dw_b, w_ffn_down, g_final):
    import concourse.bacc as bacc
    from concourse.bass_utils import run_bass_kernel_spmd

    def rows(a):
        return np.asarray(a).reshape(-1, P)

    def pad_row(a):
        a = np.asarray(a).reshape(-1, MLP)
        return np.concatenate([a, np.zeros((a.shape[0], P - MLP), a.dtype)], axis=1)

    def on_partitions(a):
        return np.ascontiguousarray(np.asarray(a)[0].T.reshape(KT, P, S).transpose(1, 0, 2))

    ffn = np.concatenate([np.asarray(ffn_dw_w)[0].reshape(3, SLABS, 4, P),
                          np.asarray(ffn_dw_b)[0].reshape(1, SLABS, 4, P)], axis=0).transpose(1, 0, 2, 3)
    packed = [rows(conf_dw_w), rows(conf_dw_b), rows(conf_ln_g), rows(conf_ln_b), rows(hyena_short_w),
              rows(hyena_short_b), rows(ffn), rows(g_mix), rows(g_mem), rows(g_xattn), rows(g_ffn),
              rows(g_final), pad_row(hyena_b1), pad_row(hyena_b_inner), pad_row(hyena_sin_freq)]
    packed.append(np.zeros((PARAM_TILES * P - PARAM_COLS, P), packed[0].dtype))
    params = np.ascontiguousarray(np.concatenate(packed, axis=0).reshape(PARAM_TILES, P, P).transpose(1, 0, 2))
    forward, back = transform_tables()
    features, decay = filter_tables()
    arrays = {
        "x_t": on_partitions(x), "mem_t": on_partitions(mem), "params": params,
        "w_in": w_in, "w1": hyena_w1, "w_inner": hyena_w_inner, "w_filt": hyena_w_filt,
        "skip": hyena_skip, "w_out": w_out, "w_q": w_q, "w_k": w_k, "w_v": w_v, "w_o": w_o,
        "w_up": w_ffn_up, "w_down": w_ffn_down,
        "dft": forward, "idft": back, "decay": decay, "features": features,
    }
    for name in ("w_in", "w1", "w_inner", "w_filt", "skip", "w_out", "w_q", "w_k", "w_v", "w_o", "w_up", "w_down"):
        arrays[name] = np.ascontiguousarray(np.asarray(arrays[name])[0])
    nc = bacc.Bacc("TRN2", target_bir_lowering=False, num_devices=1)
    args = [nc.dram_tensor(n, a.shape, mybir.dt.from_np(a.dtype), kind="ExternalInput").ap()
            for n, a in arrays.items()]
    out = nc.dram_tensor("out", (P, KT, S), F32, kind="ExternalOutput").ap()
    block_program(nc, *args, out)
    result = run_bass_kernel_spmd(nc, [arrays], core_ids=[0]).results[0]["out"]
    return np.ascontiguousarray(np.asarray(result).transpose(1, 0, 2).reshape(D, S).T)[None]
```

```python
from contextlib import ExitStack

import concourse.bass as bass
import numpy as np
from concourse import mybir

F32 = mybir.dt.float32
F32R = mybir.dt.float32r
ALU = mybir.AluOpType
ACT = mybir.ActivationFunctionType
AX_X = mybir.AxisListType.X

P = 128
S = 256
D = 2048
KT = D // P
HALF = 512
CONF = 1024
HY = 1024
TAPS = 31
HEADS = 4
FF = 5632
SLABS = FF // 512
RING = 4
MLP = 64
FEATURES = 33
EPS = 1e-6
SM_SCALE = float(D // HEADS) ** -0.5
PANELS = 30
SLOTS = 2 * PANELS

CONF_PANELS = [("gate", 0), ("value", 0), ("gate", 1), ("value", 1)]
HYENA_PANELS = [(0, 0), (1, 0), (0, 1), (1, 1), (2, 0), (2, 1)]
K0, V0, OUT0, Q0, O0 = 10, 14, 18, 22, 26

COL = {}
_at = 0
for _name, _n in (("conf_w", TAPS * 8), ("conf_b", 8), ("ln_g", 8), ("ln_b", 8),
                  ("short_w", 3 * 24), ("short_b", 24), ("ffn", SLABS * 16),
                  ("g_mix", KT), ("g_mem", KT), ("g_xattn", KT), ("g_ffn", KT), ("g_final", KT),
                  ("mlp_b", 3), ("freq", 1)):
    COL[_name] = _at
    _at += _n
PARAM_COLS = _at

SIDE = [("mlp0", "R"), ("mlp1", "R"), ("mlp2", "R"), ("stats0", "L"),
        ("taps0", "LR"), ("energy0", "L"), ("spec0", "LR"), ("spec_im0", "L"),
        ("taps1", "LR"), ("energy1", "L"), ("spec1", "LR"), ("spec_im1", "L"),
        ("taps2", "LR"), ("energy2", "L"), ("spec2", "LR"), ("spec_im2", "L"),
        ("taps3", "LR"), ("energy3", "L"), ("turn0", "L"), ("spec3", "LR"), ("spec_im3", "L"),
        ("turn1", "L"), ("turn2", "L"), ("turn3", "L"), ("stats1", "R"),
        ("dft0", "LR"), ("idft0", "L"), ("dft1", "LR"), ("idft1", "L"),
        ("dft2", "LR"), ("idft2", "L"), ("dft3", "LR"), ("idft3", "L"),
        ("mean", "R"), ("variance", "R"), ("stats2", "R"),
        ("scores0", "R"), ("turn_p0", "L"), ("scores1", "R"), ("pv0", "L"), ("turn_p1", "L"),
        ("scores2", "R"), ("pv1", "L"), ("turn_p2", "L"), ("scores3", "R"), ("pv2", "L"),
        ("turn_p3", "L"), ("pv3", "L"), ("stats3", "R")]


def side_counts():
    full, free, need = {"L": 0, "R": 0}, {"L": 0, "R": 0}, {}
    for name, pairs in SIDE:
        for b in pairs:
            before = free[b]
            free[b] += 1
            full[b] += 1
            need[name, b] = (before, full[b], free[b])
    return need, free


SIDE_AT, SIDE_FREE_END = side_counts()


def before(name, b):
    return SIDE_AT[name, b][0]


def filled(name, b):
    return SIDE_AT[name, b][1]


def emptied(name, b):
    return SIDE_AT[name, b][2]


def block_program(nc, x_t, mem_t, params, w_in, w1, w_inner, w_filt, skip, w_out, w_q, w_k, w_v,
                  w_o, w_up, w_down, dft, idft, decay, features, out):
    KB = 1024
    base = 16512

    def at(name, kb, shape, dt=F32):
        return nc.alloc_sbuf_tensor_at(name, shape, dt, offset=base + int(kb * KB))

    with ExitStack() as ctx:
        def sem(name):
            return ctx.enter_context(nc.semaphore(name))

        raw = at("raw", 0, [P, RING, 1024])
        w_hi = at("w_hi", 16, [P, RING, 1024], F32R)
        w_lo = at("w_lo", 32, [P, RING, 1024], F32R)
        par = at("par", 48, [P, PARAM_COLS])
        eps, peak, shift, total, inv_total = (
            at(name, 50.5 + i / 32, [P, n])
            for i, (name, n) in enumerate((("eps", 1), ("peak", 2), ("shift", 2), ("total", 2), ("inv_total", 2))))
        ident = at("ident", 51, [P, P])
        ones = at("ones", 51.5, [P, P])
        root = at("root", 52, [P, S])
        inv_rms = at("inv_rms", 53, [P, S])
        a_hi = at("a_hi", 54, [P, KT, S], F32R)
        a_lo = at("a_lo", 70, [P, KT, S], F32R)
        x_first = at("x_first", 86, [P, KT, S])
        taps = at("taps", 86, [P, 4, HALF])
        folded = at("folded", 94, [P, 4, HALF])
        mem_x = at("mem_x", 86, [P, KT, S])
        keys = at("keys", 86, [P, KT, S])
        spec = [at("spec_first", 102, [P, 2, 5, HALF]), at("spec_second", 122, [P, 2, 5, HALF])]
        values = at("values", 102, [P, 2, D])
        dft_sb = at("dft_sb", 142, [P, 2, 768])
        idft_sb = at("idft_sb", 148, [P, 4, S])
        u = at("u", 152, [P, 8, S])
        conf = at("conf", 160, [P, 8, S])
        v_t = at("v_t", 168, [P, 2, 2, HALF])
        x1_t = at("x1_t", 176, [P, 2, 2, HALF])
        x2 = at("x2", 184, [P, 8, S])
        decay_sb = at("decay_sb", 184, [P, 4, HALF])
        spectrum = at("spectrum", 192, [P, 4, HALF])
        sigm = at("sigm", 192, [P, 4, S])
        skip_sb = at("skip_sb", 196, [P, HALF])
        k_norm = at("k_norm", 198, [P, HALF])
        w_filt_sb = at("w_filt_sb", 200, [MLP, 2, HALF])
        cross = at("cross", 200, [P, 2, HALF])
        turned = at("turned", 200, [P, 4, S])
        proj = at("proj", 192, [P, 4, S])
        squares_x = at("squares_x", 168, [P, 4, 4, S])
        sum_x = at("sum_x", 206.5, [P, S])
        squares_m = at("squares_m", 196, [P, 1, 4, S])
        sum_m = at("sum_m", 204, [P, S])
        inv_mem = at("inv_mem", 205, [P, S])
        feat = at("feat", 102, [FEATURES, S])
        w1_sb = at("w1_sb", 103, [FEATURES, MLP])
        w_inner_sb = at("w_inner_sb", 103.5, [MLP, 2, MLP])
        angle = at("angle", 104, [MLP, S])
        turns = at("turns", 105, [MLP, S])
        hidden = at("hidden", 204, [MLP, 2, S + 1])
        x = at("x", 191.75, [P, KT, S])
        squares = at("squares", 186, [P, 1, 4, S])
        sum_sq = at("sum_sq", 190.5, [P, S])
        b_hi = at("b_hi", 142, [P, KT, S], F32R)
        b_lo = at("b_lo", 158, [P, KT, S], F32R)
        q = at("q", 174, [P, 2, 4, S])
        prob = at("prob", 182, [P, 2, S])
        prob_t = at("prob_t", 184, [P, 2, S])
        h_hi = at("h_hi", 86, [P, SLABS * 4, S], F32R)
        h_lo = at("h_lo", 130, [P, SLABS * 4, S], F32R)
        gate = at("gate", 174, [P, 4, S])
        silu = at("silu", 178, [P, 4, S])
        hv = at("hv", 182, [P, 4, S])
        gate_in = at("gate_in", 186, [P, 4, S])
        ffn_par = at("ffn_par", 190, [P, 16])
        y_out = at("y_out", 86, [P, KT, S])

        stream = ctx.enter_context(nc.psum_tensor("stream", [P, 4, 2, S], F32))
        side = ctx.enter_context(nc.psum_tensor("side", [P, 4, 512], F32))

        def stream_bank(b):
            return stream[:, b, :, :]

        raw_landed = [sem(f"raw_landed{i}") for i in range(RING)]
        hi_done, lo_done, piece_used = sem("hi_done"), sem("lo_done"), sem("piece_used")
        stream_full = [sem(f"stream_full{b}") for b in range(4)]
        stream_free = [sem(f"stream_free{b}") for b in range(4)]
        side_full = {b: sem(f"side_full_{b}") for b in "LR"}
        side_free = {b: sem(f"side_free_{b}") for b in "LR"}
        params_landed, mlp_landed, w_inner_landed = sem("params_landed"), sem("mlp_landed"), sem("w_inner_landed")
        x_landed = [sem(f"x_landed{g}") for g in range(4)]
        dft_landed, decay_landed = sem("dft_landed"), sem("decay_landed")
        w_filt_landed, skip_landed = sem("w_filt_landed"), sem("skip_landed")
        mem_landed, x_again_landed = sem("mem_landed"), sem("x_again_landed")
        out_written = sem("out_written")
        zeroed, ident_made, made = sem("zeroed"), sem("ident_made"), sem("made")
        angle_step, sin_done = sem("angle_step"), sem("sin_done")
        squared, fold_step, folded_in = sem("squared"), sem("fold_step"), sem("folded_in")
        rms_ready, mem_scaled = sem("rms_ready"), sem("mem_scaled")
        a_hi_done, a_ready = sem("a_hi_done"), sem("a_ready")
        k_squared, k_summed, k_norm_ready = sem("k_squared"), sem("k_summed"), sem("k_norm_ready")
        k_folded, spec_done = sem("k_folded"), sem("spec_done")
        short_center, short_left, short_done = sem("short_center"), sem("short_left"), sem("short_done")
        product_step, product_done = sem("product_step"), sem("product_done")
        sigmoid_done, glu_gate_ready = sem("sigmoid_done"), sem("glu_gate_ready")
        mean_summed, squares_summed = sem("mean_summed"), sem("squares_summed")
        conf_center, conf_taps = sem("conf_center"), sem("conf_taps")
        conf_squared, ln_step, conf_done = sem("conf_squared"), sem("ln_step"), sem("conf_done")
        peak_done, shift_done = sem("peak_done"), sem("shift_done")
        inv_total_done, prob_ready, o_hi_done = sem("inv_total_done"), sem("prob_ready"), sem("o_hi_done")
        ffn_par_ready, gate_center, gate_left = sem("ffn_par_ready"), sem("gate_center"), sem("gate_left")
        gate_done, silu_done, silu_scaled = sem("gate_done"), sem("silu_done"), sem("silu_scaled")
        h_hi_done, h_ready = sem("h_hi_done"), sem("h_ready")
        down_full, down_added = sem("down_full"), sem("down_added")
        final_squares_used, y_gained, last_gained, y_done, y_done_pool = (
            sem("final_squares_used"), sem("y_gained"), sem("last_gained"), sem("y_done"), sem("y_done_pool"))

        block = ctx.enter_context(nc.Block())

        def norm_phase(n):
            return [(x_first, "g_mix", squares_x, 4, sum_x, "L", inv_rms),
                    (mem_x, "g_mem", squares_m, 1, sum_m, "R", inv_mem),
                    (x, "g_xattn", squares, 1, sum_sq, "R", inv_rms),
                    (x, "g_ffn", squares, 1, sum_sq, "R", inv_rms),
                    (x, "g_final", squares, 1, sum_sq, "L", inv_rms)][n]

        def per_tile(vector, n):
            return vector[:, :].rearrange("p (a s) -> p a s", a=1).to_broadcast([P, n, S])

        def pair(b):
            return side[:, 0:2, :] if b == "L" else side[:, 2:4, :]

        A_PHASE = [0, 1, 3, 4]
        A_NEXT = [0, K0, OUT0, Q0, O0]

        def group_free(m, g):
            return 8 * A_NEXT[m] - 8 + 2 * g + 2

        FFN_PIECE0 = 8 * PANELS
        DOWN_PIECE0 = FFN_PIECE0 + 16 * SLABS

        @block.sync
        def _(sp):
            def panel_source(panel):
                if panel < 4:
                    kind, i = CONF_PANELS[panel]
                    return w_in, (CONF if kind == "gate" else 0) + i * HALF
                if panel < K0:
                    part, half = HYENA_PANELS[panel - 4]
                    return w_in, 2 * CONF + part * HY + half * HALF
                for w, first in ((w_k, K0), (w_v, V0), (w_out, OUT0), (w_q, Q0), (w_o, O0)):
                    if first <= panel < first + 4:
                        return w, (panel - first) * HALF

            def rows(w, r0, c0):
                return w[bass.ds(r0, 256), bass.ds(c0, HALF)].rearrange("(k p) n -> p k n", p=P)

            def load_piece(p, source):
                slot = p % RING
                sp.dma_start(raw[:, slot, :].rearrange("p (k n) -> p k n", k=2),
                             source).then_inc(raw_landed[slot], 16)

            sp.dma_start(feat[:, :], features).then_inc(mlp_landed, 16)
            sp.dma_start(w1_sb[:, :], w1).then_inc(mlp_landed, 16)
            sp.dma_start(par[:, :], params).then_inc(params_landed, 16)
            for s in range(SLOTS):
                f = (s - 1) // 3
                if s and (s - 1) % 3 == 0 and f < 4:
                    if f:
                        sp.wait_ge(side_full["R"], filled(f"taps{f - 1}", "R"))
                    half, order = f // 2, f % 2
                    w = w_filt.rearrange("k (o d c) -> k o d c", o=2, d=2)
                    sp.dma_start(w_filt_sb[:, :, :], w[:, order, :, half * HALF:(half + 1) * HALF]).then_inc(w_filt_landed, 16)
                if s in (1, 7):
                    if s == 7:
                        sp.wait_ge(side_free["R"], emptied("taps1", "R"))
                    sp.dma_start(decay_sb[:, :, :], decay[s // 7]).then_inc(decay_landed, 16)
                if s and (s - 1) % 3 == 2 and f < 4:
                    if f:
                        sp.wait_ge(spec_done, f)
                    half, order = f // 2, f % 2
                    sp.dma_start(skip_sb[:, :], skip[order:order + 1, half * HALF:(half + 1) * HALF]
                                 .to_broadcast([P, HALF])).then_inc(skip_landed, 16)
                if s == 2:
                    sp.dma_start(dft_sb[:, :, :], dft).then_inc(dft_landed, 16)
                    sp.dma_start(idft_sb[:, :, :], idft).then_inc(dft_landed, 16)
                if s == 15:
                    sp.wait_ge(side_full["L"], filled("spec_im3", "L"))
                    sp.dma_start(mem_x[:, :, :], mem_t).then_inc(mem_landed, 16)
                if s == 38:
                    sp.wait_ge(a_ready, 12)
                    sp.dma_start(x[:, :, :], x_t).then_inc(x_again_landed, 16)
                for p in range(4 * s, 4 * s + 4):
                    if s == 0:
                        sp.dma_start(x_first[:, 4 * p:4 * p + 4, :], x_t[:, 4 * p:4 * p + 4, :]).then_inc(x_landed[p], 16)
                    if p >= RING:
                        sp.wait_ge(lo_done, p - RING + 1)
                    w, c0 = panel_source(p // 8)
                    load_piece(p, rows(w, (p % 8) * 256, c0))
                    if p == 0:
                        sp.dma_start(w_inner_sb[:, :, :], w_inner.rearrange("l k n -> k l n")).then_inc(w_inner_landed, 16)
            with sp.Fori(0, SLABS) as i:
                for j in range(16):
                    sp.wait_ge(lo_done, i * 16 + (FFN_PIECE0 + j - RING + 1))
                    load_piece(j, rows(w_up, (j % 8) * 256, i * HALF + (j // 8) * FF))
            with sp.Fori(0, SLABS) as g:
                for j in range(8):
                    sp.wait_ge(lo_done, g * 8 + (DOWN_PIECE0 + j - RING + 1))
                    load_piece(j, rows(w_down, g * 512 + (j % 2) * 256, (j // 2) * HALF))
            for g in (1, 2, 3, 0):
                if g == 0:
                    sp.wait_ge(y_done_pool, 1)
                else:
                    sp.wait_ge(y_done, g)
                sp.dma_start(out[:, 4 * g:4 * g + 4, :], y_out[:, 4 * g:4 * g + 4, :]).then_inc(out_written, 16)
            sp.wait_ge(out_written, 64)

        @block.gpsimd
        def _(pool):
            pool.memset(ident[:, :], 0.0).then_inc(zeroed, 1)
            pool.memset(ones[:, :], 1.0).then_inc(made, 1)
            pool.memset(eps[:, :], EPS).then_inc(made, 1)
            pool.memset(hidden[:, :, 0:1], 0.0).then_inc(made, 1)
            pool.wait_ge(zeroed, 1)
            pool.affine_select(out=ident[:, :], in_=ident[:, :], compare_op=ALU.not_equal, fill=1.0,
                               base=0, pattern=[[-1, P]], channel_multiplier=1).then_inc(ident_made, 1)
            steps = iter(range(1, 10 ** 6))

            def add(to, a, b, done=None):
                op = pool.tensor_tensor(to, a, b, ALU.add)
                if done is None:
                    op.then_inc(fold_step, 1)
                    pool.wait_ge(fold_step, next(steps))
                else:
                    op.then_inc(done, 1)

            def fold_squares(n, g):
                bufs, count, total_sq = norm_phase(n)[2], norm_phase(n)[3], norm_phase(n)[4]
                sq = bufs[:, g % count, :, :]
                pool.wait_ge(squared, 4 * n + g + 1)
                if g == 0 and n >= 3:
                    pool.wait_ge(side_full["R"], filled(f"stats{n - 1}", "R"))
                add(sq[:, 0:2, :], sq[:, 0:2, :], sq[:, 2:4, :])
                if g == 0:
                    add(total_sq[:, :], sq[:, 0, :], sq[:, 1, :], folded_in)
                else:
                    add(sq[:, 0, :], sq[:, 0, :], sq[:, 1, :])
                    pool.wait_ge(folded_in, 4 * n + g)
                    add(total_sq[:, :], total_sq[:, :], sq[:, 0, :], folded_in)

            def sum_filter(f):
                pool.wait_ge(k_squared, f + 1)
                add(folded[:, 0:2, :], folded[:, 0:2, :], folded[:, 2:4, :])
                add(folded[:, 0, :], folded[:, 0, :], folded[:, 1, :], k_summed)

            def scale_sigmoid(i):
                pool.wait_ge(sigmoid_done, i + 1)
                pool.tensor_tensor(sigm[:, :, :], sigm[:, :, :], per_tile(inv_rms, 4), ALU.mult).then_inc(glu_gate_ready, 1)

            def sum_channels(source, done):
                add(u[:, 0:4, :], source[:, 0:4, :], source[:, 4:8, :])
                add(u[:, 0:2, :], u[:, 0:2, :], u[:, 2:4, :])
                add(u[:, 0, :], u[:, 0, :], u[:, 1, :], done)

            for g in range(4):
                fold_squares(0, g)
            sum_filter(0)
            scale_sigmoid(0)
            sum_filter(1)
            scale_sigmoid(1)
            sum_filter(2)
            sum_filter(3)
            for g in range(4):
                fold_squares(1, g)
            pool.wait_ge(conf_taps, 8 * (TAPS - 1))
            sum_channels(conf, mean_summed)
            pool.wait_ge(conf_squared, 1)
            sum_channels(u, squares_summed)
            for n in (2, 3):
                for g in range(4):
                    fold_squares(n, g)
            with pool.Fori(0, SLABS) as i:
                pool.wait_ge(silu_done, i + 1)
                pool.tensor_tensor(silu[:, :, :], silu[:, :, :], per_tile(inv_rms, 4), ALU.mult).then_inc(silu_scaled, 1)
            for g in range(3):
                fold_squares(4, g)
            pool.wait_ge(y_gained, 4)
            pool.wait_ge(rms_ready, 5)
            pool.tensor_tensor(y_out[:, 0:4, :], y_out[:, 0:4, :], per_tile(inv_rms, 4), ALU.mult).then_inc(y_done_pool, 1)

        @block.tensor
        def _(pe):
            def products(out_, wh, wl, ah, al, start, stop, shared):
                pe.matmul(out_, wh, ah, start=start, stop=False, skip_group_check=shared)
                pe.matmul(out_, wh, al, start=False, stop=False, skip_group_check=shared)
                return pe.matmul(out_, wl, ah, start=False, stop=stop, skip_group_check=shared)

            def half_panel(s):
                panel, first = s // 2, (s % 2) * 4
                banks = (panel % 2) * 2
                act_hi, act_lo = (b_hi, b_lo) if panel >= O0 else (a_hi, a_lo)
                if s % 2 == 0 and panel >= 2:
                    for b in (banks, banks + 1):
                        pe.wait_ge(stream_free[b], panel // 2)
                for j in range(first, first + 4):
                    phase = A_NEXT.index(panel) if panel in (0, K0, OUT0, Q0) else None
                    if phase is not None and j % 2 == 0:
                        pe.wait_ge(a_ready, 4 * phase + j // 2 + 1)
                    if panel == O0 and j % 2 == 0:
                        pe.wait_ge(side_free["L"], emptied(f"pv{j // 2}", "L"))
                    p = 8 * panel + j
                    pe.wait_ge(lo_done, p + 1)
                    piece(banks, p % RING, j, V0 <= panel < OUT0, act_hi, act_lo, 2 * j,
                          j == 0, j == 7)
                    if (panel, j) == (O0, 5):
                        attend(3)
                    if (panel, j) == (0, 1):
                        mlp_layer(1)
                    if (panel, j) == (0, 5):
                        statistics(0)

            def piece(banks, slot, j, swapped, act_hi, act_lo, kt, first, last):
                if swapped:
                    for m in range(2):
                        for k in range(2):
                            a = bass.ts(m, P)
                            w = bass.ts(k, HALF)
                            mm = products(stream_bank(banks + m).rearrange("p a b -> p (a b)"),
                                          act_hi[:, kt + k, a], act_lo[:, kt + k, a],
                                          w_hi[:, slot, w], w_lo[:, slot, w],
                                          first and k == 0, last and k == 1, False)
                        if last and m == 0:
                            mm.then_inc(stream_full[banks], 1)
                    mm.then_inc(piece_used, 1)
                    return
                for t in range(4):
                    for k in range(2):
                        w = bass.ds(k * HALF + t * P, P)
                        mm = products(stream[:, banks + t // 2, t % 2, :],
                                      w_hi[:, slot, w], w_lo[:, slot, w],
                                      act_hi[:, kt + k, :], act_lo[:, kt + k, :],
                                      first and t % 2 == 0 and k == 0, last and k == 1, True)
                    if last and t == 1:
                        mm.then_inc(stream_full[banks], 1)
                mm.then_inc(piece_used, 1)

            def claim(name, pairs):
                for b in pairs:
                    if before(name, b):
                        pe.wait_ge(side_free[b], before(name, b))

            def statistics(n):
                b = norm_phase(n)[5]
                claim(f"stats{n}", b)
                pe.wait_ge(folded_in, 4 * n + 4)
                pe.matmul(pair(b)[:, 0, 0:S], ones[:, :], norm_phase(n)[4][:, :],
                          start=True, stop=True).then_inc(side_full[b], 1)

            def mlp_layer(layer):
                claim(f"mlp{layer}", "R")
                if layer == 0:
                    pe.wait_ge(mlp_landed, 32)
                    w, h = w1_sb[:, :], feat[:, :]
                else:
                    pe.wait_ge(w_inner_landed, 16)
                    pe.wait_ge(sin_done, layer)
                    w, h = w_inner_sb[:, layer - 1, :], hidden[:, (layer - 1) % 2, 1:S + 1]
                pe.matmul(side[0:MLP, 2, 0:S], w, h, start=True, stop=True).then_inc(side_full["R"], 1)

            def filter_taps(f):
                claim(f"taps{f}", "LR")
                pe.wait_ge(w_filt_landed, 16 * (f + 1))
                if f == 0:
                    pe.wait_ge(sin_done, 3)
                    pe.wait_ge(made, 3)
                for d in range(2):
                    for t in range(2):
                        mm = pe.matmul(side[:, 2 * d + t, :], hidden[:, 0, bass.ds(1 - d + t * P, P)],
                                       w_filt_sb[:, d, :], start=True, stop=True)
                    mm.then_inc(side_full["LR"[d]], 1)

            def filter_energy(f):
                claim(f"energy{f}", "L")
                pe.wait_ge(k_summed, f + 1)
                pe.matmul(side[:, 0, :], ones[:, :], folded[:, 0, :], start=True, stop=True).then_inc(side_full["L"], 1)

            def spectrum_tile(bank, column, part):
                for k in range(2):
                    mm = pe.matmul(side[:, bank, :], dft_sb[:, k, bass.ts(column, P)],
                                   folded[:, 2 * part + k, :], start=(k == 0), stop=(k == 1))
                return mm

            def filter_spectrum(f):
                claim(f"spec{f}", "LR")
                if f == 0:
                    pe.wait_ge(dft_landed, 32)
                pe.wait_ge(k_folded, 2 * f + 1)
                spectrum_tile(0, 0, 0)
                spectrum_tile(1, 1, 0).then_inc(side_full["L"], 1)
                spectrum_tile(2, 5, 0)
                pe.wait_ge(k_folded, 2 * f + 2)
                spectrum_tile(3, 4, 1).then_inc(side_full["R"], 1)
                claim(f"spec_im{f}", "L")
                spectrum_tile(0, 3, 1).then_inc(side_full["L"], 1)

            def turn(e):
                claim(f"turn{e}", "L")
                pe.wait_ge(short_done, 2 * (e + 1))
                for t in range(2):
                    for c in range(4):
                        mm = pe.transpose(side[:, t, bass.ts(c, P)], turned[:, c, bass.ts(t, P)], ident[:, :])
                mm.then_inc(side_full["L"], 1)

            def transform(c):
                claim(f"dft{c}", "LR")
                order, half = c // 2, c % 2
                if order == 0:
                    pe.wait_ge(side_free["L"], emptied(f"turn{2 * half}", "L"))
                else:
                    pe.wait_ge(side_free["L"], emptied(f"idft{half}", "L"))
                source = (v_t, x1_t)[order]
                for j in range(4):
                    for k in range(2):
                        mm = pe.matmul(side[:, j, :], dft_sb[:, k, bass.ts(j, P)], source[:, half, k, :],
                                       start=(k == 0), stop=(k == 1))
                    if j % 2:
                        mm.then_inc(side_full["LR"[j // 2]], 1)

            def transform_back(c):
                claim(f"idft{c}", "L")
                pe.wait_ge(product_done, 2 * (c + 1))
                if c < 2:
                    for t in range(2):
                        for k in range(4):
                            mm = pe.matmul(side[:, t, :], idft_sb[:, k, bass.ts(t, P)], spectrum[:, k, :],
                                           start=(k == 0), stop=(k == 3))
                else:
                    for t in range(4):
                        for k in range(4):
                            mm = pe.matmul(side[:, t // 2, bass.ts(t % 2, S)], spectrum[:, k, bass.ts(t, P)],
                                           idft_sb[:, k, :], start=(k == 0), stop=(k == 3))
                mm.then_inc(side_full["L"], 1)

            def channel_sum(name, summed):
                claim(name, "R")
                pe.wait_ge(summed, 1)
                pe.matmul(side[:, 2, 0:S], ones[:, :], u[:, 0, :], start=True, stop=True).then_inc(side_full["R"], 1)

            def scores(h):
                claim(f"scores{h}", "R")
                for b in range(2):
                    bank = ((Q0 + h) % 2) * 2 + b
                    pe.wait_ge(stream_free[bank], (Q0 + h) // 2 + 1)
                for t in range(2):
                    for k in range(4):
                        mm = pe.matmul(side[:, 2, bass.ts(t, S)], q[:, h % 2, k, bass.ts(t, P)],
                                       keys[:, 4 * h + k, :], start=(k == 0), stop=(k == 3))
                mm.then_inc(side_full["R"], 1)

            def turn_probs(h):
                claim(f"turn_p{h}", "L")
                pe.wait_ge(prob_ready, h + 1)
                for m in range(2):
                    for t in range(2):
                        mm = pe.transpose(side[:, 0, bass.ds(m * S + t * P, P)], prob[:, t, bass.ts(m, P)], ident[:, :])
                mm.then_inc(side_full["L"], 1)

            def attend(h):
                claim(f"pv{h}", "L")
                for t in range(4):
                    for m in range(2):
                        mm = pe.matmul(side[:, t // 2, bass.ts(t % 2, S)],
                                       values[:, m, bass.ds(h * HALF + t * P, P)], prob_t[:, m, :],
                                       start=(m == 0), stop=(m == 1))
                mm.then_inc(side_full["L"], 1)

            mlp_layer(0)
            pe.wait_ge(made, 1)
            pe.wait_ge(ident_made, 1)
            for s in range(SLOTS):
                half_panel(s)
                if s == 0:
                    mlp_layer(2)
                if 1 <= s < 13:
                    (filter_taps, filter_energy, filter_spectrum)[(s - 1) % 3]((s - 1) // 3)
                if s in (11, 12, 14, 16):
                    turn((11, 12, 14, 16).index(s))
                if s == 17:
                    statistics(1)
                if s in (19, 22, 25, 28):
                    transform((s - 19) // 3)
                if s in (21, 24, 27, 30):
                    transform_back((s - 21) // 3)
                if s == 32:
                    channel_sum("mean", mean_summed)
                if s == 33:
                    channel_sum("variance", squares_summed)
                if s == 44:
                    statistics(2)
                if s in (48, 50):
                    attend(s // 2 - 24)
                if s in (46, 48, 50):
                    scores(s // 2 - 23)
                if s in (47, 49, 51):
                    turn_probs(s // 2 - 23)
                if s == 51:
                    scores(3)
                    attend(2)
                if s == 52:
                    turn_probs(3)

            def up_slab(i, first):
                for j in range(16):
                    if j % 8 == 0:
                        for b in (j // 4, j // 4 + 1):
                            pe.wait_ge(stream_free[b], i + PANELS // 2)
                    if first and j < 8 and j % 2 == 0:
                        pe.wait_ge(a_ready, 4 * 4 + j // 2 + 1)
                    pe.wait_ge(lo_done, i * 16 + (FFN_PIECE0 + j + 1))
                    piece((j // 8) * 2, j % RING, j % 8, False, a_hi, a_lo, 2 * (j % 8), j % 8 == 0, j % 8 == 7)
                    if first and j == 5:
                        statistics(3)

            up_slab(0, True)
            with pe.Fori(1, SLABS) as i:
                up_slab(i, False)

            def down_tile(panel, t):
                if panel < 2:
                    return side[:, 2 * panel + t // 2, bass.ts(t % 2, S)]
                return stream[:, 2 * (panel - 2) + t // 2, t % 2, :]

            def down_group(g, first, last):
                for j in range(8):
                    panel, half = j // 2, j % 2
                    if first and half == 0:
                        if panel < 2:
                            b = "LR"[panel]
                            pe.wait_ge(side_free[b], SIDE_FREE_END[b])
                        else:
                            for b in (2 * (panel - 2), 2 * (panel - 2) + 1):
                                pe.wait_ge(stream_free[b], PANELS // 2 + SLABS)
                    pe.wait_ge(lo_done, g * 8 + (DOWN_PIECE0 + j + 1))
                    for t in range(4):
                        for k in range(2):
                            w = bass.ds(k * HALF + t * P, P)
                            kt = g * 4 + (2 * half + k)
                            mm = products(down_tile(panel, t), w_hi[:, j % RING, w], w_lo[:, j % RING, w],
                                          h_hi[:, bass.ds(kt, 1), :].rearrange("p a b -> p (a b)"),
                                          h_lo[:, bass.ds(kt, 1), :].rearrange("p a b -> p (a b)"),
                                          first and half == 0 and t % 2 == 0 and k == 0,
                                          last and half == 1 and k == 1, True)
                        if last and half == 1 and t == 1:
                            mm.then_inc(down_full, 1)
                    mm.then_inc(piece_used, 1)

            pe.wait_ge(h_ready, SLABS - 1)
            down_group(0, True, False)
            with pe.Fori(1, SLABS - 1) as g:
                down_group(g, False, False)
            pe.wait_ge(h_ready, SLABS)
            down_group(SLABS - 1, False, True)
            pe.wait_ge(down_added, 2)
            pe.wait_ge(folded_in, 4 * 4 + 3)
            pe.matmul(side[:, 0, 0:S], ones[:, :], sum_sq[:, :], start=True, stop=False)
            for b in range(2):
                pe.wait_ge(squared, 4 * 4 + 4 + b)
                for j in (2 * b, 2 * b + 1):
                    mm = pe.matmul(side[:, 0, 0:S], ones[:, :], squares[:, 0, j, :], start=False, stop=(j == 3))
            mm.then_inc(final_squares_used, 1)

        def wait_bank(eng, panel, b):
            if b == 0:
                eng.wait_ge(stream_full[(panel % 2) * 2], panel // 2 + 1)
            else:
                eng.wait_ge(piece_used, 8 * panel + 8)

        @block.scalar
        def _(act):
            def split_piece(p):
                act.wait_ge(raw_landed[p % RING], 16 * (p // RING + 1))
                if p >= RING:
                    act.wait_ge(piece_used, p - RING + 1)
                act.activation(w_hi[:, p % RING, :], raw[:, p % RING, :], ACT.Copy).then_inc(hi_done, 1)

            def evacuate(panel, tiles):
                for b in range(2):
                    bank = (panel % 2) * 2 + b
                    wait_bank(act, panel, b)
                    act.activation(tiles(b), stream_bank(bank), ACT.Copy).then_inc(stream_free[bank], 1)

            def square(n, g):
                source, _, bufs, count, _, _, _ = norm_phase(n)
                if g >= count:
                    act.wait_ge(folded_in, 4 * n + g + 1 - count)
                act.activation(bufs[:, g % count, :, :], source[:, 4 * g:4 * g + 4, :], ACT.Square).then_inc(squared, 1)

            def rms_root(n):
                b = norm_phase(n)[5]
                act.wait_ge(side_full[b], filled(f"stats{n}", b))
                act.activation(root[:, :], pair(b)[:, 0, 0:S], ACT.Sqrt, bias=eps[:, 0:1],
                               scale=1.0 / D).then_inc(side_free[b], 1)

            def gain_hi(n, g):
                m = A_PHASE[n]
                if m:
                    act.wait_ge(piece_used, group_free(m, g))
                for j in range(4 * g, 4 * g + 4):
                    op = act.activation(a_hi[:, j, :], norm_phase(n)[0][:, j, :], ACT.Identity,
                                        scale=column(norm_phase(n)[1], j))
                op.then_inc(a_hi_done, 1)

            def mix_hi(g):
                act.wait_ge(piece_used, group_free(2, g))
                source = conf[:, 4 * g:4 * g + 4, :] if g < 2 else x2[:, 4 * g - 8:4 * g - 4, :]
                act.activation(a_hi[:, 4 * g:4 * g + 4, :], source, ACT.Copy).then_inc(a_hi_done, 1)

            def column(name, i):
                return par[:, COL[name] + i:COL[name] + i + 1]

            def short_centers(e):
                part, half = HYENA_PANELS[e]
                if 1 <= e < 4:
                    act.wait_ge(side_full["L"], filled(f"turn{e - 1}", "L"))
                for t in range(4):
                    if t % 2 == 0:
                        act.wait_ge(stream_free[((4 + e) % 2) * 2 + t // 2], (4 + e) // 2 + 1)
                    c = part * 8 + half * 4 + t
                    to = x2[:, 4 * half + t, :] if part == 2 else turned[:, t, :]
                    act.activation(to, proj[:, t, :], ACT.Identity,
                                   bias=column("short_b", c), scale=column("short_w", 24 + c)).then_inc(short_center, 1)

            def evacuate_turned(e):
                part, half = HYENA_PANELS[e]
                act.wait_ge(side_full["L"], filled(f"turn{e}", "L"))
                act.activation((v_t, x1_t)[part][:, half, :, :], pair("L"), ACT.Copy).then_inc(side_free["L"], 1)

            def filter_square(f):
                act.wait_ge(side_free["R"], emptied(f"taps{f}", "R"))
                if f:
                    act.wait_ge(side_full["L"], filled(f"spec_im{f - 1}", "L"))
                act.activation(folded[:, :, :], taps[:, :, :], ACT.Square).then_inc(k_squared, 1)

            def filter_root(f):
                act.wait_ge(side_full["L"], filled(f"energy{f}", "L"))
                if f:
                    act.wait_ge(spec_done, f)
                act.activation(k_norm[:, :], side[:, 0, :], ACT.Sqrt, bias=eps[:, 0:1]).then_inc(side_free["L"], 1)

            def conf_centers(i):
                for b in range(2):
                    act.wait_ge(stream_free[2 + b], i + 1)
                for t in range(4 * i, 4 * i + 4):
                    act.activation(conf[:, t, :], u[:, t, :], ACT.Identity, bias=column("conf_b", t),
                                   scale=column("conf_w", (TAPS // 2) * 8 + t)).then_inc(conf_center, 1)

            def softmax(h):
                act.wait_ge(shift_done, h + 1)
                if h:
                    act.wait_ge(side_full["L"], filled(f"turn_p{h - 1}", "L"))
                for t in range(2):
                    e = act.activation(prob[:, t, :], side[:, 2, bass.ts(t, S)], ACT.Exp, bias=shift[:, t:t + 1],
                                       scale=SM_SCALE, accum_out=total[:, t:t + 1])
                e.then_inc(side_free["R"], 1)

            def evacuate_probs(h):
                act.wait_ge(side_full["L"], filled(f"turn_p{h}", "L"))
                act.activation(prob_t[:, :, :], side[:, 0, :].rearrange("p (a b) -> p a b", a=2), ACT.Copy).then_inc(side_free["L"], 1)

            def split_head(h):
                act.wait_ge(side_full["L"], filled(f"pv{h}", "L"))
                act.activation(b_hi[:, 4 * h:4 * h + 4, :], pair("L").rearrange("p a (t s) -> p (a t) s", t=2),
                               ACT.Copy).then_inc(o_hi_done, 1)

            def sine(layer):
                act.wait_ge(angle_step, 5 * (layer + 1))
                act.activation(hidden[:, layer % 2, 1:S + 1], angle[:, :], ACT.Sin).then_inc(sin_done, 1)

            act.wait_ge(params_landed, 16)
            for p in range(4):
                act.wait_ge(x_landed[p], 16)
                gain_hi(0, p)
                split_piece(p)
                if p == 1:
                    sine(0)
            for g in range(4):
                square(0, g)
            sine(1)
            for s in range(SLOTS):
                for p in range(4 * s + 4, 4 * s + 8):
                    split_piece(p)
                    if s in (15, 16) and p % 4 == 1:
                        if s == 15:
                            act.wait_ge(mem_landed, 16)
                            act.wait_ge(spec_done, 4)
                        square(1, 2 * s - 30)
                if s == 0:
                    sine(2)
                    act.wait_ge(made, 3)
                    rms_root(0)
                if 1 <= s < 13 and s % 3 == 1:
                    filter_square(s // 3)
                if 1 <= s < 13 and s % 3 == 2:
                    filter_root(s // 3)
                if s in (1, 5):
                    i = s // 4
                    for b in range(2):
                        act.wait_ge(stream_free[b], i + 1)
                    act.activation(sigm[:, :, :], sigm[:, :, :], ACT.Sigmoid).then_inc(sigmoid_done, 1)
                if s in (3, 7):
                    conf_centers(s // 4)
                if s in (11, 12, 14, 16):
                    evacuate_turned((11, 12, 14, 16).index(s))
                if s in (10, 11, 13, 15, 17, 19):
                    short_centers(s // 2 - 4 if s > 10 else 0)
                if s in (15, 16):
                    square(1, 2 * s - 29)
                if s == 17:
                    rms_root(1)
                if s in (18, 19):
                    if s == 18:
                        act.wait_ge(mem_scaled, 4)
                    for g in (2 * s - 36, 2 * s - 35):
                        gain_hi(1, g)
                if s in (21, 23, 25, 27):
                    i = (s - 21) // 2
                    evacuate(K0 + i, lambda b: keys[:, 4 * i + 2 * b:4 * i + 2 * b + 2, :])
                if s in (29, 31, 33, 35):
                    i = (s - 29) // 2
                    evacuate(V0 + i, lambda b: values[:, b, i * HALF:(i + 1) * HALF].rearrange("p (a s) -> p a s", a=2))
                if s == 32:
                    act.wait_ge(side_free["R"], emptied("mean", "R"))
                    act.activation(u[:, :, :], conf[:, :, :], ACT.Square).then_inc(conf_squared, 1)
                if s == 33:
                    act.wait_ge(side_full["R"], filled("variance", "R"))
                    act.activation(root[:, :], side[:, 2, 0:S], ACT.Sqrt, bias=eps[:, 0:1], scale=1.0 / CONF).then_inc(side_free["R"], 1)
                if s == 34:
                    for t in range(8):
                        if t % 4 == 0:
                            act.wait_ge(ln_step, 2 + t // 4)
                        act.activation(conf[:, t, :], conf[:, t, :], ACT.Silu, bias=column("ln_b", t),
                                       scale=column("ln_g", t)).then_inc(conf_done, 1)
                if s == 34:
                    act.wait_ge(conf_done, 8)
                    mix_hi(0)
                    mix_hi(1)
                if s == 35:
                    act.wait_ge(side_free["L"], emptied("idft3", "L"))
                    mix_hi(2)
                    mix_hi(3)
                if s in (37, 39, 41, 43, 53, 55, 57, 59):
                    g = (s - 37) // 2 % 4
                    n = 2 if s < 44 else 3
                    for b in range(2):
                        panel = s // 2
                        act.wait_ge(stream_free[(panel % 2) * 2 + b], panel // 2 + 1)
                    if n == 3 or g == 3:
                        gain_hi(n, g)
                    square(n, g)
                if s == 42:
                    gain_hi(2, 0)
                    gain_hi(2, 1)
                    gain_hi(2, 2)
                if s == 44:
                    rms_root(2)
                if s in (47, 49):
                    evacuate_probs((s - 47) // 2)
                if s in (48, 50):
                    split_head((s - 48) // 2)
                if s in (46, 48, 50):
                    softmax((s - 46) // 2)
                if s == 51:
                    evacuate_probs(2)
                    softmax(3)
                    split_head(2)
                if s == 52:
                    evacuate_probs(3)
                    split_head(3)
            def up_slab(i, first):
                for j in range(4, 20):
                    act.wait_ge(raw_landed[j % RING], i * 64 + 16 * ((FFN_PIECE0 + j) // RING + 1))
                    act.wait_ge(piece_used, i * 16 + (FFN_PIECE0 + j - RING + 1))
                    act.activation(w_hi[:, j % RING, :], raw[:, j % RING, :], ACT.Copy).then_inc(hi_done, 1)
                    if first and j == 8:
                        rms_root(3)
                    if j == 11:
                        act.wait_ge(ffn_par_ready, i + 1)
                        act.wait_ge(hi_done, i * 16 + (FFN_PIECE0 + j + 1))
                        for t in range(4):
                            if t % 2 == 0:
                                act.wait_ge(stream_free[t // 2], i + (PANELS // 2 + 1))
                            act.activation(gate[:, t, :], gate_in[:, t, :], ACT.Identity,
                                           bias=ffn_par[:, 12 + t:13 + t], scale=ffn_par[:, 4 + t:5 + t]).then_inc(gate_center, 1)
                        act.wait_ge(gate_done, i * 2 + 2)
                        act.wait_ge(stream_free[3], i + PANELS // 2)
                        act.activation(silu[:, :, :], gate[:, :, :], ACT.Silu).then_inc(silu_done, 1)
                act.wait_ge(stream_free[3], i + (PANELS // 2 + 1))
                act.activation(h_hi[:, bass.ds(i * 4, 4), :], hv[:, :, :], ACT.Copy).then_inc(h_hi_done, 1)

            up_slab(0, True)
            with act.Fori(1, SLABS) as i:
                up_slab(i, False)
            def split_down(g, first, last):
                for j in range(first, last):
                    act.wait_ge(raw_landed[j % RING], g * 32 + 16 * ((DOWN_PIECE0 + j) // RING + 1))
                    act.wait_ge(piece_used, g * 8 + (DOWN_PIECE0 + j - RING + 1))
                    act.activation(w_hi[:, j % RING, :], raw[:, j % RING, :], ACT.Copy).then_inc(hi_done, 1)

            with act.Fori(0, SLABS - 1) as g:
                split_down(g, 4, 12)
            split_down(SLABS - 1, 4, 8)
            for g in range(3):
                act.wait_ge(down_added, 2 * g + 2)
                square(4, g)
                for j in range(4 * g, 4 * g + 4):
                    act.activation(y_out[:, j, :], x[:, j, :], ACT.Identity, scale=column("g_final", j)).then_inc(y_gained, 1)
            act.wait_ge(folded_in, 4 * 4 + 3)
            for b in range(2):
                act.wait_ge(down_added, 7 + b)
                act.activation(squares[:, 0, 2 * b:2 * b + 2, :], x[:, 12 + 2 * b:14 + 2 * b, :], ACT.Square).then_inc(squared, 1)
            act.wait_ge(final_squares_used, 1)
            act.activation(root[:, :], side[:, 0, 0:S], ACT.Sqrt, bias=eps[:, 0:1], scale=1.0 / D).then_inc(side_free["L"], 1)

        @block.vector
        def _(dve):
            rounds = iter(range(2 * (TAPS - 1)))

            def conf_round():
                r = next(rounds, None)
                if r is None:
                    return
                i, tap = r // (TAPS - 1), r % (TAPS - 1)
                off = [j for j in range(TAPS) if j != TAPS // 2][tap] - TAPS // 2
                a, b = max(0, -off), S - max(0, off)
                for t in range(4):
                    c = 4 * i + t
                    if tap == 0:
                        dve.wait_ge(conf_center, c + 1)
                    else:
                        dve.wait_ge(conf_taps, 4 * (r - 1) + t + 1)
                    w = COL["conf_w"] + (off + TAPS // 2) * 8 + c
                    dve.scalar_tensor_tensor(out=conf[:, c, a:b], in0=u[:, c, a + off:b + off],
                                             scalar=par[:, w:w + 1], in1=conf[:, c, a:b],
                                             op0=ALU.mult, op1=ALU.add).then_inc(conf_taps, 1)

            def split_piece(p):
                dve.wait_ge(hi_done, p + 1)
                dve.tensor_tensor(w_lo[:, p % RING, :], raw[:, p % RING, :],
                                  w_hi[:, p % RING, :].bitcast(F32), ALU.subtract).then_inc(lo_done, 1)

            def rms_inverse(n):
                b = norm_phase(n)[5]
                dve.wait_ge(side_free[b], emptied(f"stats{n}", b) if n < 4 else SIDE_FREE_END["L"] + 1)
                dve.reciprocal(norm_phase(n)[6][:, :], root[:, :]).then_inc(rms_ready, 1)
                dve.wait_ge(rms_ready, n + 1)

            def gain_lo(n, g):
                dve.wait_ge(a_hi_done, 4 * A_PHASE[n] + g + 1)
                for j in range(4 * g, 4 * g + 4):
                    c = COL[norm_phase(n)[1]] + j
                    op = dve.scalar_tensor_tensor(out=a_lo[:, j, :], in0=norm_phase(n)[0][:, j, :],
                                                  scalar=par[:, c:c + 1], in1=a_hi[:, j, :].bitcast(F32),
                                                  op0=ALU.mult, op1=ALU.subtract)
                op.then_inc(a_ready, 1)

            def mix_lo(g):
                source = conf[:, 4 * g:4 * g + 4, :] if g < 2 else x2[:, 4 * g - 8:4 * g - 4, :]
                dve.wait_ge(a_hi_done, 8 + g + 1)
                dve.tensor_tensor(a_lo[:, 4 * g:4 * g + 4, :], source,
                                  a_hi[:, 4 * g:4 * g + 4, :].bitcast(F32), ALU.subtract).then_inc(a_ready, 1)

            def normalise(panel, b, to):
                bank = (panel % 2) * 2 + b
                wait_bank(dve, panel, b)
                dve.tensor_tensor(to, stream_bank(bank), per_tile(inv_rms, 2), ALU.mult).then_inc(stream_free[bank], 1)

            def add_panel(panel, i):
                for b in range(2):
                    bank = (panel % 2) * 2 + b
                    wait_bank(dve, panel, b)
                    rows = x[:, 4 * i + 2 * b:4 * i + 2 * b + 2, :]
                    dve.tensor_tensor(rows, stream_bank(bank), rows, ALU.add).then_inc(stream_free[bank], 1)

            def short_sides(e):
                panel = 4 + e
                part, half = HYENA_PANELS[e]
                if e:
                    dve.wait_ge(short_done, 2 * e)
                for b in range(2):
                    normalise(panel, b, proj[:, 2 * b:2 * b + 2, :])
                for b in range(2):
                    dve.wait_ge(short_center, 4 * e + 2 * b + 2)
                    for side_ in range(2):
                        for t in range(2):
                            to = x2[:, 4 * half + 2 * b + t, :] if part == 2 else turned[:, 2 * b + t, :]
                            c = COL["short_w"] + 48 * side_ + part * 8 + half * 4 + 2 * b + t
                            o, i_ = ((1, S), (0, S - 1)) if side_ == 0 else ((0, S - 1), (1, S))
                            if side_:
                                dve.wait_ge(short_left, 4 * e + 2 * b + t + 1)
                            op = dve.scalar_tensor_tensor(out=to[:, o[0]:o[1]], in0=proj[:, 2 * b + t, i_[0]:i_[1]],
                                                          scalar=par[:, c:c + 1], in1=to[:, o[0]:o[1]],
                                                          op0=ALU.mult, op1=ALU.add)
                            if side_ == 0:
                                op.then_inc(short_left, 1)
                            elif t:
                                op.then_inc(short_done, 1)

            def filter_window(f):
                if f == 0:
                    dve.wait_ge(a_ready, 4)
                if f % 2 == 0:
                    dve.wait_ge(decay_landed, 16 * (f // 2 + 1))
                if f:
                    dve.wait_ge(k_folded, 2 * f)
                for d in range(2):
                    dve.wait_ge(side_full["LR"[d]], filled(f"taps{f}", "LR"[d]))
                    dve.tensor_tensor(taps[:, 2 * d:2 * d + 2, :], side[:, 2 * d:2 * d + 2, :],
                                      decay_sb[:, 2 * d:2 * d + 2, :], ALU.mult).then_inc(side_free["LR"[d]], 1)

            def filter_fold(f):
                dve.wait_ge(side_free["L"], emptied(f"energy{f}", "L"))
                dve.tensor_tensor(folded[:, 0:2, :], taps[:, 0:2, :], taps[:, 2:4, :], ALU.add).then_inc(k_folded, 1)
                dve.tensor_tensor(folded[:, 2:4, :], taps[:, 0:2, :], taps[:, 2:4, :], ALU.subtract).then_inc(k_folded, 1)
                dve.reciprocal(k_norm[:, :], k_norm[:, :]).then_inc(k_norm_ready, 1)

            def filter_finish(f):
                to = spec[f % 2]
                half = f // 2
                dve.wait_ge(k_norm_ready, f + 1)
                dve.wait_ge(side_full["L"], filled(f"spec{f}", "L"))
                norm2 = k_norm[:, :].rearrange("p (a n) -> p a n", a=1).to_broadcast([P, 2, HALF])
                dve.tensor_tensor(to[:, half, 0:2, :], pair("L"), norm2, ALU.mult).then_inc(side_free["L"], 1)
                dve.wait_ge(side_full["R"], filled(f"spec{f}", "R"))
                dve.tensor_tensor(to[:, half, 2:4, :], pair("R"), norm2, ALU.mult).then_inc(side_free["R"], 1)
                dve.wait_ge(side_full["L"], filled(f"spec_im{f}", "L"))
                dve.tensor_tensor(to[:, half, 4, :], side[:, 0, :], k_norm[:, :], ALU.mult).then_inc(side_free["L"], 1)
                dve.wait_ge(skip_landed, 16 * (f + 1))
                dve.wait_ge(side_free["L"], emptied(f"spec_im{f}", "L"))
                skip3 = skip_sb[:, :].rearrange("p (a n) -> p a n", a=1).to_broadcast([P, 3, HALF])
                dve.tensor_tensor(to[:, half, 0:3, :], to[:, half, 0:3, :], skip3, ALU.add).then_inc(spec_done, 1)

            def multiply(c):
                order, half = c // 2, c % 2
                k = spec[order]
                real, real_nyq = [k[:, half, 0, :], k[:, half, 1, :]], [k[:, half, 2, :], k[:, half, 1, :]]
                if c == 0:
                    dve.wait_ge(short_done, 12)
                dve.wait_ge(side_full["L"], filled(f"dft{c}", "L"))
                dve.tensor_tensor(spectrum[:, 0:2, :], pair("L"), k[:, half, 0:2, :], ALU.mult)
                dve.tensor_tensor(spectrum[:, 2:4, :], pair("L"), k[:, half, 3:5, :], ALU.mult).then_inc(side_free["L"], 1)
                dve.wait_ge(side_full["R"], filled(f"dft{c}", "R"))
                if c:
                    dve.wait_ge(product_done, 2 * c)
                dve.tensor_tensor(cross[:, :, :], pair("R"), k[:, half, 3:5, :], ALU.mult).then_inc(product_step, 1)
                dve.wait_ge(product_step, 2 * c + 1)
                dve.tensor_tensor(spectrum[:, 0:2, :], spectrum[:, 0:2, :], cross[:, :, :], ALU.subtract).then_inc(product_done, 1)
                dve.wait_ge(product_done, 2 * c + 1)
                dve.tensor_tensor(cross[:, 0, :], side[:, 2, :], real_nyq[0], ALU.mult).then_inc(product_step, 1)
                dve.tensor_tensor(cross[:, 1, :], side[:, 3, :], real_nyq[1], ALU.mult).then_inc(side_free["R"], 1)
                dve.wait_ge(side_free["R"], emptied(f"dft{c}", "R"))
                dve.tensor_tensor(spectrum[:, 2:4, :], spectrum[:, 2:4, :], cross[:, :, :], ALU.add).then_inc(product_done, 1)

            def gate_by(c):
                dve.wait_ge(side_full["L"], filled(f"idft{c}", "L"))
                half = c % 2
                if c < 2:
                    to = x1_t[:, half, :, :]
                    dve.wait_ge(side_free["L"], emptied(f"turn{2 * half + 1}", "L"))
                    dve.tensor_tensor(to, pair("L"), to, ALU.mult).then_inc(side_free["L"], 1)
                else:
                    to = x2[:, 4 * half:4 * half + 4, :]
                    dve.tensor_tensor(to, pair("L").rearrange("p a (t s) -> p (a t) s", t=2), to,
                                      ALU.mult).then_inc(side_free["L"], 1)

            def softmax_shift(h):
                dve.wait_ge(side_full["R"], filled(f"scores{h}", "R"))
                dve.tensor_reduce(peak[:, :], side[:, 2, :].rearrange("p (a s) -> p a s", a=2), AX_X,
                                  ALU.max).then_inc(peak_done, 1)
                dve.wait_ge(peak_done, h + 1)
                dve.tensor_scalar(shift[:, :], peak[:, :], -SM_SCALE, None, ALU.mult).then_inc(shift_done, 1)

            def softmax_norm(h):
                dve.wait_ge(side_free["R"], emptied(f"scores{h}", "R"))
                dve.reciprocal(inv_total[:, :], total[:, :]).then_inc(inv_total_done, 1)
                dve.wait_ge(inv_total_done, h + 1)
                for t in range(2):
                    op = dve.tensor_scalar(prob[:, t, :], prob[:, t, :], inv_total[:, t:t + 1], None, ALU.mult)
                op.then_inc(prob_ready, 1)

            def split_head(h):
                dve.wait_ge(o_hi_done, h + 1)
                dve.tensor_tensor(b_lo[:, 4 * h:4 * h + 4, :], pair("L").rearrange("p a (t s) -> p (a t) s", t=2),
                                  b_hi[:, 4 * h:4 * h + 4, :].bitcast(F32), ALU.subtract).then_inc(side_free["L"], 1)

            magic = 1.5 * 2.0 ** 23
            two_pi_hi = 6.28125
            two_pi_lo = 2 * np.pi - two_pi_hi
            def mlp_angle(layer):
                dve.wait_ge(side_full["R"], filled(f"mlp{layer}", "R"))
                if layer == 0:
                    dve.wait_ge(params_landed, 16)
                else:
                    dve.wait_ge(sin_done, layer)
                b = COL["mlp_b"] + layer
                dve.tensor_scalar(angle[:, :], side[0:MLP, 2, 0:S], par[0:MLP, b:b + 1],
                                  par[0:MLP, COL["freq"]:COL["freq"] + 1], ALU.add, ALU.mult).then_inc(side_free["R"], 1)
                dve.wait_ge(side_free["R"], emptied(f"mlp{layer}", "R"))
                dve.tensor_scalar(turns[:, :], angle[:, :], 1.0 / (2 * np.pi), magic, ALU.mult, ALU.add).then_inc(angle_step, 1)
                dve.wait_ge(angle_step, 5 * layer + 1)
                dve.tensor_scalar(turns[:, :], turns[:, :], -magic, None, ALU.add).then_inc(angle_step, 1)
                dve.wait_ge(angle_step, 5 * layer + 2)
                dve.scalar_tensor_tensor(out=angle[:, :], in0=turns[:, :], scalar=-two_pi_hi, in1=angle[:, :],
                                         op0=ALU.mult, op1=ALU.add).then_inc(angle_step, 1)
                dve.wait_ge(angle_step, 5 * layer + 3)
                dve.scalar_tensor_tensor(out=angle[:, :], in0=turns[:, :], scalar=-two_pi_lo, in1=angle[:, :],
                                         op0=ALU.mult, op1=ALU.add).then_inc(angle_step, 1)
                dve.wait_ge(angle_step, 5 * layer + 4)
                dve.tensor_scalar(angle[:, :], angle[:, :], PI_BELOW, -PI_BELOW, ALU.min, ALU.max).then_inc(angle_step, 1)
            mlp_angle(0)
            for p in range(4):
                dve.wait_ge(x_landed[p], 16)
                gain_lo(0, p)
                split_piece(p)
            mlp_angle(1)
            for s in range(SLOTS):
                conv = 0 if s < 4 else 3 if s % 7 == 0 else 2
                for p in range(4 * s + 4, 4 * s + 8):
                    split_piece(p)
                    if p % 4 >= 4 - conv:
                        conf_round()
                if s == 0:
                    mlp_angle(2)
                    rms_inverse(0)
                if 1 <= s < 13:
                    (filter_window, filter_fold, filter_finish)[(s - 1) % 3]((s - 1) // 3)
                if s in (1, 5):
                    i = s // 4
                    if i:
                        dve.wait_ge(stream_free[3], i)
                    for b in range(2):
                        normalise(2 * i, b, sigm[:, 2 * b:2 * b + 2, :])
                if s in (3, 7):
                    i = s // 4
                    panel = 2 * i + 1
                    dve.wait_ge(glu_gate_ready, i + 1)
                    for b in range(2):
                        wait_bank(dve, panel, b)
                        dve.tensor_tensor(u[:, 4 * i + 2 * b:4 * i + 2 * b + 2, :], stream_bank(2 + b),
                                          sigm[:, 2 * b:2 * b + 2, :], ALU.mult).then_inc(stream_free[2 + b], 1)
                if s in (10, 11, 13, 15, 17, 19):
                    short_sides(s // 2 - 4 if s > 10 else 0)
                if s == 17:
                    rms_inverse(1)
                    for g in range(4):
                        m = mem_x[:, 4 * g:4 * g + 4, :]
                        dve.tensor_tensor(m, m, per_tile(inv_mem, 4), ALU.mult).then_inc(mem_scaled, 1)
                if s in (18, 19):
                    dve.wait_ge(mem_scaled, 4)
                    for g in (2 * s - 36, 2 * s - 35):
                        gain_lo(1, g)
                if s in (19, 22, 25, 28):
                    multiply((s - 19) // 3)
                if s in (21, 24, 27, 30):
                    gate_by((s - 21) // 3)
                if s == 32:
                    dve.wait_ge(side_full["R"], filled("mean", "R"))
                    mean4 = side[:, 2:3, 0:S].to_broadcast([P, 4, S])
                    dve.wait_ge(conf_taps, 8 * (TAPS - 1))
                    for i in range(2):
                        c = conf[:, 4 * i:4 * i + 4, :]
                        op = dve.scalar_tensor_tensor(out=c, in0=mean4, scalar=-1.0 / CONF, in1=c,
                                                      op0=ALU.mult, op1=ALU.add)
                    op.then_inc(side_free["R"], 1)
                if s == 33:
                    dve.wait_ge(side_free["R"], emptied("variance", "R"))
                    dve.reciprocal(inv_rms[:, :], root[:, :]).then_inc(ln_step, 1)
                    dve.wait_ge(ln_step, 1)
                    inv4 = inv_rms[:, :].rearrange("p (a s) -> p a s", a=1).to_broadcast([P, 4, S])
                    for i in range(2):
                        c = conf[:, 4 * i:4 * i + 4, :]
                        dve.tensor_tensor(c, c, inv4, ALU.mult).then_inc(ln_step, 1)
                if s in (34, 35):
                    for g in (2 * s - 68, 2 * s - 67):
                        mix_lo(g)
                if s in (37, 39, 41, 43, 53, 55, 57, 59):
                    i = (s - 37) // 2 % 4
                    if s == 37:
                        dve.wait_ge(x_again_landed, 16)
                    add_panel(s // 2, i)
                    if s > 44 or i == 3:
                        gain_lo(2 if s < 44 else 3, i)
                if s == 42:
                    for g in range(3):
                        gain_lo(2, g)
                if s == 44:
                    rms_inverse(2)
                if s in (45, 47, 49, 51):
                    h = (s - 45) // 2
                    if h >= 2:
                        dve.wait_ge(side_full["R"], filled(f"scores{h - 2}", "R"))
                    for b in range(2):
                        normalise(Q0 + h, b, q[:, h % 2, 2 * b:2 * b + 2, :])
                if s in (48, 50):
                    split_head((s - 48) // 2)
                if s in (46, 48, 50):
                    softmax_shift((s - 46) // 2)
                    softmax_norm((s - 46) // 2)
                if s == 51:
                    softmax_shift(3)
                    softmax_norm(3)
                    split_head(2)
                if s == 52:
                    split_head(3)
            def up_slab(i, first):
                if not first:
                    dve.wait_ge(gate_done, i * 2)
                dve.tensor_copy(ffn_par[:, :], par[:, bass.ds(i * 16 + COL["ffn"], 16)]).then_inc(ffn_par_ready, 1)
                for j in range(4, 20):
                    dve.wait_ge(hi_done, i * 16 + (FFN_PIECE0 + j + 1))
                    dve.tensor_tensor(w_lo[:, j % RING, :], raw[:, j % RING, :],
                                      w_hi[:, j % RING, :].bitcast(F32), ALU.subtract).then_inc(lo_done, 1)
                    if first and j == 8:
                        rms_inverse(3)
                    if j == 11:
                        dve.wait_ge(ffn_par_ready, i + 1)
                        dve.wait_ge(lo_done, i * 16 + (FFN_PIECE0 + j + 1))
                        for b in range(2):
                            if b == 0:
                                dve.wait_ge(stream_full[0], i + (PANELS // 2 + 1))
                            else:
                                dve.wait_ge(piece_used, i * 16 + (FFN_PIECE0 + 8))
                            dve.tensor_tensor(gate_in[:, 2 * b:2 * b + 2, :], stream_bank(b), per_tile(inv_rms, 2),
                                              ALU.mult).then_inc(stream_free[b], 1)
                        for b in range(2):
                            dve.wait_ge(gate_center, i * 4 + (2 * b + 2))
                            for side_ in range(2):
                                for t in range(2):
                                    c = 8 * side_ + 2 * b + t
                                    o, i_ = ((1, S), (0, S - 1)) if side_ == 0 else ((0, S - 1), (1, S))
                                    if side_:
                                        dve.wait_ge(gate_left, i * 4 + (2 * b + t + 1))
                                    op = dve.scalar_tensor_tensor(
                                        out=gate[:, 2 * b + t, o[0]:o[1]], in0=gate_in[:, 2 * b + t, i_[0]:i_[1]],
                                        scalar=ffn_par[:, c:c + 1], in1=gate[:, 2 * b + t, o[0]:o[1]],
                                        op0=ALU.mult, op1=ALU.add)
                                    if side_ == 0:
                                        op.then_inc(gate_left, 1)
                                    elif t:
                                        op.then_inc(gate_done, 1)
                dve.wait_ge(silu_scaled, i + 1)
                dve.wait_ge(lo_done, i * 16 + (FFN_PIECE0 + 20))
                for b in range(2):
                    if b == 0:
                        dve.wait_ge(stream_full[2], i + (PANELS // 2 + 1))
                    else:
                        dve.wait_ge(piece_used, i * 16 + (FFN_PIECE0 + 16))
                    dve.tensor_tensor(hv[:, 2 * b:2 * b + 2, :], stream_bank(2 + b),
                                      silu[:, 2 * b:2 * b + 2, :], ALU.mult).then_inc(stream_free[2 + b], 1)
                dve.wait_ge(h_hi_done, i + 1)
                dve.tensor_tensor(h_lo[:, bass.ds(i * 4, 4), :], hv[:, :, :],
                                  h_hi[:, bass.ds(i * 4, 4), :].bitcast(F32), ALU.subtract).then_inc(h_ready, 1)

            up_slab(0, True)
            with dve.Fori(1, SLABS) as i:
                up_slab(i, False)
            def split_down(g, first, last):
                for j in range(first, last):
                    dve.wait_ge(hi_done, g * 8 + (DOWN_PIECE0 + j + 1))
                    dve.tensor_tensor(w_lo[:, j % RING, :], raw[:, j % RING, :],
                                      w_hi[:, j % RING, :].bitcast(F32), ALU.subtract).then_inc(lo_done, 1)

            with dve.Fori(0, SLABS - 1) as g:
                split_down(g, 4, 12)
            split_down(SLABS - 1, 4, 8)
            for panel in range(4):
                for b in range(2):
                    if b == 0:
                        dve.wait_ge(down_full, panel + 1)
                    else:
                        dve.wait_ge(piece_used, DOWN_PIECE0 + 8 * (SLABS - 1) + 2 * panel + 2)
                    if panel < 2:
                        tiles = side[:, 2 * panel + b, :].rearrange("p (a s) -> p a s", a=2)
                    else:
                        tiles = stream_bank(2 * (panel - 2) + b)
                    rows = x[:, 4 * panel + 2 * b:4 * panel + 2 * b + 2, :]
                    dve.tensor_tensor(rows, tiles, rows, ALU.add).then_inc(down_added, 1)
            dve.wait_ge(down_added, 8)
            for j in range(12, 16):
                c = COL["g_final"] + j
                dve.tensor_scalar(y_out[:, j, :], x[:, j, :], par[:, c:c + 1], None, ALU.mult).then_inc(last_gained, 1)
            rms_inverse(4)
            dve.wait_ge(y_gained, 12)
            dve.wait_ge(last_gained, 4)
            for g in range(1, 4):
                y = y_out[:, 4 * g:4 * g + 4, :]
                dve.tensor_tensor(y, y, per_tile(inv_rms, 4), ALU.mult).then_inc(y_done, 1)


PI_BELOW = float(np.nextafter(np.float32(np.pi), np.float32(0)))


def transform_tables():
    n = 2 * S
    t = np.arange(S)[:, None]
    f = np.arange(S)[None, :]
    turn = 2 * np.pi * ((t * f) % n) / n
    re, im = np.cos(turn), -np.sin(turn)
    nyquist = np.where(t % 2 == 0, 1.0, -1.0)
    im_nyq, re_nyq = im.copy(), re.copy()
    im_nyq[:, 0:1] = nyquist
    re_nyq[:, 0:1] = nyquist
    forward = np.concatenate([re[:, :P], re[:, P:], im_nyq[:, :P], im[:, P:], im[:, :P], re_nyq[:, :P]], axis=1)
    back_re, back_im = 2 * re.T / n, 2 * im.T / n
    back_re[0] = 1.0 / n
    back_im[0] = nyquist[:, 0] / n
    back = np.concatenate([back_re, back_im], axis=0)
    tile = lambda a: np.ascontiguousarray(a.reshape(-1, P, a.shape[1]).transpose(1, 0, 2)).astype(np.float32)
    return tile(forward), tile(back)


def filter_tables():
    f32 = np.float32
    t = np.linspace(0.0, 1.0, S, dtype=f32)
    w = (f32(2.0 * np.pi) * np.arange(S, dtype=f32)) / f32(S)
    bands = (FEATURES - 1) // 2
    f = np.linspace(1e-4, bands - 1, bands, dtype=f32)
    angle = (f[None, :] * w[:, None]).astype(f32).astype(np.float64)
    features = np.concatenate([t[:, None], np.cos(angle), -np.sin(angle)], axis=1).astype(f32).T
    deltas = np.abs(np.linspace(np.log(1e-2) / 1.5, np.log(1e-2) / 0.3, HY, dtype=f32))
    fwd = np.exp((-t[:, None] * deltas[None, :]).astype(f32).astype(np.float64)).astype(f32)
    bwd = np.concatenate([np.zeros((1, HY), f32), fwd[:-1]], axis=0)
    both = np.stack([fwd, bwd]).reshape(2, 2, P, 2, HALF)
    return np.ascontiguousarray(features), np.ascontiguousarray(both.transpose(3, 2, 0, 1, 4).reshape(2, P, 4, HALF))


def kernel(x, mem, g_mix, w_in, conf_dw_w, conf_dw_b, conf_ln_g, conf_ln_b, hyena_short_w,
           hyena_short_b, hyena_w1, hyena_b1, hyena_w_inner, hyena_b_inner, hyena_w_filt,
           hyena_sin_freq, hyena_skip, w_out, g_xattn, g_mem, w_q, w_k, w_v, w_o, g_ffn, w_ffn_up,
           ffn_dw_w, ffn_dw_b, w_ffn_down, g_final):
    import concourse.bacc as bacc
    from concourse.bass_utils import run_bass_kernel_spmd

    def rows(a):
        return np.asarray(a).reshape(-1, P)

    def pad_row(a):
        a = np.asarray(a).reshape(-1, MLP)
        return np.concatenate([a, np.zeros((a.shape[0], P - MLP), a.dtype)], axis=1)

    def on_partitions(a):
        return np.ascontiguousarray(np.asarray(a)[0].T.reshape(KT, P, S).transpose(1, 0, 2))

    ffn = np.concatenate([np.asarray(ffn_dw_w)[0].reshape(3, SLABS, 4, P),
                          np.asarray(ffn_dw_b)[0].reshape(1, SLABS, 4, P)], axis=0).transpose(1, 0, 2, 3)
    packed = [rows(conf_dw_w), rows(conf_dw_b), rows(conf_ln_g), rows(conf_ln_b), rows(hyena_short_w),
              rows(hyena_short_b), rows(ffn), rows(g_mix), rows(g_mem), rows(g_xattn), rows(g_ffn),
              rows(g_final), pad_row(hyena_b1), pad_row(hyena_b_inner), pad_row(hyena_sin_freq)]
    params = np.ascontiguousarray(np.concatenate(packed, axis=0).T)
    forward, back = transform_tables()
    features, decay = filter_tables()
    arrays = {
        "x_t": on_partitions(x), "mem_t": on_partitions(mem), "params": params,
        "w_in": w_in, "w1": hyena_w1, "w_inner": hyena_w_inner, "w_filt": hyena_w_filt,
        "skip": hyena_skip, "w_out": w_out, "w_q": w_q, "w_k": w_k, "w_v": w_v, "w_o": w_o,
        "w_up": w_ffn_up, "w_down": w_ffn_down,
        "dft": forward, "idft": back, "decay": decay, "features": features,
    }
    for name in ("w_in", "w1", "w_inner", "w_filt", "skip", "w_out", "w_q", "w_k", "w_v", "w_o", "w_up", "w_down"):
        arrays[name] = np.ascontiguousarray(np.asarray(arrays[name])[0])
    nc = bacc.Bacc("TRN2", target_bir_lowering=False, num_devices=1)
    args = [nc.dram_tensor(n, a.shape, mybir.dt.from_np(a.dtype), kind="ExternalInput").ap()
            for n, a in arrays.items()]
    out = nc.dram_tensor("out", (P, KT, S), F32, kind="ExternalOutput").ap()
    block_program(nc, *args, out)
    result = run_bass_kernel_spmd(nc, [arrays], core_ids=[0]).results[0]["out"]
    return np.ascontiguousarray(np.asarray(result).transpose(1, 0, 2).reshape(D, S).T)[None]
```

```python
from contextlib import ExitStack

import concourse.bass as bass
import numpy as np
from concourse import mybir

F32 = mybir.dt.float32
F32R = mybir.dt.float32r
ALU = mybir.AluOpType
ACT = mybir.ActivationFunctionType
AX_X = mybir.AxisListType.X

P = 128
S = 256
D = 2048
KT = D // P
HALF = 512
CONF = 1024
HY = 1024
TAPS = 31
HEADS = 4
FF = 5632
SLABS = FF // 512
RING = 4
MLP = 64
FEATURES = 33
EPS = 1e-6
SM_SCALE = float(D // HEADS) ** -0.5
PANELS = 30
SLOTS = 2 * PANELS

CONF_PANELS = [("gate", 0), ("value", 0), ("gate", 1), ("value", 1)]
HYENA_PANELS = [(0, 0), (1, 0), (0, 1), (1, 1), (2, 0), (2, 1)]
K0, V0, OUT0, Q0, O0 = 10, 14, 18, 22, 26

COL = {}
_at = 0
for _name, _n in (("conf_w", TAPS * 8), ("conf_b", 8), ("ln_g", 8), ("ln_b", 8),
                  ("short_w", 3 * 24), ("short_b", 24), ("ffn", SLABS * 16),
                  ("g_mix", KT), ("g_mem", KT), ("g_xattn", KT), ("g_ffn", KT), ("g_final", KT),
                  ("mlp_b", 3), ("freq", 1)):
    COL[_name] = _at
    _at += _n
PARAM_COLS = _at

SIDE = [("mlp0", "R"), ("mlp1", "R"), ("mlp2", "R"), ("stats0", "L"),
        ("taps0", "LR"), ("energy0", "L"), ("spec0", "LR"), ("spec_im0", "L"),
        ("taps1", "LR"), ("energy1", "L"), ("spec1", "LR"), ("spec_im1", "L"),
        ("taps2", "LR"), ("energy2", "L"), ("spec2", "LR"), ("spec_im2", "L"),
        ("taps3", "LR"), ("energy3", "L"), ("turn0", "L"), ("spec3", "LR"), ("turn1", "L"),
        ("spec_im3", "L"), ("turn2", "L"), ("turn3", "L"), ("stats1", "R"),
        ("dft0", "LR"), ("idft0", "L"), ("dft1", "LR"), ("idft1", "L"),
        ("dft2", "LR"), ("idft2", "L"), ("dft3", "LR"), ("idft3", "L"),
        ("mean", "R"), ("variance", "R"), ("stats2", "R"),
        ("scores0", "R"), ("turn_p0", "L"), ("pv0", "L"), ("scores1", "R"), ("turn_p1", "L"),
        ("pv1", "L"), ("scores2", "R"), ("turn_p2", "L"), ("pv2", "L"), ("scores3", "R"),
        ("turn_p3", "L"), ("pv3", "L"), ("stats3", "R")]


SHORT = ((11, 0), (12, 1), (14, 0), (16, 0), (18, 0), (20, 0))

SPEC_IM = ((4, 1), (7, 1), (10, 1), (13, 2))

TURNS = ((12, 1), (13, 1), (15, 1), (17, 1))

SCORES = ((46, 2), (48, 2), (50, 2), (52, 1))
SOFTMAX = ((46, 3), (48, 3), (50, 3), (52, 2))
TURN_PROBS = ((47, 1), (49, 1), (51, 1), (52, 3))
ATTEND = ((47, 3), (49, 3), (51, 3), (53, 0))

TRANSFORM = ((19, 3), (23, 0), (26, 0), (29, 0))
PRODUCT = ((20, 3), (23, 1), (26, 1), (29, 1))
PRODUCT_HI = ((21, 1), (24, 0), (27, 0), (30, 0))
PRODUCT_LO = ((21, 2), (24, 1), (27, 1), (30, 1))
TRANSFORM_BACK = ((22, 2), (25, 1), (28, 1), (31, 1))


def chain_step(s, j, n):
    at = divmod(4 * s + j - n, 4)
    return PRODUCT.index(at) if at in PRODUCT else None


CHAIN_WORK = [divmod(4 * s + j + n, 4) for s, j in PRODUCT for n in range(3)] + [*PRODUCT_LO, TRANSFORM_BACK[0]]

FIRST_TAPS = sorted([(14, 3), (16, 3)] + [(s, j) for s in (15, 17) for j in range(3)] + [(19, 0), (19, 2)]
                    + [(s, j) for s in range(21, 32) for j in range(3) if (s, j) not in CHAIN_WORK])[:TAPS - 1]
assert len(FIRST_TAPS) == TAPS - 1


def side_counts():
    full, free, need = {"L": 0, "R": 0}, {"L": 0, "R": 0}, {}
    for name, pairs in SIDE:
        for b in pairs:
            before = free[b]
            free[b] += 1
            full[b] += 1
            need[name, b] = (before, full[b], free[b])
    return need, free


SIDE_AT, SIDE_FREE_END = side_counts()


def before(name, b):
    return SIDE_AT[name, b][0]


def filled(name, b):
    return SIDE_AT[name, b][1]


def emptied(name, b):
    return SIDE_AT[name, b][2]


def block_program(nc, x_t, mem_t, params, w_in, w1, w_inner, w_filt, skip, w_out, w_q, w_k, w_v,
                  w_o, w_up, w_down, filter_dft, dft, idft, decay, features, out):
    KB = 1024
    base = 16512

    def at(name, kb, shape, dt=F32):
        return nc.alloc_sbuf_tensor_at(name, shape, dt, offset=base + int(kb * KB))

    with ExitStack() as ctx:
        def sem(name):
            return ctx.enter_context(nc.semaphore(name))

        raw = at("raw", 0, [P, RING, 1024])
        w_hi = at("w_hi", 16, [P, RING, 1024], F32R)
        w_lo = at("w_lo", 32, [P, RING, 1024], F32R)
        par = at("par", 48, [P, PARAM_COLS])
        eps, peak, shift, total, inv_total, warm = (
            at(name, 50.5 + i / 32, [P, n])
            for i, (name, n) in enumerate((("eps", 1), ("peak", 2), ("shift", 2), ("total", 2), ("inv_total", 2), ("warm", 2))))
        ident = at("ident", 51, [P, P])
        ones = at("ones", 51.5, [P, P])
        root = at("root", 52, [P, S])
        inv_rms = at("inv_rms", 53, [P, S])
        a_hi = at("a_hi", 54, [P, KT, S], F32R)
        a_lo = at("a_lo", 70, [P, KT, S], F32R)
        x_first = at("x_first", 86, [P, KT, S])
        taps = at("taps", 86, [P, 4, HALF])
        folded = at("folded", 94, [P, 4, HALF])
        mem_x = at("mem_x", 86, [P, KT, S])
        keys_hi = at("keys_hi", 86, [P, KT, S], F32R)
        keys_lo = at("keys_lo", 102, [P, KT, S], F32R)
        values_hi = [at(f"values_hi{h}", 118 + 8 * h, [P, 2, HALF], F32R) for h in range(HEADS)]
        values_lo = [at(f"values_lo{h}", 122 + 8 * h, [P, 2, HALF], F32R) for h in range(HEADS)]
        spec = [at("spec_first", 102, [P, 2, 5, HALF]), at("spec_second", 122, [P, 2, 5, HALF])]
        filter_dft_raw = at("filter_dft_raw", 112, [P, 2, 640])
        filter_dft_hi = at("filter_dft_hi", 142, [P, 2, 640], F32R)
        filter_dft_lo = at("filter_dft_lo", 147, [P, 2, 640], F32R)
        folded_lo = at("folded_lo", 94, [P, 4, HALF], F32R)
        folded_hi = [at(f"folded_hi{f}", 132, [P, 4, HALF], F32R) for f in range(3)]
        folded_hi.append(at("folded_hi3", 184, [P, 4, HALF], F32R))
        k_squares = [at(f"k_squares{f}", 132 if f < 3 else 184, [P, 4, HALF]) for f in range(4)]
        dft_sb = at("dft_sb", 142, [P, 2, 512])
        idft_raw = at("idft_raw", 196, [P, 4, S])
        idft_hi = at("idft_hi", 146, [P, 4, S], F32R)
        idft_lo = [at("idft_lo_re", 150, [P, 2, S], F32R), at("idft_lo_im", 204, [P, 2, S], F32R)]
        u = at("u", 152, [P, 8, S])
        conf = at("conf", 160, [P, 8, S])
        v_t = at("v_t", 168, [P, 2, 2, HALF])
        x1_t = at("x1_t", 176, [P, 2, 2, HALF])
        x2 = at("x2", 184, [P, 8, S])
        decay_sb = at("decay_sb", 184, [P, 4, HALF])
        spectrum = at("spectrum", 192, [P, 4, HALF])
        spectrum_lo = at("spectrum_lo", 192, [P, 4, HALF], F32R)
        spectrum_hi = [at(f"spectrum_hi{c}", 168 if c else 94, [P, 4, HALF], F32R) for c in range(4)]
        sigm = at("sigm", 192, [P, 4, S])
        skip_sb = at("skip_sb", 196, [P, HALF])
        k_norm = at("k_norm", 198, [P, HALF])
        w_filt_sb = at("w_filt_sb", 200, [P, 2, HALF])
        w_filt_hi = at("w_filt_hi", 176, [P, 2, HALF], F32R)
        w_filt_lo = at("w_filt_lo", 180, [MLP, 2, HALF], F32R)
        cross = at("cross", 200, [P, 2, HALF])
        turned = at("turned", 200, [P, 4, S])
        proj = at("proj", 192, [P, 4, S])
        squares_x = at("squares_x", 168, [P, 4, 4, S])
        sum_x = at("sum_x", 206.5, [P, S])
        tapped = at("tapped", 206.5, [P, S])
        squares_m = at("squares_m", 196, [P, 1, 4, S])
        sum_m = at("sum_m", 204, [P, S])
        inv_mem = at("inv_mem", 205, [P, S])
        feat = at("feat", 102, [FEATURES, S])
        w1_sb = at("w1_sb", 103, [FEATURES, MLP])
        w_inner_sb = at("w_inner_sb", 103.25, [MLP, 3, MLP])
        angle = at("angle", 104, [P, S])
        turns = at("turns", 105, [P, S])
        hidden = at("hidden", 204, [P, 2, 264])
        hidden_hl = at("hidden_hl", 204 + 264 * 4 / 1024, [P, S + 1], F32R)
        x = at("x", 191.75, [P, KT, S])
        squares = at("squares", 186, [P, 1, 4, S])
        squares_y = at("squares_y", 174, [P, 4, 4, S])
        sum_sq = at("sum_sq", 190.5, [P, S])
        b_hi = at("b_hi", 86, [P, KT, S], F32R)
        b_lo = at("b_lo", 102, [P, KT, S], F32R)
        q = at("q", 174, [P, 4, S])
        q_lo = at("q_lo", 174, [P, 4, S], F32R)
        q_hi = at("q_hi", 178, [P, 4, S], F32R)
        prob = at("prob", 182, [P, 2, S])
        prob_t_hi = at("prob_t_hi", 184, [P, 2, S], F32R)
        prob_t_lo = at("prob_t_lo", 150, [P, 2, S], F32R)
        h_hi = at("h_hi", 86, [P, SLABS * 4, S], F32R)
        h_lo = at("h_lo", 130, [P, SLABS * 4, S], F32R)
        gate = at("gate", 174, [P, 4, S])
        silu = at("silu", 178, [P, 4, S])
        hv = at("hv", 182, [P, 4, S])
        gate_in = at("gate_in", 186, [P, 4, S])
        ffn_par = at("ffn_par", 190, [P, 16])
        y_out = at("y_out", 86, [P, KT, S])

        stream = ctx.enter_context(nc.psum_tensor("stream", [P, 4, 2, S], F32))
        side = ctx.enter_context(nc.psum_tensor("side", [P, 4, 512], F32))

        def stream_bank(b):
            return stream[:, b, :, :]

        raw_landed = [sem(f"raw_landed{i}") for i in range(RING)]
        hi_done, lo_done, piece_used = sem("hi_done"), sem("lo_done"), sem("piece_used")
        stream_full = [sem(f"stream_full{b}") for b in range(4)]
        stream_free = [sem(f"stream_free{b}") for b in range(4)]
        side_full = {b: sem(f"side_full_{b}") for b in "LR"}
        side_free = {b: sem(f"side_free_{b}") for b in "LR"}
        params_landed, mlp_landed, w_inner_landed = sem("params_landed"), sem("mlp_landed"), sem("w_inner_landed")
        x_landed = [sem(f"x_landed{g}") for g in range(4)]
        filter_dft_landed, dft_landed, decay_landed = sem("filter_dft_landed"), sem("dft_landed"), sem("decay_landed")
        w_filt_landed, skip_landed = sem("w_filt_landed"), sem("skip_landed")
        mem_landed = [sem(f"mem_landed{g}") for g in range(4)]
        x_again_landed = sem("x_again_landed")
        out_written = sem("out_written")
        zeroed, ident_made, made = sem("zeroed"), sem("ident_made"), sem("made")
        angle_step, sin_done = sem("angle_step"), sem("sin_done")
        squared, fold_step, folded_in = sem("squared"), sem("fold_step"), sem("folded_in")
        rms_ready, mem_scaled = sem("rms_ready"), sem("mem_scaled")
        a_hi_done, a_ready = sem("a_hi_done"), sem("a_ready")
        k_squared, k_summed, k_norm_ready = sem("k_squared"), sem("k_summed"), sem("k_norm_ready")
        k_folded, spec_done = sem("k_folded"), sem("spec_done")
        hidden_hi_done, hidden_lo_done = sem("hidden_hi_done"), sem("hidden_lo_done")
        w_filt_hi_done, w_filt_split = sem("w_filt_hi_done"), sem("w_filt_split")
        filter_dft_hi_done, filter_dft_split = sem("filter_dft_hi_done"), sem("filter_dft_split")
        folded_hi_done, folded_split = sem("folded_hi_done"), sem("folded_split")
        short_center, short_left, short_done = sem("short_center"), sem("short_left"), sem("short_done")
        product_step, product_done = sem("product_step"), sem("product_done")
        idft_landed, idft_hi_done, idft_split = sem("idft_landed"), sem("idft_hi_done"), sem("idft_split")
        spectrum_hi_done, spectrum_split = sem("spectrum_hi_done"), sem("spectrum_split")
        sigmoid_done, glu_gate_ready = sem("sigmoid_done"), sem("glu_gate_ready")
        mean_summed, squares_summed = sem("mean_summed"), sem("squares_summed")
        conf_center = sem("conf_center")
        conf_taps, tap_product, conf_taps_pool = sem("conf_taps"), sem("tap_product"), sem("conf_taps_pool")
        conf_squared, ln_step, conf_done = sem("conf_squared"), sem("ln_step"), sem("conf_done")
        memory_hi_done, q_hi_done, q_split, prob_t_hi_done = (
            sem("memory_hi_done"), sem("q_hi_done"), sem("q_split"), sem("prob_t_hi_done"))
        peak_done, shift_done = sem("peak_done"), sem("shift_done")
        inv_total_done, prob_ready, o_hi_done = sem("inv_total_done"), sem("prob_ready"), sem("o_hi_done")
        ffn_par_ready, gate_center, gate_left = sem("ffn_par_ready"), sem("gate_center"), sem("gate_left")
        gate_done, silu_done, silu_scaled = sem("gate_done"), sem("silu_done"), sem("silu_scaled")
        h_hi_done, h_ready = sem("h_hi_done"), sem("h_ready")
        down_full, down_added = sem("down_full"), sem("down_added")
        final_squares_used, y_gained, last_gained, y_done, y_done_pool = (
            sem("final_squares_used"), sem("y_gained"), sem("last_gained"), sem("y_done"), sem("y_done_pool"))

        block = ctx.enter_context(nc.Block())

        def norm_phase(n):
            return [(x_first, "g_mix", squares_x, 4, sum_x, "L", inv_rms),
                    (mem_x, "g_mem", squares_m, 1, sum_m, "R", inv_mem),
                    (x, "g_xattn", squares, 1, sum_sq, "R", inv_rms),
                    (x, "g_ffn", squares, 1, sum_sq, "R", inv_rms),
                    (x, "g_final", squares_y, 4, sum_sq, "L", inv_rms)][n]

        def per_tile(vector, n):
            return vector[:, :].rearrange("p (a s) -> p a s", a=1).to_broadcast([P, n, S])

        def pair(b):
            return side[:, 0:2, :] if b == "L" else side[:, 2:4, :]

        A_PHASE = [0, 1, 3, 4]
        A_NEXT = [0, K0, OUT0, Q0, O0]

        def group_free(m, g):
            return 8 * A_NEXT[m] - 8 + 2 * g + 2

        FFN_PIECE0 = 8 * PANELS
        DOWN_PIECE0 = FFN_PIECE0 + 16 * SLABS

        def tap_range(r):
            off = [j for j in range(TAPS) if j != TAPS // 2][r] - TAPS // 2
            return off, max(0, -off), S - max(0, off)

        @block.sync
        def _(sp):
            def panel_source(panel):
                if panel < 4:
                    kind, i = CONF_PANELS[panel]
                    return w_in, (CONF if kind == "gate" else 0) + i * HALF
                if panel < K0:
                    part, half = HYENA_PANELS[panel - 4]
                    return w_in, 2 * CONF + part * HY + half * HALF
                for w, first in ((w_k, K0), (w_v, V0), (w_out, OUT0), (w_q, Q0), (w_o, O0)):
                    if first <= panel < first + 4:
                        return w, (panel - first) * HALF

            def rows(w, r0, c0):
                return w[bass.ds(r0, 256), bass.ds(c0, HALF)].rearrange("(k p) n -> p k n", p=P)

            def load_piece(p, source):
                slot = p % RING
                sp.dma_start(raw[:, slot, :].rearrange("p (k n) -> p k n", k=2),
                             source).then_inc(raw_landed[slot], 16)

            sp.dma_start(feat[:, :], features).then_inc(mlp_landed, 16)
            sp.dma_start(w1_sb[:, :], w1).then_inc(mlp_landed, 16)
            sp.dma_start(par[:, :], params).then_inc(params_landed, 16)
            for s in range(SLOTS):
                f = (s - 1) // 3
                if s and (s - 1) % 3 == 0 and f < 4:
                    if f:
                        sp.wait_ge(w_filt_split, f)
                    half, order = f // 2, f % 2
                    w = w_filt.rearrange("k (o d c) -> k o d c", o=2, d=2)
                    for copy in range(2):
                        sp.dma_start(w_filt_sb[copy * MLP:(copy + 1) * MLP, :, :],
                                     w[:, order, :, half * HALF:(half + 1) * HALF]).then_inc(w_filt_landed, 16)
                if s in (2, 7):
                    if s == 7:
                        sp.wait_ge(side_free["R"], emptied("taps1", "R"))
                    sp.dma_start(decay_sb[:, :, :], decay[s // 7]).then_inc(decay_landed, 16)
                if s and (s - 1) % 3 == 2 and f < 4:
                    if f:
                        sp.wait_ge(spec_done, f)
                    half, order = f // 2, f % 2
                    sp.dma_start(skip_sb[:, :], skip[order:order + 1, half * HALF:(half + 1) * HALF]
                                 .to_broadcast([P, HALF])).then_inc(skip_landed, 16)
                if s == 3:
                    sp.dma_start(filter_dft_raw[:, :, :], filter_dft).then_inc(filter_dft_landed, 16)
                if s == 15:
                    sp.wait_ge(side_full["L"], filled("spec_im3", "L"))
                    sp.dma_start(dft_sb[:, :, :], dft).then_inc(dft_landed, 16)
                if s == 19:
                    sp.wait_ge(folded_in, 8)
                    sp.dma_start(idft_raw[:, :, :], idft).then_inc(idft_landed, 16)
                if s == 38:
                    sp.wait_ge(a_ready, 12)
                    sp.dma_start(x[:, :, :], x_t).then_inc(x_again_landed, 16)
                for p in range(4 * s, 4 * s + 4):
                    if s == 0:
                        sp.dma_start(x_first[:, 4 * p:4 * p + 4, :], x_t[:, 4 * p:4 * p + 4, :]).then_inc(x_landed[p], 16)
                    if p >= RING:
                        sp.wait_ge(lo_done, p - RING + 1)
                    if s == 15:
                        g = p % 4
                        sp.dma_start(mem_x[:, 4 * g:4 * g + 4, :], mem_t[:, 4 * g:4 * g + 4, :]).then_inc(mem_landed[g], 16)
                    w, c0 = panel_source(p // 8)
                    load_piece(p, rows(w, (p % 8) * 256, c0))
                    if p == 0:
                        sp.dma_start(w_inner_sb[:, 0:2, :], w_inner.rearrange("l k n -> k l n")).then_inc(w_inner_landed, 16)
                        sp.dma_start(w_inner_sb[:, 2, :], w_inner[1]).then_inc(w_inner_landed, 16)
            with sp.Fori(0, SLABS) as i:
                for j in range(16):
                    sp.wait_ge(lo_done, i * 16 + (FFN_PIECE0 + j - RING + 1))
                    load_piece(j, rows(w_up, (j % 8) * 256, i * HALF + (j // 8) * FF))
            with sp.Fori(0, SLABS) as g:
                for j in range(8):
                    sp.wait_ge(lo_done, g * 8 + (DOWN_PIECE0 + j - RING + 1))
                    load_piece(j, rows(w_down, g * 512 + (j % 2) * 256, (j // 2) * HALF))
            for g in (1, 2, 3, 0):
                if g == 0:
                    sp.wait_ge(y_done_pool, 1)
                else:
                    sp.wait_ge(y_done, g)
                sp.dma_start(out[:, 4 * g:4 * g + 4, :], y_out[:, 4 * g:4 * g + 4, :]).then_inc(out_written, 16)
            sp.wait_ge(out_written, 64)

        @block.gpsimd
        def _(pool):
            pool.memset(ident[:, :], 0.0).then_inc(zeroed, 1)
            pool.memset(ones[:, :], 1.0).then_inc(made, 1)
            pool.memset(hidden[:, :, 0:1], 0.0).then_inc(made, 1)
            pool.memset(eps[:, :], EPS).then_inc(made, 1)
            pool.wait_ge(zeroed, 1)
            pool.affine_select(out=ident[:, :], in_=ident[:, :], compare_op=ALU.not_equal, fill=1.0,
                               base=0, pattern=[[-1, P]], channel_multiplier=1).then_inc(ident_made, 1)
            steps = iter(range(1, 10 ** 6))

            def add(to, a, b, done=None):
                op = pool.tensor_tensor(to, a, b, ALU.add)
                if done is None:
                    op.then_inc(fold_step, 1)
                    pool.wait_ge(fold_step, next(steps))
                else:
                    op.then_inc(done, 1)

            def fold_squares(n, g):
                bufs, count, total_sq = norm_phase(n)[2], norm_phase(n)[3], norm_phase(n)[4]
                sq = bufs[:, g % count, :, :]
                pool.wait_ge(squared, 4 * n + g + 1)
                if g == 0 and n >= 3:
                    pool.wait_ge(side_full["R"], filled(f"stats{n - 1}", "R"))
                add(sq[:, 0:2, :], sq[:, 0:2, :], sq[:, 2:4, :])
                if g == 0:
                    add(total_sq[:, :], sq[:, 0, :], sq[:, 1, :], folded_in)
                else:
                    add(sq[:, 0, :], sq[:, 0, :], sq[:, 1, :])
                    pool.wait_ge(folded_in, 4 * n + g)
                    add(total_sq[:, :], total_sq[:, :], sq[:, 0, :], folded_in)

            def sum_filter(f):
                pool.wait_ge(k_squared, f + 1)
                sq = k_squares[f]
                add(sq[:, 0:2, :], sq[:, 0:2, :], sq[:, 2:4, :])
                add(sq[:, 0, :], sq[:, 0, :], sq[:, 1, :], k_summed)

            def scale_sigmoid(i):
                pool.wait_ge(sigmoid_done, i + 1)
                pool.tensor_tensor(sigm[:, :, :], sigm[:, :, :], per_tile(inv_rms, 4), ALU.mult).then_inc(glu_gate_ready, 1)

            def sum_channels(source, done):
                add(u[:, 0:4, :], source[:, 0:4, :], source[:, 4:8, :])
                add(u[:, 0:2, :], u[:, 0:2, :], u[:, 2:4, :])
                add(u[:, 0, :], u[:, 0, :], u[:, 1, :], done)

            for g in range(4):
                fold_squares(0, g)
            sum_filter(0)
            scale_sigmoid(0)
            sum_filter(1)
            scale_sigmoid(1)
            def taps_of_second(first, last):
                for r in range(first, last):
                    off, a, b = tap_range(r)
                    for c in range(4, 8):
                        if r == 0:
                            pool.wait_ge(conf_center, c + 1)
                        w = COL["conf_w"] + (off + TAPS // 2) * 8 + c
                        if r or c > 4:
                            pool.wait_ge(conf_taps_pool, 4 * r + c - 4)
                        pool.tensor_tensor(tapped[:, a:b], u[:, c, a + off:b + off],
                                           par[:, w:w + 1].to_broadcast([P, b - a]), ALU.mult).then_inc(tap_product, 1)
                        pool.wait_ge(tap_product, 4 * r + c - 3)
                        pool.tensor_tensor(conf[:, c, a:b], conf[:, c, a:b], tapped[:, a:b], ALU.add).then_inc(conf_taps_pool, 1)

            sum_filter(2)
            taps_of_second(0, 4)
            sum_filter(3)
            taps_of_second(4, 10)
            for g in range(4):
                fold_squares(1, g)
            pool.wait_ge(rms_ready, 2)
            for g in range(4):
                m = mem_x[:, 4 * g:4 * g + 4, :]
                pool.tensor_tensor(m, m, per_tile(inv_mem, 4), ALU.mult).then_inc(mem_scaled, 1)
            taps_of_second(10, TAPS - 1)
            pool.wait_ge(conf_taps_pool, 4 * (TAPS - 1))
            pool.wait_ge(conf_taps, 4 * (TAPS - 1))
            sum_channels(conf, mean_summed)
            pool.wait_ge(conf_squared, 1)
            sum_channels(u, squares_summed)
            for n in (2, 3):
                for g in range(4):
                    fold_squares(n, g)
            with pool.Fori(0, SLABS) as i:
                pool.wait_ge(silu_done, i + 1)
                pool.tensor_tensor(silu[:, :, :], silu[:, :, :], per_tile(inv_rms, 4), ALU.mult).then_inc(silu_scaled, 1)
            for g in range(3):
                fold_squares(4, g)
            pool.wait_ge(y_gained, 4)
            pool.wait_ge(rms_ready, 5)
            pool.tensor_tensor(y_out[:, 0:4, :], y_out[:, 0:4, :], per_tile(inv_rms, 4), ALU.mult).then_inc(y_done_pool, 1)

        @block.tensor
        def _(pe):
            def products(out_, wh, wl, ah, al, start, stop, shared):
                pe.matmul(out_, wh, ah, start=start, stop=False, skip_group_check=shared)
                pe.matmul(out_, wh, al, start=False, stop=False, skip_group_check=shared)
                return pe.matmul(out_, wl, ah, start=False, stop=stop, skip_group_check=shared)

            def half_panel(s):
                panel, first = s // 2, (s % 2) * 4
                banks = (panel % 2) * 2
                act_hi, act_lo = (b_hi, b_lo) if panel >= O0 else (a_hi, a_lo)
                if s % 2 == 0 and panel >= 2:
                    for b in (banks, banks + 1):
                        pe.wait_ge(stream_free[b], panel // 2)
                for j in range(first, first + 4):
                    phase = A_NEXT.index(panel) if panel in (0, K0, OUT0, Q0) else None
                    if phase is not None and j % 2 == 0:
                        pe.wait_ge(a_ready, 4 * phase + j // 2 + 1)
                    if panel == O0 and j % 2 == 0:
                        pe.wait_ge(side_free["L"], emptied(f"pv{j // 2}", "L"))
                    p = 8 * panel + j
                    pe.wait_ge(lo_done, p + 1)
                    piece(banks, p % RING, j, V0 <= panel < OUT0, act_hi, act_lo, 2 * j,
                          j == 0, j == 7)
                    side_product(s, j % 4)

            def piece(banks, slot, j, swapped, act_hi, act_lo, kt, first, last):
                if swapped:
                    for m in range(2):
                        for k in range(2):
                            a = bass.ts(m, P)
                            w = bass.ts(k, HALF)
                            mm = products(stream_bank(banks + m).rearrange("p a b -> p (a b)"),
                                          act_hi[:, kt + k, a], act_lo[:, kt + k, a],
                                          w_hi[:, slot, w], w_lo[:, slot, w],
                                          first and k == 0, last and k == 1, False)
                        if last and m == 0:
                            mm.then_inc(stream_full[banks], 1)
                    mm.then_inc(piece_used, 1)
                    return
                for t in range(4):
                    for k in range(2):
                        w = bass.ds(k * HALF + t * P, P)
                        mm = products(stream[:, banks + t // 2, t % 2, :],
                                      w_hi[:, slot, w], w_lo[:, slot, w],
                                      act_hi[:, kt + k, :], act_lo[:, kt + k, :],
                                      first and t % 2 == 0 and k == 0, last and k == 1, True)
                    if last and t == 1:
                        mm.then_inc(stream_full[banks], 1)
                mm.then_inc(piece_used, 1)

            def claim(name, pairs):
                for b in pairs:
                    if before(name, b):
                        pe.wait_ge(side_free[b], before(name, b))

            def statistics(n):
                b = norm_phase(n)[5]
                claim(f"stats{n}", b)
                pe.wait_ge(folded_in, 4 * n + 4)
                pe.matmul(pair(b)[:, 0, 0:S], ones[:, :], norm_phase(n)[4][:, :],
                          start=True, stop=True).then_inc(side_full[b], 1)

            def mlp_layer(layer):
                claim(f"mlp{layer}", "R")
                if layer == 0:
                    pe.wait_ge(mlp_landed, 32)
                    w, h = w1_sb[:, :], feat[:, :]
                else:
                    pe.wait_ge(w_inner_landed, 32)
                    pe.wait_ge(sin_done, layer)
                    w, h = w_inner_sb[:, layer - 1, :], hidden[0:MLP, (layer - 1) % 2, 1:S + 1]
                if layer == 2:
                    w = w_inner_sb[:, 1:3, :].rearrange("p a b -> p (a b)")
                pe.matmul(side[0:(P if layer == 2 else MLP), 2, 0:S], w, h, start=True, stop=True).then_inc(side_full["R"], 1)

            def filter_taps(f):
                claim(f"taps{f}", "LR")
                pe.wait_ge(w_filt_split, f + 1)
                if f == 0:
                    pe.wait_ge(hidden_lo_done, 1)
                for d in range(2):
                    for t in range(2):
                        h = bass.ds(1 - d + t * P, P)
                        pe.matmul(side[:, 2 * d + t, :], hidden_hl[:, h], w_filt_hi[:, d, :], start=True, stop=False)
                        mm = pe.matmul(side[:, 2 * d + t, :], hidden_hl[0:MLP, h], w_filt_lo[:, d, :], start=False, stop=True)
                    mm.then_inc(side_full["LR"[d]], 1)

            def filter_energy(f):
                claim(f"energy{f}", "L")
                pe.wait_ge(k_summed, f + 1)
                pe.matmul(side[:, 0, :], ones[:, :], k_squares[f][:, 0, :], start=True, stop=True).then_inc(side_full["L"], 1)

            def spectrum_tile(f, bank, column, part):
                for k in range(2):
                    c = bass.ts(column, P)
                    mm = products(side[:, bank, :], filter_dft_hi[:, k, c], filter_dft_lo[:, k, c],
                                  folded_hi[f][:, 2 * part + k, :], folded_lo[:, 2 * part + k, :],
                                  k == 0, k == 1, False)
                return mm

            def filter_spectrum(f):
                claim(f"spec{f}", "LR")
                if f == 0:
                    pe.wait_ge(filter_dft_split, 1)
                pe.wait_ge(folded_split, f + 1)
                spectrum_tile(f, 0, 0, 0)
                spectrum_tile(f, 1, 1, 0).then_inc(side_full["L"], 1)
                spectrum_tile(f, 2, 2, 0)
                spectrum_tile(f, 3, 3, 1).then_inc(side_full["R"], 1)

            def filter_spectrum_im(f):
                claim(f"spec_im{f}", "L")
                spectrum_tile(f, 0, 4, 1).then_inc(side_full["L"], 1)

            def turn(e):
                claim(f"turn{e}", "L")
                pe.wait_ge(short_done, 2 * (e + 1))
                for t in range(2):
                    for c in range(4):
                        mm = pe.transpose(side[:, t, bass.ts(c, P)], turned[:, c, bass.ts(t, P)], ident[:, :])
                mm.then_inc(side_full["L"], 1)

            def transform(c):
                claim(f"dft{c}", "LR")
                if c == 0:
                    pe.wait_ge(dft_landed, 16)
                order, half = c // 2, c % 2
                if order == 0:
                    pe.wait_ge(side_free["L"], emptied(f"turn{2 * half}", "L"))
                else:
                    pe.wait_ge(side_free["L"], emptied(f"idft{half}", "L"))
                source = (v_t, x1_t)[order]
                for j in range(4):
                    for k in range(2):
                        mm = pe.matmul(side[:, j, :], dft_sb[:, k, bass.ts(j, P)], source[:, half, k, :],
                                       start=(k == 0), stop=(k == 1))
                    if j % 2:
                        mm.then_inc(side_full["LR"[j // 2]], 1)

            def transform_back(c):
                claim(f"idft{c}", "L")
                if c == 0:
                    pe.wait_ge(idft_split, 2)
                pe.wait_ge(spectrum_split, c + 1)
                hi = spectrum_hi[c]
                if c < 2:
                    for t in range(2):
                        for k in range(4):
                            i = bass.ts(t, P)
                            mm = products(side[:, t, :], idft_hi[:, k, i], idft_lo[k // 2][:, k % 2, i],
                                          hi[:, k, :], spectrum_lo[:, k, :], k == 0, k == 3, False)
                else:
                    for t in range(4):
                        for k in range(4):
                            i = bass.ts(t, P)
                            mm = products(side[:, t // 2, bass.ts(t % 2, S)], hi[:, k, i], spectrum_lo[:, k, i],
                                          idft_hi[:, k, :], idft_lo[k // 2][:, k % 2, :], k == 0, k == 3, False)
                mm.then_inc(side_full["L"], 1)

            def channel_sum(name, summed):
                claim(name, "R")
                pe.wait_ge(summed, 1)
                pe.matmul(side[:, 2, 0:S], ones[:, :], u[:, 0, :], start=True, stop=True).then_inc(side_full["R"], 1)

            def scores(h):
                claim(f"scores{h}", "R")
                pe.wait_ge(q_split, h + 1)
                for t in range(2):
                    for k in range(4):
                        q_ = bass.ts(t, P)
                        mm = products(side[:, 2, bass.ts(t, S)], q_hi[:, k, q_], q_lo[:, k, q_],
                                      keys_hi[:, 4 * h + k, :], keys_lo[:, 4 * h + k, :], k == 0, k == 3, False)
                mm.then_inc(side_full["R"], 1)

            def turn_probs(h):
                claim(f"turn_p{h}", "L")
                pe.wait_ge(prob_ready, h + 1)
                for m in range(2):
                    for t in range(2):
                        mm = pe.transpose(side[:, 0, bass.ds(m * S + t * P, P)], prob[:, t, bass.ts(m, P)], ident[:, :])
                mm.then_inc(side_full["L"], 1)

            def attend(h):
                claim(f"pv{h}", "L")
                for t in range(4):
                    for m in range(2):
                        v = bass.ts(t, P)
                        mm = products(side[:, t // 2, bass.ts(t % 2, S)], values_hi[h][:, m, v], values_lo[h][:, m, v],
                                      prob_t_hi[:, m, :], prob_t_lo[:, m, :], m == 0, m == 1, False)
                mm.then_inc(side_full["L"], 1)

            def side_product(s, j):
                if (s, j) == (0, 0):
                    mlp_layer(1)
                if (s, j) == (0, 3):
                    mlp_layer(2)
                if (s, j) == (1, 1):
                    pe.wait_ge(made, 1)
                    statistics(0)
                if j == 3 and s in (1, 4, 7, 10):
                    filter_taps(s // 3)
                if j == 3 and s in (2, 5, 8, 11):
                    filter_energy(s // 3)
                if j == 3 and s in (3, 6, 9, 12):
                    filter_spectrum(s // 3 - 1)
                if (s, j) in TURNS:
                    if TURNS.index((s, j)) == 0:
                        pe.wait_ge(ident_made, 1)
                    turn(TURNS.index((s, j)))
                if (s, j) in SPEC_IM:
                    filter_spectrum_im(SPEC_IM.index((s, j)))
                if (s, j) == (17, 3):
                    statistics(1)
                if (s, j) in TRANSFORM_BACK:
                    transform_back(TRANSFORM_BACK.index((s, j)))
                if (s, j) in TRANSFORM:
                    transform(TRANSFORM.index((s, j)))
                if (s, j) == (32, 3):
                    channel_sum("mean", mean_summed)
                if (s, j) == (33, 3):
                    channel_sum("variance", squares_summed)
                if (s, j) == (44, 3):
                    statistics(2)
                if (s, j) in SCORES:
                    scores(SCORES.index((s, j)))
                if (s, j) in TURN_PROBS:
                    turn_probs(TURN_PROBS.index((s, j)))
                if (s, j) in ATTEND:
                    attend(ATTEND.index((s, j)))

            mlp_layer(0)
            for s in range(SLOTS):
                half_panel(s)

            def up_slab(i, first):
                for j in range(16):
                    if j % 8 == 0:
                        for b in (j // 4, j // 4 + 1):
                            pe.wait_ge(stream_free[b], i + PANELS // 2)
                    if first and j < 8 and j % 2 == 0:
                        pe.wait_ge(a_ready, 4 * 4 + j // 2 + 1)
                    pe.wait_ge(lo_done, i * 16 + (FFN_PIECE0 + j + 1))
                    piece((j // 8) * 2, j % RING, j % 8, False, a_hi, a_lo, 2 * (j % 8), j % 8 == 0, j % 8 == 7)
                    if first and j == 5:
                        statistics(3)

            up_slab(0, True)
            with pe.Fori(1, SLABS) as i:
                up_slab(i, False)

            def down_tile(panel, t):
                if panel < 2:
                    return side[:, 2 * panel + t // 2, bass.ts(t % 2, S)]
                return stream[:, 2 * (panel - 2) + t // 2, t % 2, :]

            def down_group(g, first, last):
                for j in range(8):
                    panel, half = j // 2, j % 2
                    if first and half == 0:
                        if panel < 2:
                            b = "LR"[panel]
                            pe.wait_ge(side_free[b], SIDE_FREE_END[b])
                        else:
                            for b in (2 * (panel - 2), 2 * (panel - 2) + 1):
                                pe.wait_ge(stream_free[b], PANELS // 2 + SLABS)
                    pe.wait_ge(lo_done, g * 8 + (DOWN_PIECE0 + j + 1))
                    for t in range(4):
                        for k in range(2):
                            w = bass.ds(k * HALF + t * P, P)
                            kt = g * 4 + (2 * half + k)
                            mm = products(down_tile(panel, t), w_hi[:, j % RING, w], w_lo[:, j % RING, w],
                                          h_hi[:, bass.ds(kt, 1), :].rearrange("p a b -> p (a b)"),
                                          h_lo[:, bass.ds(kt, 1), :].rearrange("p a b -> p (a b)"),
                                          first and half == 0 and t % 2 == 0 and k == 0,
                                          last and half == 1 and k == 1, True)
                        if last and half == 1 and t == 1:
                            mm.then_inc(down_full, 1)
                    mm.then_inc(piece_used, 1)

            pe.wait_ge(h_ready, SLABS - 1)
            down_group(0, True, False)
            with pe.Fori(1, SLABS - 1) as g:
                down_group(g, False, False)
            pe.wait_ge(h_ready, SLABS)
            down_group(SLABS - 1, False, True)
            pe.wait_ge(down_added, 2)
            for b in range(2):
                pe.wait_ge(squared, 4 * 4 + 4 + b)
                for j in (2 * b, 2 * b + 1):
                    pe.matmul(side[:, 0, 0:S], ones[:, :], squares_y[:, 3, j, :], start=(j == 0), stop=False)
            pe.wait_ge(folded_in, 4 * 4 + 3)
            mm = pe.matmul(side[:, 0, 0:S], ones[:, :], sum_sq[:, :], start=False, stop=True)
            mm.then_inc(final_squares_used, 1)

        def memory_bank(panel, b, keys, values):
            if panel < V0:
                i = 4 * (panel - K0) + 2 * b
                return keys[:, i:i + 2, :]
            return values[panel - V0][:, b, :].rearrange("p (a s) -> p a s", a=2)

        def wait_bank(eng, panel, b):
            if b == 0:
                eng.wait_ge(stream_full[(panel % 2) * 2], panel // 2 + 1)
            else:
                eng.wait_ge(piece_used, 8 * panel + 8)

        @block.scalar
        def _(act):
            def split_piece(p):
                act.wait_ge(raw_landed[p % RING], 16 * (p // RING + 1))
                if p >= RING:
                    act.wait_ge(piece_used, p - RING + 1)
                act.activation(w_hi[:, p % RING, :], raw[:, p % RING, :], ACT.Copy).then_inc(hi_done, 1)

            def memory_hi(panel):
                for b in range(2):
                    wait_bank(act, panel, b)
                    act.activation(memory_bank(panel, b, keys_hi, values_hi), stream_bank((panel % 2) * 2 + b), ACT.Copy).then_inc(memory_hi_done, 1)

            def square(n, g):
                source, _, bufs, count, _, _, _ = norm_phase(n)
                if n == 1:
                    act.wait_ge(mem_landed[g], 16)
                if g >= count:
                    act.wait_ge(folded_in, 4 * n + g + 1 - count)
                act.activation(bufs[:, g % count, :, :], source[:, 4 * g:4 * g + 4, :], ACT.Square).then_inc(squared, 1)

            def rms_root(n):
                b = norm_phase(n)[5]
                act.wait_ge(side_full[b], filled(f"stats{n}", b))
                act.activation(root[:, :], pair(b)[:, 0, 0:S], ACT.Sqrt, bias=eps[:, 0:1],
                               scale=1.0 / D).then_inc(side_free[b], 1)

            def gain_hi(n, g):
                m = A_PHASE[n]
                if m:
                    act.wait_ge(piece_used, group_free(m, g))
                for j in range(4 * g, 4 * g + 4):
                    act.activation(a_hi[:, j, :], norm_phase(n)[0][:, j, :], ACT.Identity,
                                   scale=column(norm_phase(n)[1], j)).then_inc(a_hi_done, 1)

            def mix_hi(g):
                act.wait_ge(piece_used, group_free(2, g))
                source = conf[:, 4 * g:4 * g + 4, :] if g < 2 else x2[:, 4 * g - 8:4 * g - 4, :]
                act.activation(a_hi[:, 4 * g:4 * g + 4, :], source, ACT.Copy).then_inc(a_hi_done, 4)

            def column(name, i):
                return par[:, COL[name] + i:COL[name] + i + 1]

            def short_centers(e):
                part, half = HYENA_PANELS[e]
                if 1 <= e < 4:
                    act.wait_ge(side_full["L"], filled(f"turn{e - 1}", "L"))
                for t in range(4):
                    if t % 2 == 0:
                        act.wait_ge(stream_free[((4 + e) % 2) * 2 + t // 2], (4 + e) // 2 + 1)
                    c = part * 8 + half * 4 + t
                    to = x2[:, 4 * half + t, :] if part == 2 else turned[:, t, :]
                    act.activation(to, proj[:, t, :], ACT.Identity,
                                   bias=column("short_b", c), scale=column("short_w", 24 + c)).then_inc(short_center, 1)

            def evacuate_turned(e):
                part, half = HYENA_PANELS[e]
                act.wait_ge(side_full["L"], filled(f"turn{e}", "L"))
                act.activation((v_t, x1_t)[part][:, half, :, :], pair("L"), ACT.Copy).then_inc(side_free["L"], 1)

            def filter_square(f):
                act.wait_ge(side_free["R"], emptied(f"taps{f}", "R"))
                if f:
                    act.wait_ge(side_full["L"], filled(f"spec_im{f - 1}", "L"))
                act.activation(k_squares[f][:, :, :], taps[:, :, :], ACT.Square).then_inc(k_squared, 1)

            def filter_root(f):
                act.wait_ge(side_full["L"], filled(f"energy{f}", "L"))
                if f:
                    act.wait_ge(spec_done, f)
                act.activation(k_norm[:, :], side[:, 0, :], ACT.Sqrt, bias=eps[:, 0:1]).then_inc(side_free["L"], 1)

            def conf_centers(i):
                for b in range(2):
                    act.wait_ge(stream_free[2 + b], i + 1)
                for t in range(4 * i, 4 * i + 4):
                    act.activation(conf[:, t, :], u[:, t, :], ACT.Identity, bias=column("conf_b", t),
                                   scale=column("conf_w", (TAPS // 2) * 8 + t)).then_inc(conf_center, 1)

            def softmax(h):
                act.wait_ge(shift_done, h + 1)
                if h:
                    act.wait_ge(side_full["L"], filled(f"turn_p{h - 1}", "L"))
                for t in range(2):
                    e = act.activation(prob[:, t, :], side[:, 2, bass.ts(t, S)], ACT.Exp, bias=shift[:, t:t + 1],
                                       scale=SM_SCALE, accum_out=total[:, t:t + 1])
                e.then_inc(side_free["R"], 1)

            def evacuate_probs(h):
                act.wait_ge(side_full["L"], filled(f"turn_p{h}", "L"))
                act.activation(prob_t_hi[:, :, :], side[:, 0, :].rearrange("p (a b) -> p a b", a=2),
                               ACT.Copy).then_inc(prob_t_hi_done, 1)

            def split_head(h):
                act.wait_ge(side_full["L"], filled(f"pv{h}", "L"))
                act.activation(b_hi[:, 4 * h:4 * h + 4, :], pair("L").rearrange("p a (t s) -> p (a t) s", t=2),
                               ACT.Copy).then_inc(o_hi_done, 1)

            def sine(layer):
                act.wait_ge(angle_step, 5 * (layer + 1))
                n = P if layer == 2 else MLP
                act.activation(hidden[0:n, layer % 2, 1:S + 1], angle[0:n, :], ACT.Sin).then_inc(sin_done, 1)
                if layer == 2:
                    act.wait_ge(sin_done, 3)
                    act.activation(hidden_hl[:, :], hidden[:, 0, 0:S + 1], ACT.Copy).then_inc(hidden_hi_done, 1)

            def filter_weights_hi(f):
                act.wait_ge(w_filt_landed, 32 * (f + 1))
                if f == 0:
                    act.wait_ge(folded_in, 4)
                else:
                    act.wait_ge(side_full["R"], filled(f"taps{f - 1}", "R"))
                act.activation(w_filt_hi[:, :, :], w_filt_sb[:, :, :], ACT.Copy).then_inc(w_filt_hi_done, 1)

            def filter_folded_hi(f):
                act.wait_ge(side_full["L"], filled(f"energy{f}", "L"))
                act.wait_ge(k_folded, 2 * f + 2)
                act.activation(folded_hi[f][:, :, :], folded[:, :, :], ACT.Copy).then_inc(folded_hi_done, 1)

            act.wait_ge(made, 3)
            act.activation(warm[:, 0:1], eps[:, :], ACT.Sin)
            act.wait_ge(params_landed, 16)
            for p in range(4):
                act.wait_ge(x_landed[p], 16)
                gain_hi(0, p)
                split_piece(p)
                if p == 0:
                    sine(0)
            for g in range(4):
                square(0, g)
            for s in range(SLOTS):
                for j in range(4):
                    split_piece(4 * s + 4 + j)
                    if (s, j) in ((0, 0), (1, 0)):
                        sine(1 + s)
                    if (s, j) == (1, 1):
                        rms_root(0)
                    if j == 1 and s in (2, 6):
                        i = s // 4
                        for b in range(2):
                            act.wait_ge(stream_free[b], i + 1)
                        act.activation(sigm[:, :, :], sigm[:, :, :], ACT.Sigmoid).then_inc(sigmoid_done, 1)
                    if (s, j) == (2, 2):
                        act.wait_ge(filter_dft_landed, 16)
                        act.activation(filter_dft_hi[:, :, :], filter_dft_raw[:, :, :], ACT.Copy).then_inc(filter_dft_hi_done, 1)
                    if j == 1 and s in (1, 4, 7, 10):
                        filter_weights_hi(s // 3)
                    if j == 3 and s in (2, 5, 8, 11):
                        filter_root(s // 3)
                    if j == 0 and s in (3, 6, 9, 12):
                        filter_folded_hi(s // 3 - 1)
                    if j == 1 and s in (4, 8):
                        conf_centers(s // 4 - 1)
                    if (s, j) == (19, 3):
                        act.wait_ge(idft_landed, 16)
                        act.activation(idft_hi[:, :, :], idft_raw[:, :, :], ACT.Copy).then_inc(idft_hi_done, 1)
                    if (s, j) in PRODUCT_HI:
                        c = PRODUCT_HI.index((s, j))
                        act.wait_ge(product_done, 2 * c + 2)
                        act.activation(spectrum_hi[c][:, :, :], spectrum[:, :, :], ACT.Copy).then_inc(spectrum_hi_done, 1)
                    if (s, j) in TURNS:
                        evacuate_turned(TURNS.index((s, j)))
                    if (s, j) in SHORT:
                        short_centers(SHORT.index((s, j)))
                    if s in (15, 16) and j == 1:
                        if s == 15:
                            act.wait_ge(spec_done, 4)
                        square(1, 2 * s - 30)
                    if s in (18, 19) and j in (1, 3):
                        g = 2 * (s - 18) + j // 2
                        act.wait_ge(mem_scaled, g + 1)
                        gain_hi(1, g)
                    if (s, j) == (34, 0):
                        for t in range(8):
                            if t % 4 == 0:
                                act.wait_ge(ln_step, 2 + t // 4)
                            act.activation(conf[:, t, :], conf[:, t, :], ACT.Silu, bias=column("ln_b", t),
                                           scale=column("ln_g", t)).then_inc(conf_done, 1)
                    if s in (34, 35) and j in (1, 3):
                        if j == 1:
                            if s == 34:
                                act.wait_ge(conf_done, 8)
                            else:
                                act.wait_ge(side_free["L"], emptied("idft3", "L"))
                        mix_hi(2 * (s - 34) + j // 2)
                    if (s, j) in ((42, 1), (42, 3), (43, 1)):
                        gain_hi(2, 2 * (s - 42) + j // 2)
                    if (s, j) in SCORES:
                        softmax(SCORES.index((s, j)))
                    if (s, j) in TURN_PROBS:
                        evacuate_probs(TURN_PROBS.index((s, j)))
                    if (s, j) in ATTEND:
                        split_head(ATTEND.index((s, j)))
                if 1 <= s < 13 and s % 3 == 1:
                    filter_square(s // 3)
                if s in (15, 16):
                    square(1, 2 * s - 29)
                if s == 17:
                    rms_root(1)
                if s in (21, 23, 25, 27, 29, 31, 33, 35):
                    memory_hi(s // 2)
                if s == 32:
                    act.wait_ge(side_free["R"], emptied("mean", "R"))
                    act.activation(u[:, :, :], conf[:, :, :], ACT.Square).then_inc(conf_squared, 1)
                if s == 33:
                    act.wait_ge(side_full["R"], filled("variance", "R"))
                    act.activation(root[:, :], side[:, 2, 0:S], ACT.Sqrt, bias=eps[:, 0:1], scale=1.0 / CONF).then_inc(side_free["R"], 1)
                if s in (37, 39, 41, 43, 53, 55, 57, 59):
                    g = (s - 37) // 2 % 4
                    n = 2 if s < 44 else 3
                    for b in range(2):
                        panel = s // 2
                        act.wait_ge(stream_free[(panel % 2) * 2 + b], panel // 2 + 1)
                    if n == 3 or g == 3:
                        gain_hi(n, g)
                    square(n, g)
                if s == 44:
                    rms_root(2)
                if s in (45, 47, 49, 51):
                    h = (s - 45) // 2
                    for b in range(2):
                        act.wait_ge(stream_free[((Q0 + h) % 2) * 2 + b], (Q0 + h) // 2 + 1)
                    act.activation(q_hi[:, :, :], q[:, :, :], ACT.Copy).then_inc(q_hi_done, 1)
            def up_slab(i, first):
                for j in range(4, 20):
                    act.wait_ge(raw_landed[j % RING], i * 64 + 16 * ((FFN_PIECE0 + j) // RING + 1))
                    act.wait_ge(piece_used, i * 16 + (FFN_PIECE0 + j - RING + 1))
                    act.activation(w_hi[:, j % RING, :], raw[:, j % RING, :], ACT.Copy).then_inc(hi_done, 1)
                    if first and j == 10:
                        rms_root(3)
                    if j == 12:
                        act.wait_ge(ffn_par_ready, i + 1)
                        act.wait_ge(hi_done, i * 16 + (FFN_PIECE0 + j + 1))
                        for t in range(4):
                            if t % 2 == 0:
                                act.wait_ge(stream_free[t // 2], i + (PANELS // 2 + 1))
                            act.activation(gate[:, t, :], gate_in[:, t, :], ACT.Identity,
                                           bias=ffn_par[:, 12 + t:13 + t], scale=ffn_par[:, 4 + t:5 + t]).then_inc(gate_center, 1)
                    if j == 14:
                        act.wait_ge(gate_done, i + 1)
                        act.wait_ge(stream_free[3], i + PANELS // 2)
                        act.activation(silu[:, :, :], gate[:, :, :], ACT.Silu).then_inc(silu_done, 1)
                act.wait_ge(stream_free[3], i + (PANELS // 2 + 1))
                act.activation(h_hi[:, bass.ds(i * 4, 4), :], hv[:, :, :], ACT.Copy).then_inc(h_hi_done, 1)

            up_slab(0, True)
            with act.Fori(1, SLABS) as i:
                up_slab(i, False)
            def split_down(g, first, last):
                for j in range(first, last):
                    act.wait_ge(raw_landed[j % RING], g * 32 + 16 * ((DOWN_PIECE0 + j) // RING + 1))
                    act.wait_ge(piece_used, g * 8 + (DOWN_PIECE0 + j - RING + 1))
                    act.activation(w_hi[:, j % RING, :], raw[:, j % RING, :], ACT.Copy).then_inc(hi_done, 1)

            with act.Fori(0, SLABS - 1) as g:
                split_down(g, 4, 12)

            def square_panel(g):
                act.wait_ge(down_added, 2 * g + 2)
                square(4, g)

            def gain(g):
                for j in range(4 * g, 4 * g + 4):
                    act.activation(y_out[:, j, :], x[:, j, :], ACT.Identity, scale=column("g_final", j)).then_inc(y_gained, 1)

            split_down(SLABS - 1, 4, 6)
            square_panel(0)
            split_down(SLABS - 1, 6, 8)
            act.activation(warm[:, 1:2], eps[:, :], ACT.Sqrt)
            square_panel(1)
            gain(0)
            square_panel(2)
            gain(1)
            for b in range(2):
                act.wait_ge(down_added, 7 + b)
                act.activation(squares_y[:, 3, 2 * b:2 * b + 2, :], x[:, 12 + 2 * b:14 + 2 * b, :], ACT.Square).then_inc(squared, 1)
            gain(2)
            act.wait_ge(final_squares_used, 1)
            act.activation(root[:, :], side[:, 0, 0:S], ACT.Sqrt, bias=eps[:, 0:1], scale=1.0 / D).then_inc(side_free["L"], 1)

        @block.vector
        def _(dve):
            def taps_of_first(r):
                off, a, b = tap_range(r)
                for c in range(4):
                    if r == 0:
                        dve.wait_ge(conf_center, c + 1)
                    else:
                        dve.wait_ge(conf_taps, 4 * (r - 1) + c + 1)
                    w = COL["conf_w"] + (off + TAPS // 2) * 8 + c
                    dve.scalar_tensor_tensor(out=conf[:, c, a:b], in0=u[:, c, a + off:b + off],
                                             scalar=par[:, w:w + 1], in1=conf[:, c, a:b],
                                             op0=ALU.mult, op1=ALU.add).then_inc(conf_taps, 1)

            def split_piece(p):
                dve.wait_ge(hi_done, p + 1)
                dve.tensor_tensor(w_lo[:, p % RING, :], raw[:, p % RING, :],
                                  w_hi[:, p % RING, :].bitcast(F32), ALU.subtract).then_inc(lo_done, 1)

            def rms_inverse(n):
                b = norm_phase(n)[5]
                dve.wait_ge(side_free[b], emptied(f"stats{n}", b) if n < 4 else SIDE_FREE_END["L"] + 1)
                dve.reciprocal(norm_phase(n)[6][:, :], root[:, :]).then_inc(rms_ready, 1)
                dve.wait_ge(rms_ready, n + 1)

            def gain_lo(n, g):
                for j in range(4 * g, 4 * g + 4):
                    dve.wait_ge(a_hi_done, KT * A_PHASE[n] + j + 1)
                    c = COL[norm_phase(n)[1]] + j
                    op = dve.scalar_tensor_tensor(out=a_lo[:, j, :], in0=norm_phase(n)[0][:, j, :],
                                                  scalar=par[:, c:c + 1], in1=a_hi[:, j, :].bitcast(F32),
                                                  op0=ALU.mult, op1=ALU.subtract)
                op.then_inc(a_ready, 1)

            def mix_lo(g):
                source = conf[:, 4 * g:4 * g + 4, :] if g < 2 else x2[:, 4 * g - 8:4 * g - 4, :]
                dve.wait_ge(a_hi_done, KT * 2 + 4 * g + 4)
                dve.tensor_tensor(a_lo[:, 4 * g:4 * g + 4, :], source,
                                  a_hi[:, 4 * g:4 * g + 4, :].bitcast(F32), ALU.subtract).then_inc(a_ready, 1)

            def normalise(panel, b, to):
                bank = (panel % 2) * 2 + b
                wait_bank(dve, panel, b)
                dve.tensor_tensor(to, stream_bank(bank), per_tile(inv_rms, 2), ALU.mult).then_inc(stream_free[bank], 1)

            def add_panel(panel, i):
                for b in range(2):
                    bank = (panel % 2) * 2 + b
                    wait_bank(dve, panel, b)
                    rows = x[:, 4 * i + 2 * b:4 * i + 2 * b + 2, :]
                    dve.tensor_tensor(rows, stream_bank(bank), rows, ALU.add).then_inc(stream_free[bank], 1)

            def short_input(e):
                if e:
                    dve.wait_ge(short_done, 2 * e)
                for b in range(2):
                    normalise(4 + e, b, proj[:, 2 * b:2 * b + 2, :])

            def short_side(e, side_):
                part, half = HYENA_PANELS[e]
                for t in range(4):
                    to = x2[:, 4 * half + t, :] if part == 2 else turned[:, t, :]
                    c = COL["short_w"] + 48 * side_ + part * 8 + half * 4 + t
                    o, i_ = ((1, S), (0, S - 1)) if side_ == 0 else ((0, S - 1), (1, S))
                    if side_ == 0:
                        dve.wait_ge(short_center, 4 * e + t + 1)
                    else:
                        dve.wait_ge(short_left, 4 * e + t + 1)
                    op = dve.scalar_tensor_tensor(out=to[:, o[0]:o[1]], in0=proj[:, t, i_[0]:i_[1]],
                                                  scalar=par[:, c:c + 1], in1=to[:, o[0]:o[1]],
                                                  op0=ALU.mult, op1=ALU.add)
                    if side_ == 0:
                        op.then_inc(short_left, 1)
                    elif t % 2:
                        op.then_inc(short_done, 1)

            def filter_window(f):
                if f == 0:
                    dve.wait_ge(a_ready, 4)
                if f % 2 == 0:
                    dve.wait_ge(decay_landed, 16 * (f // 2 + 1))
                if f:
                    dve.wait_ge(k_folded, 2 * f)
                for d in range(2):
                    dve.wait_ge(side_full["LR"[d]], filled(f"taps{f}", "LR"[d]))
                    dve.tensor_tensor(taps[:, 2 * d:2 * d + 2, :], side[:, 2 * d:2 * d + 2, :],
                                      decay_sb[:, 2 * d:2 * d + 2, :], ALU.mult).then_inc(side_free["LR"[d]], 1)

            def filter_fold(f):
                dve.wait_ge(side_free["R"], emptied(f"taps{f}", "R"))
                if f:
                    dve.wait_ge(side_full["L"], filled(f"spec_im{f - 1}", "L"))
                dve.tensor_tensor(folded[:, 0:2, :], taps[:, 0:2, :], taps[:, 2:4, :], ALU.add).then_inc(k_folded, 1)
                dve.tensor_tensor(folded[:, 2:4, :], taps[:, 0:2, :], taps[:, 2:4, :], ALU.subtract).then_inc(k_folded, 1)

            def filter_norm(f):
                dve.wait_ge(side_free["L"], emptied(f"energy{f}", "L"))
                dve.reciprocal(k_norm[:, :], k_norm[:, :]).then_inc(k_norm_ready, 1)

            def filter_finish(f):
                to = spec[f % 2]
                half = f // 2
                dve.wait_ge(k_norm_ready, f + 1)
                dve.wait_ge(side_full["L"], filled(f"spec{f}", "L"))
                norm2 = k_norm[:, :].rearrange("p (a n) -> p a n", a=1).to_broadcast([P, 2, HALF])
                dve.tensor_tensor(to[:, half, 0:2, :], pair("L"), norm2, ALU.mult).then_inc(side_free["L"], 1)
                dve.wait_ge(side_full["R"], filled(f"spec{f}", "R"))
                dve.tensor_tensor(to[:, half, 2:4, :], pair("R"), norm2, ALU.mult).then_inc(side_free["R"], 1)

            def filter_finish_im(f):
                to = spec[f % 2]
                half = f // 2
                dve.wait_ge(side_full["L"], filled(f"spec_im{f}", "L"))
                dve.tensor_tensor(to[:, half, 4, :], side[:, 0, :], k_norm[:, :], ALU.mult).then_inc(side_free["L"], 1)
                dve.wait_ge(skip_landed, 16 * (f + 1))
                dve.wait_ge(side_free["L"], emptied(f"spec_im{f}", "L"))
                skip3 = skip_sb[:, :].rearrange("p (a n) -> p a n", a=1).to_broadcast([P, 3, HALF])
                dve.tensor_tensor(to[:, half, 0:3, :], to[:, half, 0:3, :], skip3, ALU.add).then_inc(spec_done, 1)

            def multiply(c, part):
                order, half = c // 2, c % 2
                k = spec[order]
                real, real_nyq = [k[:, half, 0, :], k[:, half, 1, :]], [k[:, half, 2, :], k[:, half, 1, :]]
                if part == 0:
                    if c == 0:
                        dve.wait_ge(short_done, 12)
                        dve.wait_ge(idft_split, 2)
                    dve.wait_ge(side_full["L"], filled(f"dft{c}", "L"))
                    dve.tensor_tensor(spectrum[:, 0:2, :], pair("L"), k[:, half, 0:2, :], ALU.mult)
                    dve.tensor_tensor(spectrum[:, 2:4, :], pair("L"), k[:, half, 3:5, :], ALU.mult).then_inc(side_free["L"], 1)
                if part == 1:
                    dve.wait_ge(side_full["R"], filled(f"dft{c}", "R"))
                    if c:
                        dve.wait_ge(product_done, 2 * c)
                    dve.tensor_tensor(cross[:, :, :], pair("R"), k[:, half, 3:5, :], ALU.mult).then_inc(product_step, 1)
                    dve.wait_ge(product_step, 2 * c + 1)
                    dve.tensor_tensor(spectrum[:, 0:2, :], spectrum[:, 0:2, :], cross[:, :, :], ALU.subtract).then_inc(product_done, 1)
                if part == 2:
                    dve.wait_ge(product_done, 2 * c + 1)
                    dve.tensor_tensor(cross[:, 0, :], side[:, 2, :], real_nyq[0], ALU.mult).then_inc(product_step, 1)
                    dve.tensor_tensor(cross[:, 1, :], side[:, 3, :], real_nyq[1], ALU.mult).then_inc(side_free["R"], 1)
                    dve.wait_ge(side_free["R"], emptied(f"dft{c}", "R"))
                    dve.tensor_tensor(spectrum[:, 2:4, :], spectrum[:, 2:4, :], cross[:, :, :], ALU.add).then_inc(product_done, 1)

            def gate_by(c):
                dve.wait_ge(side_full["L"], filled(f"idft{c}", "L"))
                half = c % 2
                if c < 2:
                    to = x1_t[:, half, :, :]
                    dve.wait_ge(side_free["L"], emptied(f"turn{2 * half + 1}", "L"))
                    dve.tensor_tensor(to, pair("L"), to, ALU.mult).then_inc(side_free["L"], 1)
                else:
                    to = x2[:, 4 * half:4 * half + 4, :]
                    dve.tensor_tensor(to, pair("L").rearrange("p a (t s) -> p (a t) s", t=2), to,
                                      ALU.mult).then_inc(side_free["L"], 1)

            def softmax_shift(h):
                dve.wait_ge(side_full["R"], filled(f"scores{h}", "R"))
                dve.tensor_reduce(peak[:, :], side[:, 2, :].rearrange("p (a s) -> p a s", a=2), AX_X,
                                  ALU.max).then_inc(peak_done, 1)
                dve.wait_ge(peak_done, h + 1)
                dve.tensor_scalar(shift[:, :], peak[:, :], -SM_SCALE, None, ALU.mult).then_inc(shift_done, 1)

            def softmax_norm(h):
                dve.wait_ge(side_free["R"], emptied(f"scores{h}", "R"))
                dve.reciprocal(inv_total[:, :], total[:, :]).then_inc(inv_total_done, 1)
                dve.wait_ge(inv_total_done, h + 1)
                for t in range(2):
                    op = dve.tensor_scalar(prob[:, t, :], prob[:, t, :], inv_total[:, t:t + 1], None, ALU.mult)
                op.then_inc(prob_ready, 1)

            def split_head(h):
                dve.wait_ge(o_hi_done, h + 1)
                dve.tensor_tensor(b_lo[:, 4 * h:4 * h + 4, :], pair("L").rearrange("p a (t s) -> p (a t) s", t=2),
                                  b_hi[:, 4 * h:4 * h + 4, :].bitcast(F32), ALU.subtract).then_inc(side_free["L"], 1)

            magic = 1.5 * 2.0 ** 23
            two_pi_hi = 6.28125
            two_pi_lo = 2 * np.pi - two_pi_hi
            def mlp_angle(layer):
                dve.wait_ge(side_full["R"], filled(f"mlp{layer}", "R"))
                if layer == 0:
                    dve.wait_ge(params_landed, 16)
                else:
                    dve.wait_ge(sin_done, layer)
                b = COL["mlp_b"] + layer
                n = P if layer == 2 else MLP
                a, t = angle[0:n, :], turns[0:n, :]
                dve.tensor_scalar(a, side[0:n, 2, 0:S], par[0:n, b:b + 1],
                                  par[0:n, COL["freq"]:COL["freq"] + 1], ALU.add, ALU.mult).then_inc(side_free["R"], 1)
                dve.wait_ge(side_free["R"], emptied(f"mlp{layer}", "R"))
                dve.tensor_scalar(t, a, 1.0 / (2 * np.pi), magic, ALU.mult, ALU.add).then_inc(angle_step, 1)
                dve.wait_ge(angle_step, 5 * layer + 1)
                dve.tensor_scalar(t, t, -magic, None, ALU.add).then_inc(angle_step, 1)
                dve.wait_ge(angle_step, 5 * layer + 2)
                dve.scalar_tensor_tensor(out=a, in0=t, scalar=-two_pi_hi, in1=a, op0=ALU.mult, op1=ALU.add).then_inc(angle_step, 1)
                dve.wait_ge(angle_step, 5 * layer + 3)
                dve.scalar_tensor_tensor(out=a, in0=t, scalar=-two_pi_lo, in1=a, op0=ALU.mult, op1=ALU.add).then_inc(angle_step, 1)
                dve.wait_ge(angle_step, 5 * layer + 4)
                dve.tensor_scalar(a, a, PI_BELOW, -PI_BELOW, ALU.min, ALU.max).then_inc(angle_step, 1)

            def memory_lo(panel):
                for b in range(2):
                    bank = (panel % 2) * 2 + b
                    dve.wait_ge(memory_hi_done, 2 * (panel - K0) + b + 1)
                    dve.tensor_tensor(memory_bank(panel, b, keys_lo, values_lo), stream_bank(bank),
                                      memory_bank(panel, b, keys_hi, values_hi).bitcast(F32),
                                      ALU.subtract).then_inc(stream_free[bank], 1)

            def filter_weights_lo(f):
                dve.wait_ge(w_filt_hi_done, f + 1)
                dve.tensor_tensor(w_filt_lo[:, :, :], w_filt_sb[0:MLP, :, :], w_filt_hi[0:MLP, :, :].bitcast(F32),
                                  ALU.subtract).then_inc(w_filt_split, 1)

            def filter_folded_lo(f):
                dve.wait_ge(folded_hi_done, f + 1)
                dve.tensor_tensor(folded_lo[:, :, :], folded[:, :, :], folded_hi[f][:, :, :].bitcast(F32),
                                  ALU.subtract).then_inc(folded_split, 1)

            mlp_angle(0)
            for p in range(4):
                dve.wait_ge(x_landed[p], 16)
                gain_lo(0, p)
                split_piece(p)
            mlp_angle(1)
            for s in range(SLOTS):
                for j in range(4):
                    split_piece(4 * s + 4 + j)
                    if (s, j) in FIRST_TAPS:
                        taps_of_first(FIRST_TAPS.index((s, j)))
                    if (s, j) == (0, 3):
                        mlp_angle(2)
                    if (s, j) == (1, 1):
                        dve.wait_ge(hidden_hi_done, 1)
                        lo = hidden_hl[MLP:P, :]
                        dve.tensor_tensor(lo, hidden[MLP:P, 0, 0:S + 1], lo.bitcast(F32), ALU.subtract).then_inc(hidden_lo_done, 1)
                    if (s, j) == (2, 2):
                        dve.wait_ge(filter_dft_hi_done, 1)
                        dve.tensor_tensor(filter_dft_lo[:, :, :], filter_dft_raw[:, :, :],
                                          filter_dft_hi[:, :, :].bitcast(F32), ALU.subtract).then_inc(filter_dft_split, 1)
                    if j == 1 and s in (1, 4, 7, 10):
                        filter_weights_lo(s // 3)
                    if j == 0 and s in (2, 5, 8, 11):
                        filter_fold(s // 3)
                    if s in (3, 6, 9, 12):
                        if j == 1:
                            filter_folded_lo(s // 3 - 1)
                        if j == 2:
                            filter_norm(s // 3 - 1)
                    if (s, j) == (1, 2):
                        rms_inverse(0)
                    if (s, j) in SPEC_IM:
                        filter_finish_im(SPEC_IM.index((s, j)))
                    for side_ in range(2):
                        if (s, j - 1 - side_) in SHORT:
                            short_side(SHORT.index((s, j - 1 - side_)), side_)
                    if (s, j) in TRANSFORM_BACK:
                        gate_by(TRANSFORM_BACK.index((s, j)))
                    if (s, j) == (20, 0):
                        dve.wait_ge(idft_hi_done, 1)
                        for k in range(2):
                            dve.tensor_tensor(idft_lo[k][:, :, :], idft_raw[:, 2 * k:2 * k + 2, :],
                                              idft_hi[:, 2 * k:2 * k + 2, :].bitcast(F32), ALU.subtract).then_inc(idft_split, 1)
                    for part in range(3):
                        if chain_step(s, j, part) is not None:
                            multiply(chain_step(s, j, part), part)
                    if (s, j) in PRODUCT_LO:
                        c = PRODUCT_LO.index((s, j))
                        dve.wait_ge(spectrum_hi_done, c + 1)
                        dve.tensor_tensor(spectrum_lo[:, :, :], spectrum[:, :, :], spectrum_hi[c][:, :, :].bitcast(F32),
                                          ALU.subtract).then_inc(spectrum_split, 1)
                    if s in (18, 19) and j in (1, 3):
                        g = 2 * (s - 18) + j // 2
                        dve.wait_ge(mem_scaled, g + 1)
                        gain_lo(1, g)
                    if s in (34, 35) and j in (1, 3):
                        mix_lo(2 * (s - 34) + j // 2)
                    if (s, j) in ((42, 1), (42, 3), (43, 1)):
                        gain_lo(2, 2 * (s - 42) + j // 2)
                    if (s, j) in SCORES:
                        softmax_shift(SCORES.index((s, j)))
                    if (s, j) in SOFTMAX:
                        softmax_norm(SOFTMAX.index((s, j)))
                    if (s, j) in TURN_PROBS:
                        dve.wait_ge(prob_t_hi_done, TURN_PROBS.index((s, j)) + 1)
                        dve.tensor_tensor(prob_t_lo[:, :, :], side[:, 0, :].rearrange("p (a b) -> p a b", a=2),
                                          prob_t_hi[:, :, :].bitcast(F32), ALU.subtract).then_inc(side_free["L"], 1)
                    if (s, j) in ATTEND:
                        split_head(ATTEND.index((s, j)))
                if s in (1, 5):
                    i = s // 4
                    if i:
                        dve.wait_ge(stream_free[3], i)
                    for b in range(2):
                        normalise(2 * i, b, sigm[:, 2 * b:2 * b + 2, :])
                if s in (3, 7):
                    i = s // 4
                    panel = 2 * i + 1
                    dve.wait_ge(glu_gate_ready, i + 1)
                    for b in range(2):
                        wait_bank(dve, panel, b)
                        dve.tensor_tensor(u[:, 4 * i + 2 * b:4 * i + 2 * b + 2, :], stream_bank(2 + b),
                                          sigm[:, 2 * b:2 * b + 2, :], ALU.mult).then_inc(stream_free[2 + b], 1)
                if s in (1, 4, 7, 10):
                    filter_window(s // 3)
                if s in (3, 6, 9, 12):
                    filter_finish(s // 3 - 1)
                if s in (10, 11, 13, 15, 17, 19):
                    short_input(s // 2 - 4 if s > 10 else 0)
                if s == 17:
                    rms_inverse(1)
                if s == 32:
                    dve.wait_ge(side_full["R"], filled("mean", "R"))
                    mean4 = side[:, 2:3, 0:S].to_broadcast([P, 4, S])
                    dve.wait_ge(conf_taps, 4 * (TAPS - 1))
                    dve.wait_ge(conf_taps_pool, 4 * (TAPS - 1))
                    for i in range(2):
                        c = conf[:, 4 * i:4 * i + 4, :]
                        op = dve.scalar_tensor_tensor(out=c, in0=mean4, scalar=-1.0 / CONF, in1=c,
                                                      op0=ALU.mult, op1=ALU.add)
                    op.then_inc(side_free["R"], 1)
                if s == 33:
                    dve.wait_ge(side_free["R"], emptied("variance", "R"))
                    dve.reciprocal(inv_rms[:, :], root[:, :]).then_inc(ln_step, 1)
                    dve.wait_ge(ln_step, 1)
                    inv4 = inv_rms[:, :].rearrange("p (a s) -> p a s", a=1).to_broadcast([P, 4, S])
                    for i in range(2):
                        c = conf[:, 4 * i:4 * i + 4, :]
                        dve.tensor_tensor(c, c, inv4, ALU.mult).then_inc(ln_step, 1)
                if s in (37, 39, 41, 43, 53, 55, 57, 59):
                    i = (s - 37) // 2 % 4
                    if s == 37:
                        dve.wait_ge(x_again_landed, 16)
                    add_panel(s // 2, i)
                    if s > 44 or i == 3:
                        gain_lo(2 if s < 44 else 3, i)
                if s == 44:
                    rms_inverse(2)
                if s in (21, 23, 25, 27, 29, 31, 33, 35):
                    memory_lo(s // 2)
                if s in (45, 47, 49, 51):
                    h = (s - 45) // 2
                    if h:
                        dve.wait_ge(side_full["R"], filled(f"scores{h - 1}", "R"))
                    for b in range(2):
                        normalise(Q0 + h, b, q[:, 2 * b:2 * b + 2, :])
                    dve.wait_ge(q_hi_done, h + 1)
                    dve.tensor_tensor(q_lo[:, :, :], q[:, :, :], q_hi[:, :, :].bitcast(F32),
                                      ALU.subtract).then_inc(q_split, 1)
            def up_slab(i, first):
                if not first:
                    dve.wait_ge(gate_done, i)
                dve.tensor_copy(ffn_par[:, :], par[:, bass.ds(i * 16 + COL["ffn"], 16)]).then_inc(ffn_par_ready, 1)
                for j in range(4, 20):
                    dve.wait_ge(hi_done, i * 16 + (FFN_PIECE0 + j + 1))
                    dve.tensor_tensor(w_lo[:, j % RING, :], raw[:, j % RING, :],
                                      w_hi[:, j % RING, :].bitcast(F32), ALU.subtract).then_inc(lo_done, 1)
                    if first and j == 10:
                        rms_inverse(3)
                    if j == 11:
                        dve.wait_ge(ffn_par_ready, i + 1)
                        dve.wait_ge(lo_done, i * 16 + (FFN_PIECE0 + j + 1))
                        for b in range(2):
                            if b == 0:
                                dve.wait_ge(stream_full[0], i + (PANELS // 2 + 1))
                            else:
                                dve.wait_ge(piece_used, i * 16 + (FFN_PIECE0 + 8))
                            dve.tensor_tensor(gate_in[:, 2 * b:2 * b + 2, :], stream_bank(b), per_tile(inv_rms, 2),
                                              ALU.mult).then_inc(stream_free[b], 1)
                    if j in (12, 13):
                        side_ = j - 12
                        for t in range(4):
                            if side_ == 0:
                                dve.wait_ge(gate_center, i * 4 + (t + 1))
                            else:
                                dve.wait_ge(gate_left, i * 4 + (t + 1))
                            o, i_ = ((1, S), (0, S - 1)) if side_ == 0 else ((0, S - 1), (1, S))
                            op = dve.scalar_tensor_tensor(
                                out=gate[:, t, o[0]:o[1]], in0=gate_in[:, t, i_[0]:i_[1]],
                                scalar=ffn_par[:, 8 * side_ + t:8 * side_ + t + 1], in1=gate[:, t, o[0]:o[1]],
                                op0=ALU.mult, op1=ALU.add)
                            if side_ == 0:
                                op.then_inc(gate_left, 1)
                            elif t == 3:
                                op.then_inc(gate_done, 1)
                dve.wait_ge(silu_scaled, i + 1)
                dve.wait_ge(lo_done, i * 16 + (FFN_PIECE0 + 20))
                for b in range(2):
                    if b == 0:
                        dve.wait_ge(stream_full[2], i + (PANELS // 2 + 1))
                    else:
                        dve.wait_ge(piece_used, i * 16 + (FFN_PIECE0 + 16))
                    dve.tensor_tensor(hv[:, 2 * b:2 * b + 2, :], stream_bank(2 + b),
                                      silu[:, 2 * b:2 * b + 2, :], ALU.mult).then_inc(stream_free[2 + b], 1)
                dve.wait_ge(h_hi_done, i + 1)
                dve.tensor_tensor(h_lo[:, bass.ds(i * 4, 4), :], hv[:, :, :],
                                  h_hi[:, bass.ds(i * 4, 4), :].bitcast(F32), ALU.subtract).then_inc(h_ready, 1)

            up_slab(0, True)
            with dve.Fori(1, SLABS) as i:
                up_slab(i, False)
            def split_down(g, first, last):
                for j in range(first, last):
                    dve.wait_ge(hi_done, g * 8 + (DOWN_PIECE0 + j + 1))
                    dve.tensor_tensor(w_lo[:, j % RING, :], raw[:, j % RING, :],
                                      w_hi[:, j % RING, :].bitcast(F32), ALU.subtract).then_inc(lo_done, 1)

            with dve.Fori(0, SLABS - 1) as g:
                split_down(g, 4, 12)

            def add_down(panel):
                for b in range(2):
                    if b == 0:
                        dve.wait_ge(down_full, panel + 1)
                    else:
                        dve.wait_ge(piece_used, DOWN_PIECE0 + 8 * (SLABS - 1) + 2 * panel + 2)
                    if panel < 2:
                        tiles = side[:, 2 * panel + b, :].rearrange("p (a s) -> p a s", a=2)
                    else:
                        tiles = stream_bank(2 * (panel - 2) + b)
                    rows = x[:, 4 * panel + 2 * b:4 * panel + 2 * b + 2, :]
                    dve.tensor_tensor(rows, tiles, rows, ALU.add).then_inc(down_added, 1)

            split_down(SLABS - 1, 4, 6)
            add_down(0)
            split_down(SLABS - 1, 6, 8)
            for panel in range(1, 4):
                add_down(panel)
            dve.wait_ge(down_added, 8)
            for j in range(12, 16):
                c = COL["g_final"] + j
                dve.tensor_scalar(y_out[:, j, :], x[:, j, :], par[:, c:c + 1], None, ALU.mult).then_inc(last_gained, 1)
            rms_inverse(4)
            dve.wait_ge(y_gained, 12)
            dve.wait_ge(last_gained, 4)
            for g in range(1, 4):
                y = y_out[:, 4 * g:4 * g + 4, :]
                dve.tensor_tensor(y, y, per_tile(inv_rms, 4), ALU.mult).then_inc(y_done, 1)


PI_BELOW = float(np.nextafter(np.float32(np.pi), np.float32(0)))


def transform_tables():
    n = 2 * S
    t = np.arange(S)[:, None]
    f = np.arange(S)[None, :]
    turn = 2 * np.pi * ((t * f) % n) / n
    re, im = np.cos(turn), -np.sin(turn)
    nyquist = np.where(t % 2 == 0, 1.0, -1.0)
    im_nyq, re_nyq = im.copy(), re.copy()
    im_nyq[:, 0:1] = nyquist
    re_nyq[:, 0:1] = nyquist
    filters = np.concatenate([re, re_nyq[:, :P], im], axis=1)
    forward = np.concatenate([re, im_nyq], axis=1)
    back_re, back_im = 2 * re.T / n, 2 * im.T / n
    back_re[0] = 1.0 / n
    back_im[0] = nyquist[:, 0] / n
    back = np.concatenate([back_re, back_im], axis=0)
    tile = lambda a: np.ascontiguousarray(a.reshape(-1, P, a.shape[1]).transpose(1, 0, 2)).astype(np.float32)
    return tile(filters), tile(forward), tile(back)


def filter_tables():
    f32 = np.float32
    t = np.linspace(0.0, 1.0, S, dtype=f32)
    w = (f32(2.0 * np.pi) * np.arange(S, dtype=f32)) / f32(S)
    bands = (FEATURES - 1) // 2
    f = np.linspace(1e-4, bands - 1, bands, dtype=f32)
    angle = (f[None, :] * w[:, None]).astype(f32).astype(np.float64)
    features = np.concatenate([t[:, None], np.cos(angle), -np.sin(angle)], axis=1).astype(f32).T
    deltas = np.abs(np.linspace(np.log(1e-2) / 1.5, np.log(1e-2) / 0.3, HY, dtype=f32))
    fwd = np.exp((-t[:, None] * deltas[None, :]).astype(f32).astype(np.float64)).astype(f32)
    bwd = np.concatenate([np.zeros((1, HY), f32), fwd[:-1]], axis=0)
    both = np.stack([fwd, bwd]).reshape(2, 2, P, 2, HALF)
    return np.ascontiguousarray(features), np.ascontiguousarray(both.transpose(3, 2, 0, 1, 4).reshape(2, P, 4, HALF))


def kernel(x, mem, g_mix, w_in, conf_dw_w, conf_dw_b, conf_ln_g, conf_ln_b, hyena_short_w,
           hyena_short_b, hyena_w1, hyena_b1, hyena_w_inner, hyena_b_inner, hyena_w_filt,
           hyena_sin_freq, hyena_skip, w_out, g_xattn, g_mem, w_q, w_k, w_v, w_o, g_ffn, w_ffn_up,
           ffn_dw_w, ffn_dw_b, w_ffn_down, g_final):
    import concourse.bacc as bacc
    from concourse.bass_utils import run_bass_kernel_spmd

    def rows(a):
        return np.asarray(a).reshape(-1, P)

    def twice(a):
        a = np.asarray(a).reshape(-1, MLP)
        return np.concatenate([a, a], axis=1)

    def on_partitions(a):
        return np.ascontiguousarray(np.asarray(a)[0].T.reshape(KT, P, S).transpose(1, 0, 2))

    ffn = np.concatenate([np.asarray(ffn_dw_w)[0].reshape(3, SLABS, 4, P),
                          np.asarray(ffn_dw_b)[0].reshape(1, SLABS, 4, P)], axis=0).transpose(1, 0, 2, 3)
    packed = [rows(conf_dw_w), rows(conf_dw_b), rows(conf_ln_g), rows(conf_ln_b), rows(hyena_short_w),
              rows(hyena_short_b), rows(ffn), rows(g_mix), rows(g_mem), rows(g_xattn), rows(g_ffn),
              rows(g_final), twice(hyena_b1), twice(hyena_b_inner), twice(hyena_sin_freq)]
    params = np.ascontiguousarray(np.concatenate(packed, axis=0).T)
    filter_forward, forward, back = transform_tables()
    features, decay = filter_tables()
    arrays = {
        "x_t": on_partitions(x), "mem_t": on_partitions(mem), "params": params,
        "w_in": w_in, "w1": hyena_w1, "w_inner": hyena_w_inner, "w_filt": hyena_w_filt,
        "skip": hyena_skip, "w_out": w_out, "w_q": w_q, "w_k": w_k, "w_v": w_v, "w_o": w_o,
        "w_up": w_ffn_up, "w_down": w_ffn_down,
        "filter_dft": filter_forward, "dft": forward, "idft": back, "decay": decay, "features": features,
    }
    for name in ("w_in", "w1", "w_inner", "w_filt", "skip", "w_out", "w_q", "w_k", "w_v", "w_o", "w_up", "w_down"):
        arrays[name] = np.ascontiguousarray(np.asarray(arrays[name])[0])
    nc = bacc.Bacc("TRN2", target_bir_lowering=False, num_devices=1)
    args = [nc.dram_tensor(n, a.shape, mybir.dt.from_np(a.dtype), kind="ExternalInput").ap()
            for n, a in arrays.items()]
    out = nc.dram_tensor("out", (P, KT, S), F32, kind="ExternalOutput").ap()
    block_program(nc, *args, out)
    result = run_bass_kernel_spmd(nc, [arrays], core_ids=[0]).results[0]["out"]
    return np.ascontiguousarray(np.asarray(result).transpose(1, 0, 2).reshape(D, S).T)[None]
```
